# Optimizing a Trainium2 kernel written in Bass

```python
import jax, jax.numpy as jnp
from jax import lax
import numpy as np

D_MODEL = 1024
BATCH = 1
SEQ = 256
DEPTH = 2

GRID_W = 64
CTX_LEN = 256
HEAD_DIM = 64
A_HEADS = 8
A_KV_HEADS = 2
A_GROUP = A_HEADS // A_KV_HEADS
B_HEADS = 4
C_GROUPS = 4
C_GROUP_DIM = 64
C_WIDTH = C_GROUPS * C_GROUP_DIM
POOL_WINDOWS = (2, 4, 8, 16)
NA_WIN_ROWS = 8
NA_WIN_COLS = 16
Q_BLOCK = 128
ROPE_THETA = 10000.0
AXIS_ROPE_DIM = HEAD_DIM // 2
N_BRANCHES = 3
D_FF = 2816
N_EXPERTS = 8
TOP_K = 2
D_FF_EXPERT = 3584
N_DENSE_LAYERS = (DEPTH + 1) // 2
N_MOE_LAYERS = DEPTH // 2
EPS = 1e-6

A_Q = A_HEADS * HEAD_DIM
A_KV = A_KV_HEADS * HEAD_DIM
B_W = B_HEADS * HEAD_DIM
IN_SPLITS = (A_Q, A_KV, A_KV, B_W, B_W, B_W, C_WIDTH, N_BRANCHES * D_MODEL)
IN_COLS = sum(IN_SPLITS)

kernel_name = "hybrid_parallel_gqa_natten_pool_moe_diffusion"

def rms_norm(x, g):
    xf = x.astype(jnp.float32)
    y = xf * lax.rsqrt(jnp.mean(xf * xf, axis=-1, keepdims=True) + EPS)
    return (y * g.astype(jnp.float32)).astype(x.dtype)

def modulate(h, shift, scale):
    return h * (1 + scale) + shift

def axial_rope_tables(n_tok):
    t = jnp.arange(n_tok, dtype=jnp.int32)
    pos = jnp.stack([t // GRID_W, t % GRID_W], axis=-1).astype(jnp.float32)
    inv_freq = ROPE_THETA ** (-jnp.arange(0, AXIS_ROPE_DIM, 2, dtype=jnp.float32) / AXIS_ROPE_DIM)
    ang = pos[:, :, None] * inv_freq[None, None, :]
    return jnp.cos(ang), jnp.sin(ang)

def apply_axial_rope(x, cos, sin):
    B, S, H, _ = x.shape
    xr = x.reshape(B, S, H, 2, 2, AXIS_ROPE_DIM // 2).astype(jnp.float32)
    x1, x2 = xr[..., 0, :], xr[..., 1, :]
    cs = cos[None, :, None]
    sn = sin[None, :, None]
    out = jnp.stack([x1 * cs - x2 * sn, x2 * cs + x1 * sn], axis=-2)
    return out.reshape(x.shape).astype(x.dtype)

def gqa_core(q, k, v):
    s = jnp.einsum('bqkgd,bnkd->bkgqn', q, k).astype(jnp.float32) * (HEAD_DIM ** -0.5)
    p = jax.nn.softmax(s, axis=-1).astype(v.dtype)
    return jnp.einsum('bkgqn,bnkd->bqkgd', p, v)

def gqa_axial_attention(q_x, k_x, v_x, q_c, k_c, v_c, cos, sin):
    B, S = q_x.shape[:2]
    q_x = apply_axial_rope(q_x, cos, sin)
    k_x = apply_axial_rope(k_x, cos, sin)
    k_all = jnp.concatenate([k_c, k_x], axis=1)
    v_all = jnp.concatenate([v_c, v_x], axis=1)
    qb = q_x.reshape(B, S // Q_BLOCK, Q_BLOCK, A_KV_HEADS, A_GROUP, HEAD_DIM).transpose(1, 0, 2, 3, 4, 5)
    o = lax.map(lambda qblk: gqa_core(qblk, k_all, v_all), qb)
    o_x = o.transpose(1, 0, 2, 3, 4, 5).reshape(B, S, A_Q)
    o_c = None
    if q_c is not None:
        L = q_c.shape[1]
        o_c = gqa_core(q_c.reshape(B, L, A_KV_HEADS, A_GROUP, HEAD_DIM), k_c, v_c).reshape(B, L, A_Q)
    return o_x, o_c

def neighbourhood_attention(q_x, k_x, v_x, q_c, k_c, v_c, rel_bias):
    B, S = q_x.shape[:2]
    rows = S // GRID_W
    wr = min(NA_WIN_ROWS, rows)
    n_win = wr * NA_WIN_COLS
    qg = q_x.reshape(B, rows, GRID_W, B_HEADS, HEAD_DIM)
    kg = k_x.reshape(B, rows, GRID_W, B_HEADS, HEAD_DIM)
    vg = v_x.reshape(B, rows, GRID_W, B_HEADS, HEAD_DIM)
    col = np.arange(GRID_W)
    col_start = np.clip(col - NA_WIN_COLS // 2, 0, GRID_W - NA_WIN_COLS)
    col_idx = col_start[:, None] + np.arange(NA_WIN_COLS)[None, :]
    dc_idx = col_idx - col[:, None] + (NA_WIN_COLS - 1)
    bias_c = rel_bias[:, :, dc_idx]
    scale = HEAD_DIM ** -0.5

    def one_row(r):
        rs = jnp.clip(r - wr // 2, 0, rows - wr)
        k_rows = lax.dynamic_slice_in_dim(kg, rs, wr, axis=1)
        v_rows = lax.dynamic_slice_in_dim(vg, rs, wr, axis=1)
        k_win = k_rows[:, :, col_idx]
        v_win = v_rows[:, :, col_idx]
        q_row = lax.dynamic_index_in_dim(qg, r, axis=1, keepdims=False)
        dr_idx = rs + jnp.arange(wr) - r + (NA_WIN_ROWS - 1)
        bias = jnp.take(bias_c, dr_idx, axis=1).transpose(0, 2, 1, 3)
        s_win = jnp.einsum('bjhd,brjchd->bhjrc', q_row, k_win).astype(jnp.float32) * scale
        s_win = (s_win + bias[None].astype(jnp.float32)).reshape(B, B_HEADS, GRID_W, n_win)
        s_ctx = jnp.einsum('bjhd,blhd->bhjl', q_row, k_c).astype(jnp.float32) * scale
        p = jax.nn.softmax(jnp.concatenate([s_win, s_ctx], axis=-1), axis=-1).astype(v_x.dtype)
        p_win = p[..., :n_win].reshape(B, B_HEADS, GRID_W, wr, NA_WIN_COLS)
        p_ctx = p[..., n_win:]
        o = jnp.einsum('bhjrc,brjchd->bjhd', p_win, v_win) + jnp.einsum('bhjl,blhd->bjhd', p_ctx, v_c)
        return o.reshape(B, GRID_W, B_W)

    o = lax.map(one_row, jnp.arange(rows))
    o_x = o.transpose(1, 0, 2, 3).reshape(B, S, B_W)
    o_c = None
    if q_c is not None:
        L = q_c.shape[1]
        o_c = gqa_core(q_c[:, :, :, None, :], k_c, v_c).reshape(B, L, B_W)
    return o_x, o_c

def pool_mixer(u, w, scale):
    B, N, _ = u.shape
    ug = u.reshape(B, N, C_GROUPS, C_GROUP_DIM)
    csum = jnp.cumsum(ug.astype(jnp.float32), axis=1)
    csum = jnp.concatenate([jnp.zeros((B, 1, C_GROUPS, C_GROUP_DIM), jnp.float32), csum], axis=1)
    t = np.arange(N)[:, None]
    win = np.array(POOL_WINDOWS)[None, :]
    lo = np.clip(t - win // 2, 0, N)
    hi = np.clip(t - win // 2 + win, 0, N)
    g = np.arange(C_GROUPS)[None, :]
    cnt = (hi - lo).astype(np.float32)[None, :, :, None]
    mean = (csum[:, hi, g] - csum[:, lo, g]) / cnt
    d = (mean - ug.astype(jnp.float32)).astype(u.dtype)
    y = jnp.einsum('bngc,gcd->bngd', d, w)
    return y.reshape(B, N, C_WIDTH) * scale

def branch_merge(y_a, y_b, y_c, gates, w_pa, w_pb, w_pc, w_out):
    g_a, g_b, g_c = jnp.split(gates, N_BRANCHES, axis=-1)
    m = (jax.nn.sigmoid(g_a) * (y_a @ w_pa) + jax.nn.sigmoid(g_b) * (y_b @ w_pb)
         + jax.nn.sigmoid(g_c) * (y_c @ w_pc))
    return m @ w_out

def token_mixers(px, pc, q_g, k_g, rel_bias, pool_w, pool_scale, w_pa, w_pb, w_pc, w_out, cos, sin, want_ctx):
    offs = np.cumsum(IN_SPLITS)[:-1].tolist()
    aq, ak, av, bq, bk, bv, cu, gates = jnp.split(px, offs, axis=-1)
    caq, cak, cav, cbq, cbk, cbv, ccu, cgates = jnp.split(pc, offs, axis=-1)

    def heads(t, h):
        return t.reshape(t.shape[0], t.shape[1], h, HEAD_DIM)

    qa = rms_norm(heads(aq, A_HEADS), q_g)
    ka = rms_norm(heads(ak, A_KV_HEADS), k_g)
    cka = rms_norm(heads(cak, A_KV_HEADS), k_g)
    cqa = rms_norm(heads(caq, A_HEADS), q_g) if want_ctx else None
    y_a, cy_a = gqa_axial_attention(qa, ka, heads(av, A_KV_HEADS), cqa, cka, heads(cav, A_KV_HEADS), cos, sin)
    cqb = heads(cbq, B_HEADS) if want_ctx else None
    y_b, cy_b = neighbourhood_attention(heads(bq, B_HEADS), heads(bk, B_HEADS), heads(bv, B_HEADS),
                                        cqb, heads(cbk, B_HEADS), heads(cbv, B_HEADS), rel_bias)
    y_c = pool_mixer(cu, pool_w, pool_scale)
    out_x = branch_merge(y_a, y_b, y_c, gates, w_pa, w_pb, w_pc, w_out)
    out_c = None
    if want_ctx:
        cy_c = pool_mixer(ccu, pool_w, pool_scale)
        out_c = branch_merge(cy_a, cy_b, cy_c, cgates, w_pa, w_pb, w_pc, w_out)
    return out_x, out_c

def swiglu(h, w1, w3, w2):
    return (jax.nn.silu(h @ w1) * (h @ w3)) @ w2

def moe_swiglu(h, router_w, router_b, w1, w3, w2):
    logits = (h @ router_w).astype(jnp.float32) + router_b.astype(jnp.float32)
    top_val, top_idx = lax.top_k(logits, TOP_K)
    top_p = jax.nn.softmax(top_val, axis=-1)
    combine = jnp.sum(jax.nn.one_hot(top_idx, N_EXPERTS, dtype=jnp.float32) * top_p[..., None], axis=-2)
    out = jnp.zeros_like(h)
    for e in range(N_EXPERTS):
        out = out + combine[..., e:e + 1].astype(h.dtype) * swiglu(h, w1[e], w3[e], w2[e])
    return out

def setup_inputs(seed: int = 0) -> dict:
    key = jax.random.key(seed)
    ks = jax.random.split(key, 32)
    f32 = jnp.float32
    D = D_MODEL

    def nrm(k, shape, scale):
        return jax.random.normal(k, shape, f32) * scale

    return {
        "x": nrm(ks[0], (BATCH, SEQ, D), 1.0),
        "c": nrm(ks[1], (BATCH, D), 1.0),
        "ctx": nrm(ks[2], (BATCH, CTX_LEN, D), 1.0),
        "c_ctx": nrm(ks[3], (D,), 1.0),
        "w_mod": nrm(ks[4], (DEPTH, D, 6 * D), 0.5 * D ** -0.5),
        "b_mod": nrm(ks[5], (DEPTH, 6 * D), 0.02),
        "norm1_g": 1.0 + nrm(ks[6], (DEPTH, D), 0.02),
        "norm2_g": 1.0 + nrm(ks[7], (DEPTH, D), 0.02),
        "w_in": nrm(ks[8], (DEPTH, D, IN_COLS), D ** -0.5),
        "q_norm_g": 1.0 + nrm(ks[9], (DEPTH, HEAD_DIM), 0.02),
        "k_norm_g": 1.0 + nrm(ks[10], (DEPTH, HEAD_DIM), 0.02),
        "na_rel_bias": nrm(ks[11], (DEPTH, B_HEADS, 2 * NA_WIN_ROWS - 1, 2 * NA_WIN_COLS - 1), 0.5),
        "pool_w": nrm(ks[12], (DEPTH, C_GROUPS, C_GROUP_DIM, C_GROUP_DIM), C_GROUP_DIM ** -0.5),
        "pool_scale": 1.0 + nrm(ks[13], (DEPTH, C_WIDTH), 0.1),
        "w_branch_a": nrm(ks[14], (DEPTH, A_Q, D), A_Q ** -0.5),
        "w_branch_b": nrm(ks[15], (DEPTH, B_W, D), B_W ** -0.5),
        "w_branch_c": nrm(ks[16], (DEPTH, C_WIDTH, D), C_WIDTH ** -0.5),
        "w_out": nrm(ks[17], (DEPTH, D, D), D ** -0.5),
        "ffn_w1": nrm(ks[18], (N_DENSE_LAYERS, D, D_FF), D ** -0.5),
        "ffn_w3": nrm(ks[19], (N_DENSE_LAYERS, D, D_FF), D ** -0.5),
        "ffn_w2": nrm(ks[20], (N_DENSE_LAYERS, D_FF, D), D_FF ** -0.5),
        "router_w": nrm(ks[21], (N_MOE_LAYERS, D, N_EXPERTS), D ** -0.5),
        "router_b": nrm(ks[22], (N_MOE_LAYERS, N_EXPERTS), 0.01),
        "moe_w1": nrm(ks[23], (N_MOE_LAYERS, N_EXPERTS, D, D_FF_EXPERT), D ** -0.5),
        "moe_w3": nrm(ks[24], (N_MOE_LAYERS, N_EXPERTS, D, D_FF_EXPERT), D ** -0.5),
        "moe_w2": nrm(ks[25], (N_MOE_LAYERS, N_EXPERTS, D_FF_EXPERT, D), D_FF_EXPERT ** -0.5),
        "final_g": 1.0 + nrm(ks[26], (D,), 0.02),
    }

def reference(x, c, ctx, c_ctx, w_mod, b_mod, norm1_g, norm2_g, w_in, q_norm_g, k_norm_g, na_rel_bias,
              pool_w, pool_scale, w_branch_a, w_branch_b, w_branch_c, w_out, ffn_w1, ffn_w3, ffn_w2,
              router_w, router_b, moe_w1, moe_w3, moe_w2, final_g):
    S = x.shape[1]
    L = ctx.shape[1]
    cos, sin = axial_rope_tables(S)
    xc = ctx
    silu_c = jax.nn.silu(c)
    silu_cc = jax.nn.silu(c_ctx)
    for layer in range(DEPTH):
        want_ctx = layer < DEPTH - 1
        mod = silu_c @ w_mod[layer] + b_mod[layer]
        cmod = silu_cc @ w_mod[layer] + b_mod[layer]
        sh1, sc1, g1, sh2, sc2, g2 = jnp.split(mod[:, None, :], 6, axis=-1)
        csh1, csc1, cg1, csh2, csc2, cg2 = jnp.split(cmod, 6, axis=-1)

        hx = modulate(rms_norm(x, norm1_g[layer]), sh1, sc1)
        hc = modulate(rms_norm(xc, norm1_g[layer]), csh1, csc1)
        mx, mc = token_mixers(hx @ w_in[layer], hc @ w_in[layer], q_norm_g[layer], k_norm_g[layer],
                              na_rel_bias[layer], pool_w[layer], pool_scale[layer], w_branch_a[layer],
                              w_branch_b[layer], w_branch_c[layer], w_out[layer], cos, sin, want_ctx)
        x = x + g1 * mx
        hx = modulate(rms_norm(x, norm2_g[layer]), sh2, sc2)
        if want_ctx:
            xc = xc + cg1 * mc
            hc = modulate(rms_norm(xc, norm2_g[layer]), csh2, csc2)
            h_all = jnp.concatenate([hc, hx], axis=1)
        else:
            h_all = hx
        if layer % 2 == 0:
            i = layer // 2
            f = swiglu(h_all, ffn_w1[i], ffn_w3[i], ffn_w2[i])
        else:
            i = layer // 2
            f = moe_swiglu(h_all, router_w[i], router_b[i], moe_w1[i], moe_w3[i], moe_w2[i])
        if want_ctx:
            xc = xc + cg2 * f[:, :L]
            fx = f[:, L:]
        else:
            fx = f
        x = x + g2 * fx
    return rms_norm(x, final_g)


_drawn_inputs = setup_inputs


def setup_inputs(seed=0):
    import zlib

    import numpy as np

    out = dict(_drawn_inputs(seed))
    spreads = {}
    factors = {'norm1_g': 7.039,
     'norm2_g': 3.814,
     'q_norm_g': 8.0,
     'k_norm_g': 8.0,
     'na_rel_bias': 5.724,
     'router_b': 4.63,
     'final_g': 2.79}
    for name, (base, spread) in spreads.items():
        noise = np.random.default_rng([zlib.crc32(name.encode()), seed]).standard_normal(out[name].shape)
        drawn = base * np.exp(spread * noise) if base else spread * noise
        out[name] = __import__('jax').numpy.asarray(drawn.astype(out[name].dtype))
    for name, factor in factors.items():
        out[name] = (out[name] * factor).astype(out[name].dtype)
    return out
```

```python
from contextlib import ExitStack

import numpy as np

import concourse.bass as bass
from concourse import mybir

F32 = mybir.dt.float32
I32 = mybir.dt.int32
ALU = mybir.AluOpType
ACT = mybir.ActivationFunctionType
AX = mybir.AxisListType.X

P = 128
D = 1024
DC = D // P
S = 256
T = 2 * S
CTX, LAT = 0, 1
DEPTH = 2
HD = 64
GRID_W = 64
KEY_TILES = T // P
F_DENSE = 2816
FC = F_DENSE // P
HALF_CHUNKS = (12, 10)
N_EXPERTS = 8
F_EXPERT = 3584
GROUPS = F_EXPERT // 256
SLOTS = 96
PASSES = -(-S // SLOTS)
EPS = 1e-6
SLAB = 2048
RING = 8
MOE_RING = 14
BANKS = 5
MASKED = -1e30

CONST_COLS = {}
_at = 0
for _name, _n in (("ident", P), ("ones", P), ("perm", P), ("before", P), ("blk2", 2), ("cos", S), ("sin", S),
                  ("wmask", GRID_W), ("iota", PASSES * SLOTS), ("lower", 64), ("eps", 1)):
    CONST_COLS[_name] = (_at, _at + _n)
    _at += _n
N_CONST = _at
VEC_COLS = {}
_at = 0
for _name, _n in (("bmod", 48), ("g1", DC), ("g2", DC), ("gq", 1), ("gk", 1), ("pscale", 2)):
    for _l in range(DEPTH):
        VEC_COLS[_name, _l] = (_at, _at + _n)
        _at += _n
for _name, _n in (("final", DC), ("cond", 2 * DC), ("rw", DC * N_EXPERTS), ("rb", N_EXPERTS)):
    VEC_COLS[_name] = (_at, _at + _n)
    _at += _n
N_VEC = _at

W_IN_Q = (0, 1)
W_IN_KV, W_IN_BQ, W_IN_BK, W_IN_BV, W_IN_U, W_IN_GATE = 2, 3, 4, 5, 6, 7


MOD_AT_START, MOD_IN_ATTENTION, MOD_IN_FFN = range(8), range(8, 32), range(32, 48)


def attention_units(layer):
    streams = (LAT, CTX) if layer == 0 else (LAT,)
    return [(b, h, s) for b, n in (("A", 8), ("B", 4)) for s in streams for h in range(n)]


def schedule():
    slabs, fills = [], []

    def mod(n):
        slabs.append(("mod", n))
        fills.append(("mod", n))
        if n % 4 == 3:
            fills.append(("turned_mod", n // 4))

    def norm(key):
        fills.extend([("stat", key), ("bcast", key)])

    for n in MOD_AT_START:
        mod(n)
    for layer in range(DEPTH):
        norm((layer, 1))
        for s in range(7):
            slabs.append(("in", layer, s))
        names = [("q", j) for j in range(4)] + [("k", 0), ("av", 0), ("bq", 0), ("bq", 1), ("bk", 0), ("bk", 1),
                                                ("bv", 0), ("bv", 1)]
        names += [("u", 0), ("u", 1)] if layer == 0 else [("u", 1)]
        fills.extend(("in", layer, n) for n in names)
        fills.append(("qkstat", layer))
        fills.extend(("qkb", layer, j) for j in range(5))
        fills.extend(("rope", layer, j) for j in range(5))
        units = attention_units(layer)
        for u in range(2):
            fills.extend(("score", layer, u, q) for q in range(2 if units[u][2] == LAT else 1))
        for u in range(len(units)):
            if u + 2 < len(units):
                fills.extend(("score", layer, u + 2, q) for q in range(2 if units[u + 2][2] == LAT else 1))
            if layer == 0:
                mod(MOD_IN_ATTENTION[u])
        fills.extend(("pool", layer, p) for p in range(2))
        fills.extend(("poolw", layer, p) for p in range(2))
        for j in range(4):
            slabs.extend(("in", layer, W_IN_GATE + 4 * b + j) for b in range(3))
            fills.extend(("gate", layer, j, b, m) for b in range(3) for m in range(2))
            slabs.append(("proj", layer, j))
            fills.extend(("proj", layer, j, b, m) for b in range(3) for m in range(2))
        for j in range(4):
            slabs.append(("out", layer, j))
            fills.extend(("out", layer, j, m) for m in range(2))
        norm((layer, 2))
        if layer == 0:
            later = list(MOD_IN_FFN)
            for half in range(2):
                for s in range(HALF_CHUNKS[half] // 2):
                    slabs.extend([("w1", half, s), ("w3", half, s)])
                    fills.extend([("w1", half, s, 0), ("w1", half, s, 1), ("w3", half, s, 0), ("w3", half, s, 1)])
                    if later:
                        mod(later.pop(0))
                for j in range(4):
                    slabs.extend([("w2", half, j, 0), ("w2", half, j, 1)])
                    fills.extend(("down", half, j, m) for m in range(2))
                    if later:
                        mod(later.pop(0))
            assert not later
    fills.append(("logit",))
    fills.extend(("turn", i) for i in range(4))
    fills.append(("prefix",))
    return {k: n for n, k in enumerate(slabs)}, {k: n for n, k in enumerate(fills)}


SLABS, FILLS = schedule()


def last_fill(slab):
    kind = slab[0]
    if kind == "mod":
        return slab
    if kind == "in":
        _, layer, s = slab
        if s >= W_IN_GATE:
            b, j = divmod(s - W_IN_GATE, 4)
            return ("gate", layer, j, b, 1)
        return ("in", layer, (("q", 1), ("q", 3), ("av", 0), ("bq", 1), ("bk", 1), ("bv", 1), ("u", 1))[s])
    if kind == "proj":
        return ("proj", slab[1], slab[2], 2, 1)
    if kind == "out":
        return ("out", slab[1], slab[2], 1)
    if kind in ("w1", "w3"):
        return slab + (1,)
    return ("down", slab[1], slab[2], 1 if slab[3] else 0)

EXPERT_SLABS = []
for _g in range(GROUPS):
    EXPERT_SLABS += [("up", _g, 0), ("up", _g, 1)]
    if _g:
        EXPERT_SLABS.append(("down", _g - 1, 0))
EXPERT_SLABS.append(("down", GROUPS - 1, 0))
EXPERT_AT = {k: n for n, k in enumerate(EXPERT_SLABS)}
N_EXPERT_SLABS = len(EXPERT_SLABS)
ROUNDS = N_EXPERT_SLABS // MOE_RING
assert ROUNDS * MOE_RING == N_EXPERT_SLABS


def build(nc, a):
    with ExitStack() as ctx:
        base = -(-nc.sbuf_base // 32) * 32

        def at(name, kb, shape, dt=F32):
            return nc.alloc_sbuf_tensor_at(name, shape, dt, offset=base + -(-int(kb * 1024) // 32) * 32)

        def sem(name):
            return ctx.enter_context(nc.semaphore(name))

        def psum(name, shape):
            return ctx.enter_context(nc.psum_tensor(name, shape, F32))

        ring = [at(f"slab{i}", 8 * i, [P, DC, 256]) for i in range(RING)]
        Y = at("Y", 64, [P, DC, T])
        QK = at("QK", 80, [P, 5, T])
        BQ = at("BQ", 90, [P, 2, T])
        BK = at("BK", 94, [P, 2, T])
        V = at("V", 98, [P, KEY_TILES, 384])
        U = at("U", 104, [P, KEY_TILES, 256])
        M = at("M", 80, [P, DC, T])
        GATE = at("GATE", 96, [P, 6, T])
        HID = at("HID", 64, [P, 12, T])
        SILU = at("SILU", 88, [P, 2, T])
        moe_slab = [at(f"moe_slab{i}", 8 * i, [P, SLAB]) for i in range(MOE_RING)]
        XT = at("XT", 112, [P, DC, T])
        H = at("H", 128, [P, DC, T])
        BIAS = at("BIAS", 144, [P, 2, 4, S])
        POOL = at("POOL", 152, [P, 2, 4, S])
        PR = at("PR", 160, [P, 2, 2, T])
        PT = at("PT", 168, [P, 2, 4, S])
        SQ = at("SQ", 176, [P, 2, T])
        TMP = at("TMP", 180, [P, 2, T])
        DT = at("DT", 184, [P, 2, T])
        PW = at("PW", 188, [P, 2, P])
        CONST = at("CONST", 189, [P, N_CONST])
        VEC = at("VEC", 195, [P, N_VEC])
        kb = 195 + N_VEC * 4 / 1024
        small = {}
        for name, n in (("cond", 32 * DC), ("modrow", 256), ("mod0", 96), ("mod1", 96), ("scale1", 2 * DC), ("scale2", 2 * DC),
                        ("rms", 4), ("rrms", 4), ("qks", 40), ("qkr", 40), ("gq8", 1),
                        ("mx", 48), ("nm", 48), ("rs", 48), ("ri", 48), ("t1", S)):
            kb = -(-kb * 1024 // 32) * 32 / 1024
            small[name] = at(f"s_{name}", kb, [P, n])
            kb += n * 4 / 1024
        assert kb <= 207, kb
        HTOK = at("HTOK", 160, [P, 2, D])
        HE = at("HE", 168, [P, DC, SLOTS])
        YE = at("YE", 171, [P, DC, SLOTS])
        GE = at("GE", 174, [P, 2, 2, SLOTS])
        SE = at("SE", 176, [P, 2, 2, SLOTS])
        YTOK = at("YTOK", 178, [SLOTS, D])
        ONEHOT = at("ONEHOT", 182, [P, 2, SLOTS])
        WEIGHTED = at("WEIGHTED", 183, [P, 2, SLOTS])
        SCATTER = at("SCATTER", 184, [SLOTS, S])
        R1 = at("R1", 144, [P, 2, 8])
        CMP = at("CMP", 144.25, [P, 2, 8, 8])
        CMP2 = at("CMP2", 145, [P, 2, 8, 8])
        RANK, SEL, EX, W, POS, POS1, NSEL = (at(n, 145.5 + i / 8, [P, 2, 8]) for i, n in enumerate(
            ("RANK", "SEL", "EX", "W", "POS", "POS1", "NSEL")))
        RM, RSUM, RINV = (at(n, 146.5 + i / 8, [P, 2]) for i, n in enumerate(("RM", "RSUM", "RINV")))
        COUNT = at("COUNT", 147, [P, 8], I32)
        COUNTF = at("COUNTF", 147.125, [P, 8])
        MAXF = at("MAXF", 147.25, [P, 1])
        MAXI = at("MAXI", 147.375, [P, 1], I32)
        OUT = at("OUT", 128, [P, DC, S])

        def const(name, p0=0, p1=P):
            lo, hi = CONST_COLS[name]
            return CONST[p0:p1, lo:hi]

        def vec(name):
            lo, hi = VEC_COLS[name]
            return VEC[:, lo:hi]

        ident, ones, eps = const("ident"), const("ones"), const("eps")
        MOD = [small["mod0"], small["mod1"]]

        def mod_vec(layer, part, chunk, stream):
            col = (part * DC + chunk) * 2 + (1 - stream)
            return MOD[layer][:, col:col + 1]

        bank = [psum(f"bank{i}", [P, 512]) for i in range(BANKS)]
        turned = [psum(f"turned{i}", [P, 512]) for i in range(2)]
        pv_bank = psum("pv_bank", [P, 512])

        consts_in, vecs_in, x_in, pool_in = sem("consts_in"), sem("vecs_in"), sem("x_in"), sem("pool_in")
        slab_in = [sem(f"slab_in{i}") for i in range(RING)]
        full = [sem(f"full{i}") for i in range(BANKS)]
        free = [sem(f"free{i}") for i in range(BANKS)]
        cond_ready, cond_zeroed = sem("cond_ready"), sem("cond_zeroed")
        dve_seq = sem("dve_seq")
        L = range(DEPTH)
        norms = [(0, 1), (0, 2), (1, 1), (1, 2), "final"]
        sq_ready = {k: sem(f"sq_ready{i}") for i, k in enumerate(norms)}
        sq_used = {k: sem(f"sq_used{i}") for i, k in enumerate(norms)}
        final_rms = sem("final_rms")
        rrms_ready = {k: sem(f"rrms_ready{i}") for i, k in enumerate(norms)}
        tmp_ready = {k: sem(f"tmp_ready{i}") for i, k in enumerate(norms)}
        h_ready = {k: sem(f"h_ready{i}") for i, k in enumerate(norms)}
        scale_ready = sem("scale_ready")
        qk_sq = [sem(f"qk_sq{l}") for l in L]
        qk_sq_used = [sem(f"qk_sq_used{l}") for l in L]
        qk_rrms = [sem(f"qk_rrms{l}") for l in L]
        qk_ready = [sem(f"qk_ready{l}") for l in L]
        bias_in, bias_ready = [sem(f"bias_in{l}") for l in L], [sem(f"bias_ready{l}") for l in L]
        pw_in = [sem(f"pw_in{l}") for l in L]
        nm_ready = [sem(f"nm_ready{l}") for l in L]
        p_ready = [sem(f"p_ready{l}") for l in L]
        turned_full = [sem(f"turned_full{l}") for l in L]
        turned_out_act = [sem(f"turned_out_act{l}") for l in L]
        turned_out_dve = [sem(f"turned_out_dve{l}") for l in L]
        pv_full = [sem(f"pv_full{l}") for l in L]
        y_ready = [sem(f"y_ready{l}") for l in L]
        routed = sem("routed")
        ex_ready = sem("ex_ready")
        sel_ready, counts_ready = sem("sel_ready"), sem("counts_ready")
        moe_in = [sem(f"moe_in{i}") for i in range(MOE_RING)]
        onehot_ready, gathered, he_ready = sem("onehot_ready"), sem("gathered"), sem("he_ready")
        weights_turned, scatter_ready = sem("weights_turned"), sem("scatter_ready")
        up_full, se_ready, ge_ready, down_done = sem("up_full"), sem("se_ready"), sem("ge_ready"), sem("down_done")
        ye_dve, ye_act = sem("ye_dve"), sem("ye_act")
        y_turned, ytok_dve, ytok_act = sem("y_turned"), sem("ytok_dve"), sem("ytok_act")
        scattered, x_added = sem("scattered"), sem("x_added")
        step_over = sem("step_over")
        out_ready, out_done = sem("out_ready"), sem("out_done")

        def acc(key):
            return bank[FILLS[key] % BANKS]

        def wait_full(eng, key):
            n = FILLS[key]
            eng.wait_ge(full[n % BANKS], n // BANKS + 1)

        def wait_taken(eng, key):
            n = FILLS[key]
            eng.wait_ge(free[n % BANKS], n // BANKS + 1)

        def freed(key):
            return free[FILLS[key] % BANKS]

        def x_range(layer):
            return (0, T) if layer == 0 else (S, T)

        def streams_of(layer):
            return (CTX, LAT) if layer == 0 else (LAT,)

        def lat_col(layer):
            return S if layer == 0 else 0

        def overflow_steps(eng, body, skip):
            eng.wait_ge(x_added, N_EXPERTS * 4)
            eng.wait_ge(counts_ready, 2)
            most = eng.value_load(MAXI[0:1, 0:1], min_val=0, max_val=S)
            with eng.If(most > SLOTS):
                with eng.Fori(0, N_EXPERTS) as e:
                    count = eng.value_load(COUNT[0:1, bass.ds(e, 1)], min_val=0, max_val=S)
                    for again in range(1, PASSES):
                        i = e * (PASSES - 1) + (N_EXPERTS + again - 1)
                        with eng.If(count > SLOTS * again):
                            body(e, i, again)
                            eng.wait_ge(x_added, i * 4 + 4)
                            eng.sem_inc(step_over, 1)
                        with eng.Else():
                            skip()

        block = ctx.enter_context(nc.Block())

        @block.sync
        def _(sp):
            def slab_source(key):
                kind = key[0]
                if kind == "mod":
                    return a["w_mod"][key[1]], SLAB
                if kind == "in":
                    return a["w_in"][key[1] * 19 + key[2]], SLAB
                if kind == "proj":
                    return a["w_proj"][key[1] * 4 + key[2]], SLAB
                if kind == "out":
                    return a["w_out"][key[1] * 4 + key[2]], SLAB
                if kind in ("w1", "w3"):
                    return a["ffn_" + kind][key[1] * (HALF_CHUNKS[0] // 2) + key[2]], SLAB
                half, j, part = key[1:]
                return a[f"ffn_w2_{half}"][j * 2 + part], HALF_CHUNKS[half] // 2 * 256

            def load_slab(n, key):
                if n >= RING:
                    wait_full(sp, last_fill(order[n - RING]))
                src, size = slab_source(key)
                dst = ring[n % RING].rearrange("p k n -> p (k n)")[:, 0:size]
                sp.dma_start(dst, src).then_inc(slab_in[n % RING], 16)

            order = list(SLABS)
            sp.dma_start(VEC[:], a["vecs"]).then_inc(vecs_in, 16)
            for n in range(2):
                load_slab(n, order[n])
            sp.dma_start(XT[:].rearrange("p k n -> p (k n)"), a["xt"]).then_inc(x_in, 16)
            sp.dma_start(CONST[:], a["consts"]).then_inc(consts_in, 16)
            for n in range(2, len(order)):
                load_slab(n, order[n])

            def expert_load(k, e):
                kind, g, w = EXPERT_SLABS[k]
                src = a[("moe_w1", "moe_w3")[w] if kind == "up" else "moe_w2"]
                sp.dma_start(moe_slab[k % MOE_RING][:],
                             src[bass.ds(e * (GROUPS * P) + g * P, P), :]).then_inc(moe_in[k % MOE_RING], 16)

            def expert_head(e):
                for k in range(MOE_RING):
                    expert_load(k, e)

            def wait_used(k, i):
                kind, g, _ = EXPERT_SLABS[k]
                sp.wait_ge(up_full if kind == "up" else down_done, i * GROUPS + g + 1)

            def expert_rest(e, i):
                for k in range(MOE_RING, N_EXPERT_SLABS):
                    wait_used(k - MOE_RING, i)
                    expert_load(k, e)

            wait_full(sp, ("out", 1, 3, 1))
            expert_head(0)
            with sp.Fori(0, N_EXPERTS - 1) as e:
                expert_rest(e, e)
                for k in range(MOE_RING):
                    wait_used(N_EXPERT_SLABS - MOE_RING + k, e)
                    expert_load(k, e + 1)
            expert_rest(N_EXPERTS - 1, N_EXPERTS - 1)

            def overflow(e, i, again):
                expert_head(e)
                expert_rest(e, i)

            overflow_steps(sp, overflow, lambda: [sp.sem_inc(s, 16 * ROUNDS) for s in moe_in])
            sp.wait_ge(out_ready, DC)
            sp.dma_start(a["out"], OUT[:].rearrange("p k n -> p (k n)")).then_inc(out_done, 16)
            sp.wait_ge(out_done, 16)

        @block.gpsimd
        def _(pool):
            pool.dma_start(POOL[:].rearrange("p a g n -> p (a g n)"), a["pool_mat"]).then_inc(pool_in, 16)
            for layer in L:
                if layer:
                    pool.wait_ge(bias_ready[0], 2)
                    wait_full(pool, ("poolw", 0, 1))
                    pool.wait_ge(nm_ready[0], len(attention_units(0)))
                pool.dma_start(PW[:].rearrange("p a n -> p (a n)"), a["pool_w"][layer]).then_inc(pw_in[layer], 16)
                pool.dma_start(BIAS[:].rearrange("p a h n -> p (a h n)"), a["rel_bias"][layer])\
                    .then_inc(bias_in[layer], 16)

        @block.tensor
        def _(pe):
            def fill(key):
                n = FILLS[key]
                if n >= BANKS:
                    pe.wait_ge(free[n % BANKS], n // BANKS)
                return bank[n % BANKS]

            def filled(ins, key):
                ins.then_inc(full[FILLS[key] % BANKS], 1)

            def slab(key):
                n = SLABS[key]
                pe.wait_ge(slab_in[n % RING], 16 * (n // RING + 1))
                return ring[n % RING]

            mm = nc.tensor.matmul

            def chain(out, pairs):
                last = len(pairs) - 1
                for k, (lhs, rhs) in enumerate(pairs):
                    ins = mm(out, lhs, rhs, start=k == 0, stop=k == last)
                return ins

            def mod(n):
                w, out, q = slab(("mod", n)), fill(("mod", n)), n % 4
                filled(chain(out[32 * q:32 * q + 32, 0:256],
                             [(small["cond"][:, 32 * k:32 * k + 32], w[:, k, :]) for k in range(DC)]), ("mod", n))
                if q == 3:
                    key = ("turned_mod", n // 4)
                    out = fill(key)
                    for back in range(4):
                        wait_taken(pe, ("mod", n - back))
                    for m in range(2):
                        ins = nc.tensor.transpose(out[:, P * m:P * m + P], small["modrow"][:, P * m:P * m + P], ident)
                    filled(ins, key)

            def norm(key, lo, hi):
                tiles = (hi - lo) // P
                out = fill(("stat", key))
                for c in range(DC):
                    pe.wait_ge(sq_ready[key], c + 1)
                    for t in range(tiles):
                        ins = mm(out[:, t:t + 1], SQ[:, c % 2, P * t:P * t + P], ones[:, 0:1],
                                 start=c == 0 and t == 0, stop=c == DC - 1, skip_group_check=True)
                    if c < DC - 1:
                        ins.then_inc(sq_used[key], 1)
                filled(ins, ("stat", key))
                out = fill(("bcast", key))
                pe.wait_ge(rrms_ready[key], 1)
                for t in range(tiles):
                    ins = mm(out[:, P * t:P * t + P], small["rrms"][:, t:t + 1].to_broadcast([P, P]), ident,
                             start=True, stop=True)
                filled(ins, ("bcast", key))

            def in_proj(layer):
                lo, hi = x_range(layer)
                n_str = 2
                first = [True]

                def h_chunk(k):
                    if first[0]:
                        pe.wait_ge(h_ready[layer, 1], n_str * (k + 1))
                        if k == DC - 1:
                            first[0] = False

                def by_feature(name, w, m, c0, c1):
                    out = fill(("in", layer, name))
                    for k in range(DC):
                        h_chunk(k)
                        ins = mm(out[:, 0:c1 - c0], w[:, k, P * m:P * m + P], H[:, k, c0:c1],
                                 start=k == 0, stop=k == DC - 1)
                    filled(ins, ("in", layer, name))

                def by_token(name, w, tiles, c0, c1):
                    out = fill(("in", layer, name))
                    for n, t in enumerate(tiles):
                        ins = chain(out[:, n * (c1 - c0):(n + 1) * (c1 - c0)],
                                    [(H[:, k, P * t:P * t + P], w[:, k, c0:c1]) for k in range(DC)])
                    filled(ins, ("in", layer, name))

                for s in range(2):
                    w = slab(("in", layer, s))
                    for m in range(2):
                        by_feature(("q", 2 * s + m), w, m, lo, hi)
                w = slab(("in", layer, W_IN_KV))
                by_feature(("k", 0), w, 0, 0, T)
                by_token(("av", 0), w, range(4), P, 2 * P)
                w = slab(("in", layer, W_IN_BQ))
                for m in range(2):
                    by_feature(("bq", m), w, m, lo, hi)
                w = slab(("in", layer, W_IN_BK))
                for m in range(2):
                    by_feature(("bk", m), w, m, 0, T)
                w = slab(("in", layer, W_IN_BV))
                for m in range(2):
                    by_token(("bv", m), w, (2 * m, 2 * m + 1), 0, 256)
                w = slab(("in", layer, W_IN_U))
                for m in (range(2) if layer == 0 else (1,)):
                    by_token(("u", m), w, (2 * m, 2 * m + 1), 0, 256)

            def qk_norm(layer):
                tq = 4 if layer == 0 else 2
                out = fill(("qkstat", layer))
                for j in range(5):
                    pe.wait_ge(qk_sq[layer], j + 1)
                    for t in range(tq if j < 4 else 4):
                        col = 2 * (j * tq + t)
                        ins = mm(out[:, col:col + 2], SQ[:, j % 2, P * t:P * t + P], const("blk2"),
                                 start=True, stop=True)
                    if j < 4:
                        ins.then_inc(qk_sq_used[layer], 1)
                filled(ins, ("qkstat", layer))
                for j in range(5):
                    out = fill(("qkb", layer, j))
                    if j == 0:
                        pe.wait_ge(qk_rrms[layer], 1)
                    for t in range(tq if j < 4 else 4):
                        col = 2 * (j * tq + t)
                        for g in range(2):
                            ins = mm(out[HD * g:HD * g + HD, P * t:P * t + P],
                                     small["qkr"][:, col + g:col + g + 1].to_broadcast([P, HD]), ident,
                                     start=True, stop=True)
                    filled(ins, ("qkb", layer, j))
                for j in range(5):
                    out = fill(("rope", layer, j))
                    wait_taken(pe, ("qkb", layer, j))
                    c = lat_col(layer) if j < 4 else S
                    ins = mm(out[:, 0:S], const("perm"), QK[:, j, c:c + S], start=True, stop=True)
                    filled(ins, ("rope", layer, j))

            def place(branch, h):
                if branch == "A":
                    g = h // 4
                    return QK[:, h % 4], HD * g, QK[:, 4], HD * g, h % 4
                return BQ[:, h // 2], HD * (h % 2), BK[:, h // 2], P + HD * h, 4 + h // 2

            def attention(layer):
                units = attention_units(layer)
                c_lat = lat_col(layer)

                def scores(u):
                    branch, h, stream = units[u]
                    q, p0, k, _, _ = place(branch, h)
                    col = c_lat if stream == LAT else 0
                    if u == 0:
                        pe.wait_ge(qk_ready[layer], 5)
                    if branch == "B" and h == 0:
                        for name in ("bq", "bk"):
                            for m in range(2):
                                wait_taken(pe, ("in", layer, (name, m)))
                    for t in range(2):
                        lhs = q[p0:p0 + HD, col + P * t:col + P * t + P]
                        if stream == LAT:
                            out = fill(("score", layer, u, t))
                            filled(mm(out[:], lhs, k[p0:p0 + HD, :], start=True, stop=True), ("score", layer, u, t))
                        else:
                            if t == 0:
                                out = fill(("score", layer, u, 0))
                            ins = mm(out[:, S * t:S * t + S], lhs, k[p0:p0 + HD, 0:S], start=True, stop=True)
                    if stream == CTX:
                        filled(ins, ("score", layer, u, 0))

                def turn(u):
                    stream = units[u][2]
                    pe.wait_ge(p_ready[layer], u + 1)
                    if u:
                        pe.wait_ge(turned_out_act[layer], u)
                        pe.wait_ge(turned_out_dve[layer], u)
                    tiles = 4 if stream == LAT else 2
                    for t in range(tiles):
                        b, n = divmod(t, tiles // 2)
                        for qt in range(2):
                            ins = nc.tensor.transpose(turned[b][:, S * n + P * qt:S * n + P * qt + P],
                                                      PR[:, u % 2, qt, P * t:P * t + P], ident)
                    ins.then_inc(turned_full[layer], 1)

                def values(u):
                    branch, h, stream = units[u]
                    _, p0, _, vcol, _ = place(branch, h)
                    pe.wait_ge(turned_out_act[layer], u + 1)
                    pe.wait_ge(turned_out_dve[layer], u + 1)
                    if u == 0:
                        for name in (("av", 0), ("bv", 0), ("bv", 1)):
                            wait_taken(pe, ("in", layer, name))
                    else:
                        pe.wait_ge(y_ready[layer], u)
                    tiles = 4 if stream == LAT else 2
                    ins = chain(pv_bank[p0:p0 + HD, 0:S],
                                [(V[:, t, vcol:vcol + HD], PT[:, u % 2, t, :]) for t in range(tiles)])
                    ins.then_inc(pv_full[layer], 1)

                scores(0)
                scores(1)
                for u in range(len(units)):
                    if u + 2 < len(units):
                        scores(u + 2)
                    if u:
                        values(u - 1)
                    turn(u)
                    if layer == 0:
                        mod(MOD_IN_ATTENTION[u])
                values(len(units) - 1)

            def pooling(layer):
                if layer == 0:
                    pe.wait_ge(pool_in, 16)
                for m in (range(2) if layer == 0 else (1,)):
                    wait_taken(pe, ("in", layer, ("u", m)))
                for p in range(2):
                    out = fill(("pool", layer, p))
                    for n, stream in enumerate(streams_of(layer)):
                        for gg in range(2):
                            g = 2 * p + gg
                            ins = chain(out[HD * gg:HD * gg + HD, S * n:S * n + S],
                                        [(U[:, 2 * stream + t, HD * g:HD * g + HD], POOL[:, t, g, :])
                                         for t in range(2)])
                    filled(ins, ("pool", layer, p))
                nq = S * len(streams_of(layer))
                pe.wait_ge(pw_in[layer], 16)
                for p in range(2):
                    out = fill(("poolw", layer, p))
                    wait_taken(pe, ("pool", layer, p))
                    filled(mm(out[:, 0:nq], PW[:, p, :], DT[:, p, 0:nq], start=True, stop=True), ("poolw", layer, p))

            BRANCH_CHUNKS = (range(0, 4), range(4, 6), range(6, 8))

            def merge(layer):
                lo, hi = x_range(layer)
                nq = hi - lo
                for j in range(4):
                    for b in range(3):
                        w = slab(("in", layer, W_IN_GATE + 4 * b + j))
                        for m in range(2):
                            key = ("gate", layer, j, b, m)
                            out = fill(key)
                            filled(chain(out[:, 0:nq], [(w[:, k, P * m:P * m + P], H[:, k, lo:hi])
                                                        for k in range(DC)]), key)
                    w = slab(("proj", layer, j))
                    if j == 0:
                        pe.wait_ge(y_ready[layer], len(attention_units(layer)))
                        for p in range(2):
                            wait_taken(pe, ("poolw", layer, p))
                    for b in range(3):
                        for m in range(2):
                            key = ("proj", layer, j, b, m)
                            out = fill(key)
                            filled(chain(out[:, 0:nq], [(w[:, k, P * m:P * m + P], Y[:, k, 0:nq])
                                                        for k in BRANCH_CHUNKS[b]]), key)

            def out_proj(layer):
                nq = S * len(streams_of(layer))
                wait_taken(pe, ("proj", layer, 3, 2, 1))
                for j in range(4):
                    w = slab(("out", layer, j))
                    for m in range(2):
                        key = ("out", layer, j, m)
                        out = fill(key)
                        filled(chain(out[:, 0:nq], [(w[:, k, P * m:P * m + P], M[:, k, 0:nq])
                                                    for k in range(DC)]), key)

            def feed_forward():
                later = list(MOD_IN_FFN)
                f0 = 0
                for half in range(2):
                    n = HALF_CHUNKS[half]
                    for s in range(n // 2):
                        for name in ("w1", "w3"):
                            w = slab((name, half, s))
                            for m in range(2):
                                key = (name, half, s, m)
                                out = fill(key)
                                for k in range(DC):
                                    if half == 0 and s == 0 and name == "w1" and m == 0:
                                        pe.wait_ge(h_ready[0, 2], 2 * (k + 1))
                                    ins = mm(out[:], w[:, k, P * m:P * m + P], H[:, k, :],
                                             start=k == 0, stop=k == DC - 1)
                                filled(ins, key)
                        if later:
                            mod(later.pop(0))
                    wait_taken(pe, ("w3", half, n // 2 - 1, 1))
                    part = n // 2
                    for j in range(4):
                        outs = [fill(("down", half, j, m)) for m in range(2)]
                        for h in range(2):
                            w = slab(("w2", half, j, h))
                            for m in range(2):
                                for k in range(part):
                                    ins = mm(outs[m][:], w[:, k, P * m:P * m + P], HID[:, h * part + k, :],
                                             start=h == 0 and k == 0, stop=h == 1 and k == part - 1)
                                if h:
                                    filled(ins, ("down", half, j, m))
                        if later:
                            mod(later.pop(0))
                    f0 += n

            def route():
                out = fill(("logit",))
                for t in range(2):
                    for k in range(DC):
                        if t == 0:
                            pe.wait_ge(h_ready[1, 2], k + 1)
                        lo = VEC_COLS["rw"][0] + N_EXPERTS * k
                        ins = mm(out[:, 8 * t:8 * t + 8], H[:, k, S + P * t:S + P * t + P],
                                 VEC[:, lo:lo + N_EXPERTS], start=k == 0, stop=k == DC - 1)
                filled(ins, ("logit",))
                for i in range(4):
                    out = fill(("turn", i))
                    t, half = divmod(i, 2)
                    for c in range(4):
                        ins = nc.tensor.transpose(out[:, P * c:P * c + P],
                                                  H[:, 4 * half + c, S + P * t:S + P * t + P], ident)
                    filled(ins, ("turn", i))
                out = fill(("prefix",))
                pe.wait_ge(sel_ready, 1)
                mm(out[:, 0:8], const("before"), SEL[:, 0, :], start=True, stop=True)
                mm(out[:, 8:16], ones, SEL[:, 0, :], start=True, stop=False)
                mm(out[:, 8:16], const("before"), SEL[:, 1, :], start=False, stop=True)
                mm(out[:, 16:24], ones, SEL[:, 0, :], start=True, stop=False)
                filled(mm(out[:, 16:24], ones, SEL[:, 1, :], start=False, stop=True), ("prefix",))

            up = [bank[0], bank[1]]
            down = [bank[2], bank[3]]
            gath = [bank[4], turned[0]]
            wt_bank = turned[1]
            scat = [turned[1], pv_bank]

            def expert(e, i, again=0):
                pe.wait_ge(onehot_ready, i + 1)
                for b in range(2):
                    for c in range(4):
                        for t in range(2):
                            ins = mm(gath[b][:, SLOTS * c:SLOTS * c + SLOTS],
                                     HTOK[:, t, P * (4 * b + c):P * (4 * b + c) + P], ONEHOT[:, t, :],
                                     start=t == 0, stop=t == 1)
                    ins.then_inc(gathered, 1)
                for t in range(2):
                    ins = nc.tensor.transpose(wt_bank[0:SLOTS, P * t:P * t + P], WEIGHTED[:, t, :], ident)
                ins.then_inc(weights_turned, 1)

                def wait_slab(key):
                    k = EXPERT_AT[key]
                    pe.wait_ge(moe_in[k % MOE_RING], i * (16 * ROUNDS) + 16 * (k // MOE_RING + 1))
                    return moe_slab[k % MOE_RING]

                def up_group(g):
                    if g == 0:
                        pe.wait_ge(he_ready, 2 * i + 2)
                    if g >= 2:
                        pe.wait_ge(ge_ready, i * GROUPS + g - 1)
                    for w in range(2):
                        sl = wait_slab(("up", g, w))[:].rearrange("p (k n) -> p k n", k=DC)
                        for m in range(2):
                            col = (2 * w + m) * SLOTS
                            ins = chain(up[g % 2][:, col:col + SLOTS],
                                        [(sl[:, k, P * m:P * m + P], HE[:, k, :]) for k in range(DC)])
                    ins.then_inc(up_full, 1)

                def down_group(g):
                    sl = wait_slab(("down", g, 0))[:].rearrange("p (k n) -> p k n", k=2)
                    pe.wait_ge(ge_ready, i * GROUPS + g + 1)
                    for k in range(2):
                        for c in range(DC):
                            ins = mm(down[c // 4][:, SLOTS * (c % 4):SLOTS * (c % 4) + SLOTS],
                                     sl[:, k, P * c:P * c + P], GE[:, g % 2, k, :],
                                     start=g == 0 and k == 0 and c % 4 == 0, stop=g == GROUPS - 1 and k == 1,
                                     skip_group_check=True)
                    ins.then_inc(down_done, 1)

                up_group(0)
                for g in range(1, GROUPS):
                    up_group(g)
                    down_group(g - 1)
                down_group(GROUPS - 1)
                pe.wait_ge(ye_dve, i + 1)
                pe.wait_ge(ye_act, i + 1)
                for c in range(DC):
                    ins = nc.tensor.transpose(gath[c // 4][0:SLOTS, P * (c % 4):P * (c % 4) + P], YE[:, c, :], ident)
                ins.then_inc(y_turned, 1)
                pe.wait_ge(ytok_dve, i + 1)
                pe.wait_ge(ytok_act, i + 1)
                pe.wait_ge(scatter_ready, i + 1)
                for n in range(4):
                    if n >= 2:
                        pe.wait_ge(x_added, i * 4 + n - 1)
                    for c in range(2):
                        col = P * (2 * n + c)
                        ins = mm(scat[n % 2][:, S * c:S * c + S], YTOK[:, col:col + P], SCATTER[:],
                                 start=True, stop=True)
                    ins.then_inc(scattered, 1)
                pe.wait_ge(x_added, i * 4 + 4)

            pe.wait_ge(cond_ready, 1)
            pe.wait_ge(consts_in, 16)
            for n in MOD_AT_START:
                mod(n)
            for layer in L:
                norm((layer, 1), 0, T)
                in_proj(layer)
                qk_norm(layer)
                attention(layer)
                pooling(layer)
                merge(layer)
                out_proj(layer)
                if layer == 0:
                    norm((0, 2), 0, T)
                    feed_forward()
                else:
                    norm((1, 2), S, T)
            route()
            for i in range(4):
                wait_taken(pe, ("turn", i))
            pe.wait_ge(counts_ready, 2)
            with pe.Fori(0, N_EXPERTS) as e:
                expert(e, e)

            def skip():
                for s, n in ((gathered, 2), (weights_turned, 1), (up_full, GROUPS), (down_done, GROUPS),
                             (y_turned, 1), (scattered, 4)):
                    pe.sem_inc(s, n)

            overflow_steps(pe, expert, skip)
            out = up[0]
            for c in range(DC):
                pe.wait_ge(sq_ready["final"], c + 1)
                for t in range(2):
                    ins = mm(out[:, t:t + 1], SQ[:, c % 2, P * t:P * t + P], ones[:, 0:1],
                             start=c == 0 and t == 0, stop=c == DC - 1, skip_group_check=True)
                ins.then_inc(sq_used["final"], 1)
            out = up[1]
            pe.wait_ge(rrms_ready["final"], 1)
            for t in range(2):
                ins = mm(out[:, P * t:P * t + P], small["rrms"][:, t:t + 1].to_broadcast([P, P]), ident,
                         start=True, stop=True)
            ins.then_inc(tmp_ready["final"], 1)

        @block.scalar
        def _(act):
            af = nc.scalar.activation

            def squares(key, lo, hi, src_ready):
                src_ready()
                for c in range(DC):
                    if c >= 2:
                        act.wait_ge(sq_used[key], c - 1)
                    af(SQ[:, c % 2, 0:hi - lo], XT[:, c, lo:hi], ACT.Square).then_inc(sq_ready[key], 1)

            def norm(key, lo, hi, src_ready):
                layer, w = key
                squares(key, lo, hi, src_ready)
                wait_full(act, ("stat", key))
                tiles = (hi - lo) // P
                af(small["rms"][:, 0:tiles], acc(("stat", key))[:, 0:tiles], ACT.Sqrt, scale=1.0 / D, bias=eps)\
                    .then_inc(freed(("stat", key)), 1)
                part = 0 if w == 1 else 3
                scale = small["scale1" if w == 1 else "scale2"]
                if w == 1:
                    act.wait_ge(scale_ready, 2 * layer + 1)
                else:
                    act.wait_ge(scale_ready, 2 * layer + 2)
                for c in range(DC):
                    act.wait_ge(tmp_ready[key], c + 1)
                    for n, stream in enumerate((CTX, LAT) if lo == 0 else (LAT,)):
                        col = 2 * c + (1 - stream)
                        af(H[:, c, S * stream:S * stream + S], TMP[:, c % 2, S * n:S * n + S], ACT.Identity,
                           scale=scale[:, col:col + 1], bias=mod_vec(layer, part, c, stream))\
                            .then_inc(h_ready[key], 1)

            def in_proj(layer):
                lo, hi = x_range(layer)
                nq = hi - lo
                for m in range(2):
                    key = ("in", layer, ("bq", m))
                    wait_full(act, key)
                    af(BQ[:, m, 0:nq], acc(key)[:, 0:nq], ACT.Copy, scale=HD ** -0.5).then_inc(freed(key), 1)
                for m in range(2):
                    key = ("in", layer, ("bk", m))
                    wait_full(act, key)
                    af(BK[:, m, :], acc(key)[:], ACT.Copy).then_inc(freed(key), 1)
                for m in range(2):
                    key = ("in", layer, ("bv", m))
                    wait_full(act, key)
                    af(V[:, 2 * m:2 * m + 2, P:384], acc(key)[:].rearrange("p (t n) -> p t n", t=2), ACT.Copy)\
                        .then_inc(freed(key), 1)
                for m in (range(2) if layer == 0 else (1,)):
                    key = ("in", layer, ("u", m))
                    wait_full(act, key)
                    af(U[:, 2 * m:2 * m + 2, :], acc(key)[:].rearrange("p (t n) -> p t n", t=2), ACT.Copy)\
                        .then_inc(freed(key), 1)

            def qk_norm(layer):
                lo, hi = x_range(layer)
                tq = 4 if layer == 0 else 2
                for j in range(5):
                    wait_taken(act, ("in", layer, ("q", j) if j < 4 else ("k", 0)))
                    if j >= 2:
                        act.wait_ge(qk_sq_used[layer], j - 1)
                    n = hi - lo if j < 4 else T
                    af(SQ[:, j % 2, 0:n], QK[:, j, 0:n], ACT.Square).then_inc(qk_sq[layer], 1)
                wait_full(act, ("qkstat", layer))
                cols = 2 * (4 * tq + 4)
                af(small["qks"][:, 0:cols], acc(("qkstat", layer))[:, 0:cols], ACT.Sqrt, scale=1.0 / HD, bias=eps)\
                    .then_inc(freed(("qkstat", layer)), 1)

            def attention(layer):
                units = attention_units(layer)

                def exps(u):
                    stream = units[u][2]
                    act.wait_ge(nm_ready[layer], u + 1)
                    if u >= 2:
                        act.wait_ge(turned_full[layer], u - 1)
                    for t in range(2):
                        col = 2 * u + t
                        if stream == LAT:
                            key = ("score", layer, u, t)
                            src, n = acc(key)[:], T
                        else:
                            key = ("score", layer, u, 0)
                            src, n = acc(key)[:, S * t:S * t + S], S
                        ins = af(PR[:, u % 2, t, 0:n], src, ACT.Exp, bias=small["nm"][:, col:col + 1],
                                 accum_out=small["rs"][:, col:col + 1])
                        if stream == LAT or t == 1:
                            ins.then_inc(freed(key), 1)

                def turned_out(u):
                    stream = units[u][2]
                    act.wait_ge(turned_full[layer], u + 1)
                    if u >= 2:
                        act.wait_ge(pv_full[layer], u - 1)
                    n = 2 if stream == LAT else 1
                    af(PT[:, u % 2, 0:n, :], turned[0][:, 0:S * n].rearrange("p (t n) -> p t n", t=n), ACT.Copy)\
                        .then_inc(turned_out_act[layer], 1)

                def result(u):
                    branch, h, stream = units[u]
                    p0 = HD * (h // 4) if branch == "A" else HD * (h % 2)
                    chunk = h % 4 if branch == "A" else 4 + h // 2
                    col = lat_col(layer) if stream == LAT else 0
                    act.wait_ge(pv_full[layer], u + 1)
                    af(Y[p0:p0 + HD, chunk, col:col + S], pv_bank[p0:p0 + HD, 0:S], ACT.Copy)\
                        .then_inc(y_ready[layer], 1)

                exps(0)
                for u in range(len(units)):
                    if u + 1 < len(units):
                        exps(u + 1)
                    if u:
                        result(u - 1)
                    turned_out(u)
                result(len(units) - 1)

            def pooling(layer):
                nq = S * len(streams_of(layer))
                for p in range(2):
                    key = ("pool", layer, p)
                    wait_full(act, key)
                    af(DT[:, p, 0:nq], acc(key)[:, 0:nq], ACT.Copy).then_inc(freed(key), 1)
                for p in range(2):
                    key = ("poolw", layer, p)
                    wait_full(act, key)
                    lo = VEC_COLS["pscale", layer][0] + p
                    af(Y[:, 6 + p, 0:nq], acc(key)[:, 0:nq], ACT.Copy, scale=VEC[:, lo:lo + 1])\
                        .then_inc(freed(key), 1)

            def merge(layer):
                nq = S * len(streams_of(layer))
                for j in range(4):
                    for b in range(3):
                        for m in range(2):
                            i = 2 * b + m
                            key = ("gate", layer, j, b, m)
                            wait_full(act, key)
                            if j:
                                wait_taken(act, ("proj", layer, j - 1, b, m))
                            af(GATE[:, i, 0:nq], acc(key)[:, 0:nq], ACT.Sigmoid).then_inc(freed(key), 1)

            def feed_forward():
                before = None
                for half in range(2):
                    for s in range(HALF_CHUNKS[half] // 2):
                        for m in range(2):
                            key = ("w1", half, s, m)
                            wait_full(act, key)
                            if before:
                                wait_taken(act, before + (m,))
                            af(SILU[:, m, :], acc(key)[:], ACT.Silu).then_inc(freed(key), 1)
                        before = ("w3", half, s)

            def expert(e, i, again=0):
                act.wait_ge(gathered, 2 * i + 2)
                af(HE[:, 4:8, :], turned[0][:, 0:4 * SLOTS].rearrange("p (c n) -> p c n", c=4), ACT.Copy)\
                    .then_inc(he_ready, 1)
                act.wait_ge(weights_turned, i + 1)
                af(SCATTER[:], turned[1][0:SLOTS, 0:S], ACT.Copy).then_inc(scatter_ready, 1)
                for g in range(GROUPS):
                    act.wait_ge(up_full, i * GROUPS + g + 1)
                    af(SE[:, g % 2, :, :], bank[g % 2][:, 0:2 * SLOTS].rearrange("p (m n) -> p m n", m=2), ACT.Silu)\
                        .then_inc(se_ready, 1)
                act.wait_ge(down_done, i * GROUPS + GROUPS)
                af(YE[:, 4:8, :], bank[3][:, 0:4 * SLOTS].rearrange("p (c n) -> p c n", c=4), ACT.Copy)\
                    .then_inc(ye_act, 1)
                act.wait_ge(y_turned, i + 1)
                af(YTOK[:, 512:1024], turned[0][0:SLOTS, :], ACT.Copy).then_inc(ytok_act, 1)

            act.wait_ge(vecs_in, 16)
            act.wait_ge(cond_zeroed, 1)
            af(small["cond"][:].rearrange("p (k n) -> p k n", n=32)[:, :, 0:2],
               vec("cond").rearrange("p (k n) -> p k n", n=2), ACT.Silu).then_inc(cond_ready, 1)
            act.wait_ge(consts_in, 16)
            for layer in L:
                if layer == 0:
                    norm((0, 1), 0, T, lambda: act.wait_ge(x_in, 16))
                else:
                    norm((1, 1), 0, T, lambda: wait_taken(act, ("down", 1, 3, 1)))
                in_proj(layer)
                qk_norm(layer)
                attention(layer)
                pooling(layer)
                merge(layer)
                lo, hi = x_range(layer)
                norm((layer, 2), lo, hi, lambda: wait_taken(act, ("out", layer, 3, 1)))
                if layer == 0:
                    feed_forward()
            act.wait_ge(routed, 1)
            af(EX[:], R1[:], ACT.Exp).then_inc(ex_ready, 1)
            with act.Fori(0, N_EXPERTS) as e:
                expert(e, e)

            def skip():
                for s, n in ((he_ready, 1), (scatter_ready, 1), (se_ready, GROUPS), (ye_act, 1), (ytok_act, 1)):
                    act.sem_inc(s, n)

            overflow_steps(act, expert, skip)
            for c in range(DC):
                if c >= 2:
                    act.wait_ge(sq_used["final"], c - 1)
                af(SQ[:, c % 2, 0:S], XT[:, c, S:T], ACT.Square).then_inc(sq_ready["final"], 1)
            act.wait_ge(sq_used["final"], DC)
            af(small["rms"][:, 0:2], bank[0][:, 0:2], ACT.Sqrt, scale=1.0 / D, bias=eps)\
                .then_inc(final_rms, 1)

        @block.vector
        def _(dve):
            v = nc.vector
            seq = [0]

            def link(ins):
                seq[0] += 1
                ins.then_inc(dve_seq, 1)
                dve.wait_ge(dve_seq, seq[0])

            def mod(n):
                rows = slice(32 * (n % 4), 32 * (n % 4) + 32)
                wait_full(dve, ("mod", n))
                v.tensor_copy(small["modrow"][rows, :], acc(("mod", n))[rows, 0:256]).then_inc(freed(("mod", n)), 1)
                if n % 4 < 3:
                    return
                key = ("turned_mod", n // 4)
                wait_full(dve, key)
                layer, g = divmod(n // 4, 6)
                lo = VEC_COLS["bmod", layer][0] + 8 * g
                src = acc(key)[:, 0:2 * P].rearrange("p (m q r) -> p q m r", m=2, q=4)[:, :, :, 0:2]
                b = VEC[:, lo:lo + 8].rearrange("p (q m) -> p q m", q=4).unsqueeze(3).to_broadcast([P, 4, 2, 2])
                v.tensor_tensor(MOD[layer][:, 16 * g:16 * g + 16].rearrange("p (q m r) -> p q m r", q=4, m=2),
                                src, b, ALU.add).then_inc(freed(key), 1)

            def scale(layer, w):
                wait_taken(dve, ("turned_mod", 6 * layer + (1 if w == 1 else 4)))
                part = 1 if w == 1 else 4
                lo = VEC_COLS[f"g{w}", layer][0]
                g = VEC[:, lo:lo + DC].unsqueeze(2).to_broadcast([P, DC, 2])
                v.scalar_tensor_tensor(
                    small[f"scale{w}"][:].rearrange("p (a b) -> p a b", b=2),
                    MOD[layer][:, 16 * part:16 * part + 16].rearrange("p (a b) -> p a b", b=2),
                    1.0, g, ALU.add, ALU.mult).then_inc(scale_ready, 1)

            def norm(key, lo, hi):
                tiles = (hi - lo) // P
                n = FILLS["stat", key]
                dve.wait_ge(free[n % BANKS], n // BANKS + 1)
                v.reciprocal(small["rrms"][:, 0:tiles], small["rms"][:, 0:tiles]).then_inc(rrms_ready[key], 1)
                wait_full(dve, ("bcast", key))
                streams = 2 if lo == 0 else 1
                for c in range(DC):
                    if c >= 2:
                        dve.wait_ge(h_ready[key], streams * (c - 1))
                    v.tensor_tensor(TMP[:, c % 2, 0:hi - lo], XT[:, c, lo:hi], acc(("bcast", key))[:, 0:hi - lo],
                                    ALU.mult).then_inc(tmp_ready[key], 1)
                dve.wait_ge(tmp_ready[key], DC)
                dve.sem_inc(freed(("bcast", key)), 1)

            def in_proj(layer):
                lo, hi = x_range(layer)
                for j in range(5):
                    key = ("in", layer, ("q", j) if j < 4 else ("k", 0))
                    n = hi - lo if j < 4 else T
                    wait_full(dve, key)
                    v.tensor_copy(QK[:, j, 0:n], acc(key)[:, 0:n]).then_inc(freed(key), 1)
                key = ("in", layer, ("av", 0))
                wait_full(dve, key)
                v.tensor_copy(V[:, :, 0:P], acc(key)[:].rearrange("p (t n) -> p t n", t=4)).then_inc(freed(key), 1)

            def bias(layer):
                dve.wait_ge(bias_in[layer], 16)
                dve.wait_ge(consts_in, 16)
                for qt in range(2):
                    view = BIAS[:, qt, :, :].rearrange("p h (r c) -> p (h r) c", c=GRID_W)
                    v.tensor_tensor(view, view, const("wmask").unsqueeze(1).to_broadcast([P, 16, GRID_W]), ALU.add)\
                        .then_inc(bias_ready[layer], 1)

            def qk_norm(layer):
                lo, hi = x_range(layer)
                tq = 4 if layer == 0 else 2
                cols = 2 * (4 * tq + 4)
                q_lo, k_lo = VEC_COLS["gq", layer][0], VEC_COLS["gk", layer][0]
                link(v.tensor_scalar(small["gq8"][:], VEC[:, q_lo:q_lo + 1], HD ** -0.5, None, ALU.mult))
                wait_taken(dve, ("qkstat", layer))
                v.reciprocal(small["qkr"][:, 0:cols], small["qks"][:, 0:cols]).then_inc(qk_rrms[layer], 1)
                for j in range(5):
                    key = ("qkb", layer, j)
                    n = hi - lo if j < 4 else T
                    gain = small["gq8"][:, 0:1] if j < 4 else VEC[:, k_lo:k_lo + 1]
                    wait_full(dve, key)
                    v.scalar_tensor_tensor(QK[:, j, 0:n], QK[:, j, 0:n], gain, acc(key)[:, 0:n], ALU.mult, ALU.mult)\
                        .then_inc(freed(key), 1)
                for j in range(5):
                    key = ("rope", layer, j)
                    c = lat_col(layer) if j < 4 else S
                    x = QK[:, j, c:c + S]
                    wait_full(dve, key)
                    v.tensor_tensor(small["t1"][:], acc(key)[:, 0:S], const("sin"), ALU.mult).then_inc(freed(key), 1)
                    n = FILLS[key]
                    link(v.tensor_tensor(x, x, const("cos"), ALU.mult))
                    dve.wait_ge(free[n % BANKS], n // BANKS + 1)
                    v.tensor_tensor(x, x, small["t1"][:], ALU.add).then_inc(qk_ready[layer], 1)
                    dve.wait_ge(qk_ready[layer], j + 1)

            def attention(layer):
                units = attention_units(layer)

                def maxima(u):
                    branch, h, stream = units[u]
                    for t in range(2):
                        col = 2 * u + t
                        if stream == LAT:
                            key = ("score", layer, u, t)
                            wait_full(dve, key)
                            src = acc(key)[:]
                            if branch == "B":
                                link(v.tensor_tensor(acc(key)[:, S:T], acc(key)[:, S:T], BIAS[:, t, h, :], ALU.add))
                        else:
                            key = ("score", layer, u, 0)
                            if t == 0:
                                wait_full(dve, key)
                            src = acc(key)[:, S * t:S * t + S]
                        ins = v.reduce_max(small["mx"][:, col:col + 1], src, AX)
                    link(ins)
                    v.tensor_scalar(small["nm"][:, 2 * u:2 * u + 2], small["mx"][:, 2 * u:2 * u + 2], -1.0, None,
                                    ALU.mult).then_inc(nm_ready[layer], 1)

                def normalise(u):
                    stream = units[u][2]
                    for q in range(2 if stream == LAT else 1):
                        wait_taken(dve, ("score", layer, u, q))
                    link(v.reciprocal(small["ri"][:, 2 * u:2 * u + 2], small["rs"][:, 2 * u:2 * u + 2]))
                    n = T if stream == LAT else S
                    for t in range(2):
                        p = PR[:, u % 2, t, 0:n]
                        ins = v.tensor_scalar(p, p, small["ri"][:, 2 * u + t:2 * u + t + 1], None, ALU.mult)
                    ins.then_inc(p_ready[layer], 1)

                def turned_out(u):
                    stream = units[u][2]
                    dve.wait_ge(turned_full[layer], u + 1)
                    if u >= 2:
                        dve.wait_ge(pv_full[layer], u - 1)
                    n = 2 if stream == LAT else 1
                    v.tensor_copy(PT[:, u % 2, n:2 * n, :], turned[1][:, 0:S * n].rearrange("p (t n) -> p t n", t=n))\
                        .then_inc(turned_out_dve[layer], 1)

                maxima(0)
                for u in range(len(units)):
                    if u + 1 < len(units):
                        maxima(u + 1)
                    normalise(u)
                    turned_out(u)
                    if layer == 0:
                        mod(MOD_IN_ATTENTION[u])

            def merge(layer):
                nq = S * len(streams_of(layer))
                for j in range(4):
                    for b in range(3):
                        for m in range(2):
                            key = ("proj", layer, j, b, m)
                            g = GATE[:, 2 * b + m, 0:nq]
                            dst = M[:, 2 * j + m, 0:nq]
                            wait_taken(dve, ("gate", layer, j, b, m))
                            wait_full(dve, key)
                            if b == 0:
                                v.tensor_tensor(dst, g, acc(key)[:, 0:nq], ALU.mult).then_inc(freed(key), 1)
                            else:
                                link(v.tensor_tensor(TMP[:, m, 0:nq], g, acc(key)[:, 0:nq], ALU.mult))
                                wait_taken(dve, ("proj", layer, j, b - 1, m))
                                v.tensor_tensor(dst, dst, TMP[:, m, 0:nq], ALU.add).then_inc(freed(key), 1)

            def residual(layer, part, key, c):
                streams = streams_of(layer)
                wait_full(dve, key)
                for n, stream in enumerate(streams):
                    x = XT[:, c, S * stream:S * stream + S]
                    ins = v.scalar_tensor_tensor(x, acc(key)[:, S * n:S * n + S], mod_vec(layer, part, c, stream), x,
                                                 ALU.mult, ALU.add)
                ins.then_inc(freed(key), 1)

            def feed_forward():
                later = list(MOD_IN_FFN)
                for half in range(2):
                    for s in range(HALF_CHUNKS[half] // 2):
                        for m in range(2):
                            k1, k3 = ("w1", half, s, m), ("w3", half, s, m)
                            wait_taken(dve, k1)
                            wait_full(dve, k3)
                            v.tensor_tensor(HID[:, 2 * s + m, :], SILU[:, m, :], acc(k3)[:], ALU.mult)\
                                .then_inc(freed(k3), 1)
                        if later:
                            mod(later.pop(0))
                    for j in range(4):
                        for m in range(2):
                            key = ("down", half, j, m)
                            residual(0, 5, key, 2 * j + m)
                        if later:
                            mod(later.pop(0))

            def route():
                wait_full(dve, ("logit",))
                rb = vec("rb").unsqueeze(1).to_broadcast([P, 2, 8])
                lg = R1
                link(v.tensor_tensor(lg[:], acc(("logit",))[:, 0:16].rearrange("p (t e) -> p t e", t=2), rb, ALU.add))
                dve.sem_inc(freed(("logit",)), 1)
                mine = lg[:].unsqueeze(3).to_broadcast([P, 2, 8, 8])
                other = lg[:].unsqueeze(2).to_broadcast([P, 2, 8, 8])
                low = const("lower").rearrange("p (a b) -> p a b", a=8).unsqueeze(1).to_broadcast([P, 2, 8, 8])
                link(v.tensor_tensor(CMP[:], other, mine, ALU.is_equal))
                link(v.tensor_tensor(CMP[:], CMP[:], low, ALU.mult))
                link(v.tensor_tensor(CMP2[:], other, mine, ALU.is_gt))
                link(v.tensor_tensor(CMP[:], CMP[:], CMP2[:], ALU.add))
                link(v.tensor_reduce(RANK[:], CMP[:], AX, ALU.add))
                v.tensor_scalar(SEL[:], RANK[:], 2.0, None, ALU.is_lt).then_inc(sel_ready, 1)
                link(v.reduce_max(RM[:], lg[:], AX))
                v.tensor_tensor(lg[:], lg[:], RM[:].unsqueeze(2).to_broadcast([P, 2, 8]), ALU.subtract)\
                    .then_inc(routed, 1)
                for i in range(4):
                    key = ("turn", i)
                    wait_full(dve, key)
                    t, half = divmod(i, 2)
                    v.tensor_copy(HTOK[:, t, 512 * half:512 * half + 512], acc(key)[:]).then_inc(freed(key), 1)
                dve.wait_ge(ex_ready, 1)
                link(v.tensor_tensor(EX[:], EX[:], SEL[:], ALU.mult))
                link(v.tensor_reduce(RSUM[:], EX[:], AX, ALU.add))
                link(v.reciprocal(RINV[:], RSUM[:]))
                link(v.tensor_tensor(W[:], EX[:], RINV[:].unsqueeze(2).to_broadcast([P, 2, 8]), ALU.mult))
                wait_full(dve, ("prefix",))
                src = acc(("prefix",))
                link(v.scalar_tensor_tensor(POS1[:], src[:, 0:16].rearrange("p (t e) -> p t e", t=2), 1.0, SEL[:],
                                            ALU.add, ALU.mult))
                link(v.tensor_scalar(POS[:], POS1[:], -1.0, None, ALU.add))
                link(v.tensor_copy(COUNTF[:], src[:, 16:24]))
                dve.sem_inc(freed(("prefix",)), 1)
                v.tensor_copy(COUNT[:], COUNTF[:]).then_inc(counts_ready, 1)
                link(v.reduce_max(MAXF[:], COUNTF[:], AX))
                v.tensor_copy(MAXI[:], MAXF[:]).then_inc(counts_ready, 1)
            def expert(e, i, again=0):
                iota = const("iota")[:, SLOTS * again:SLOTS * (again + 1)]
                for t in range(2):
                    pos = POS[:, t, bass.ds(e, 1)]
                    v.tensor_scalar(ONEHOT[:, t, :], iota, pos, None, ALU.is_equal)
                for t in range(2):
                    ins = v.tensor_scalar(WEIGHTED[:, t, :], iota, POS[:, t, bass.ds(e, 1)],
                                          W[:, t, bass.ds(e, 1)], ALU.is_equal, ALU.mult)
                ins.then_inc(onehot_ready, 1)
                dve.wait_ge(gathered, 2 * i + 1)
                v.tensor_copy(HE[:, 0:4, :], bank[4][:, 0:4 * SLOTS].rearrange("p (c n) -> p c n", c=4))\
                    .then_inc(he_ready, 1)
                for g in range(GROUPS):
                    dve.wait_ge(se_ready, i * GROUPS + g + 1)
                    v.tensor_tensor(GE[:, g % 2, :, :], SE[:, g % 2, :, :],
                                    bank[g % 2][:, 2 * SLOTS:4 * SLOTS].rearrange("p (m n) -> p m n", m=2), ALU.mult)\
                        .then_inc(ge_ready, 1)
                dve.wait_ge(down_done, i * GROUPS + GROUPS)
                v.tensor_copy(YE[:, 0:4, :], bank[2][:, 0:4 * SLOTS].rearrange("p (c n) -> p c n", c=4))\
                    .then_inc(ye_dve, 1)
                dve.wait_ge(y_turned, i + 1)
                v.tensor_copy(YTOK[:, 0:512], bank[4][0:SLOTS, :]).then_inc(ytok_dve, 1)
                for n in range(4):
                    dve.wait_ge(scattered, 4 * i + n + 1)
                    for c in range(2):
                        x = XT[:, 2 * n + c, S:T]
                        ins = v.scalar_tensor_tensor(x, (turned[1], pv_bank)[n % 2][:, S * c:S * c + S],
                                                     mod_vec(1, 5, 2 * n + c, LAT), x, ALU.mult, ALU.add)
                    ins.then_inc(x_added, 1)

            v.memset(small["cond"][:], 0.0).then_inc(cond_zeroed, 1)
            dve.wait_ge(vecs_in, 16)
            for n in MOD_AT_START:
                mod(n)
            for layer in L:
                scale(layer, 1)
                norm((layer, 1), 0, T)
                in_proj(layer)
                bias(layer)
                qk_norm(layer)
                attention(layer)
                merge(layer)
                for c in range(DC):
                    residual(layer, 2, ("out", layer, c // 2, c % 2), c)
                scale(layer, 2)
                lo, hi = x_range(layer)
                norm((layer, 2), lo, hi)
                if layer == 0:
                    feed_forward()
            route()
            with dve.Fori(0, N_EXPERTS) as e:
                expert(e, e)

            def skip():
                for s, n in ((onehot_ready, 1), (he_ready, 1), (ge_ready, GROUPS), (ye_dve, 1), (ytok_dve, 1),
                             (x_added, 4)):
                    dve.sem_inc(s, n)

            overflow_steps(dve, expert, skip)
            dve.wait_ge(final_rms, 1)
            v.reciprocal(small["rrms"][:, 0:2], small["rms"][:, 0:2]).then_inc(rrms_ready["final"], 1)
            dve.wait_ge(tmp_ready["final"], 1)
            lo = VEC_COLS["final"][0]
            for c in range(DC):
                v.scalar_tensor_tensor(OUT[:, c, :], XT[:, c, S:T], VEC[:, lo + c:lo + c + 1], bank[1][:, 0:S],
                                       ALU.mult, ALU.mult).then_inc(out_ready, 1)


def constants():
    c = np.zeros((P, N_CONST), np.float32)

    def put(name, value):
        lo, hi = CONST_COLS[name]
        c[:, lo:hi] = value

    put("ident", np.eye(P))
    put("ones", 1.0)
    p = np.arange(P)
    partner = np.where(p % 32 < 16, p + 16, p - 16)
    perm = np.zeros((P, P))
    perm[partner, p] = 1.0
    put("perm", perm)
    put("before", p[:, None] < p[None, :])
    put("blk2", p[:, None] // HD == np.arange(2)[None, :])
    t = np.arange(S)
    pos = np.stack([t // GRID_W, t % GRID_W], -1).astype(np.float32)
    inv_freq = np.float32(10000.0) ** (-np.arange(0, 32, 2, dtype=np.float32) / np.float32(32))
    ang = pos[:, :, None] * inv_freq[None, None, :]
    axis, i = (p % HD) // 32, p % 16
    put("cos", np.cos(ang)[:, axis, i].T)
    put("sin", np.sin(ang)[:, axis, i].T * np.where(p % 32 < 16, -1.0, 1.0)[:, None])
    col = p % GRID_W
    start = np.clip(col - 8, 0, GRID_W - 16)
    kc = np.arange(GRID_W)[None, :]
    put("wmask", np.where((kc >= start[:, None]) & (kc < start[:, None] + 16), 0.0, MASKED))
    put("iota", np.arange(PASSES * SLOTS))
    e = np.arange(8)
    put("lower", (e[None, :] < e[:, None]).reshape(1, 64))
    put("eps", EPS)
    pool = np.zeros((S, 4, S), np.float32)
    for g, w in enumerate((2, 4, 8, 16)):
        for out in range(S):
            lo, hi = max(out - w // 2, 0), min(out - w // 2 + w, S)
            pool[lo:hi, g, out] = 1.0 / (hi - lo)
            pool[out, g, out] -= 1.0
    pool = pool.reshape(2, P, 4 * S).transpose(1, 0, 2).reshape(P, -1)
    return c, np.ascontiguousarray(pool)


def slabs(w):
    k, n = w.shape
    w = w.reshape(k // P, P, n // 256, 256).transpose(2, 1, 0, 3)
    return np.ascontiguousarray(w).reshape(n // 256, P, k // P * 256)


def by_chunk(x):
    return x.reshape(-1, P).T


_ORDER = ["w_mod", "w_in", "w_proj", "w_out", "ffn_w1", "ffn_w3", "ffn_w2_0", "ffn_w2_1", "moe_w1", "moe_w3",
          "moe_w2", "xt", "vecs", "consts", "pool_mat", "pool_w", "rel_bias"]


def layout(x, c, ctx, c_ctx, w_mod, b_mod, norm1_g, norm2_g, w_in, q_norm_g, k_norm_g, na_rel_bias, pool_w,
           pool_scale, w_branch_a, w_branch_b, w_branch_c, w_out, ffn_w1, ffn_w3, ffn_w2, router_w, router_b,
           moe_w1, moe_w3, moe_w2, final_g):
    a = {}
    heads = np.array([h for j in range(4) for h in (j, 4 + j)])
    cols = (heads[:, None] * HD + np.arange(HD)).reshape(-1)
    w_in = np.concatenate([w_in[:, :, cols], w_in[:, :, 512:]], axis=2)
    a["w_mod"] = np.concatenate([slabs(w) for w in w_mod])
    a["w_in"] = np.concatenate([slabs(w) for w in w_in])
    proj = np.concatenate([w_branch_a[:, cols], w_branch_b, w_branch_c], axis=1)
    a["w_proj"] = np.concatenate([slabs(w) for w in proj])
    a["w_out"] = np.concatenate([slabs(w) for w in w_out])
    a["ffn_w1"], a["ffn_w3"] = slabs(ffn_w1[0]), slabs(ffn_w3[0])
    f0 = 0
    for half, n in enumerate(HALF_CHUNKS):
        parts = [slabs(ffn_w2[0, P * (f0 + h * n // 2):P * (f0 + (h + 1) * n // 2)]) for h in range(2)]
        a[f"ffn_w2_{half}"] = np.stack(parts, 1).reshape(8, P, -1)
        f0 += n
    for name, w in (("moe_w1", moe_w1), ("moe_w3", moe_w3)):
        w = w[0].reshape(N_EXPERTS, DC, P, GROUPS, 256).transpose(0, 3, 2, 1, 4)
        a[name] = np.ascontiguousarray(w).reshape(-1, SLAB)
    w = moe_w2[0].reshape(N_EXPERTS, GROUPS, 2, P, D).transpose(0, 1, 3, 2, 4)
    a["moe_w2"] = np.ascontiguousarray(w).reshape(-1, SLAB)
    xt = np.concatenate([ctx[0], x[0]], axis=0).T.reshape(DC, P, T).transpose(1, 0, 2)
    a["xt"] = np.ascontiguousarray(xt).reshape(P, DC * T)
    vecs = np.zeros((P, N_VEC), np.float32)

    def put(name, value):
        lo, hi = VEC_COLS[name]
        vecs[:, lo:hi] = value

    for l in range(DEPTH):
        put(("bmod", l), by_chunk(b_mod[l]))
        put(("g1", l), by_chunk(norm1_g[l]))
        put(("g2", l), by_chunk(norm2_g[l]))
        put(("gq", l), np.concatenate([q_norm_g[l]] * 2)[:, None])
        put(("gk", l), np.concatenate([k_norm_g[l]] * 2)[:, None])
        put(("pscale", l), by_chunk(pool_scale[l]))
    put("final", by_chunk(final_g))
    put("cond", np.stack([by_chunk(c[0]), by_chunk(c_ctx)], -1).reshape(P, 2 * DC))
    put("rw", router_w[0].reshape(DC, P, N_EXPERTS).transpose(1, 0, 2).reshape(P, -1))
    put("rb", router_b[0][None, :])
    a["vecs"] = vecs
    a["consts"], a["pool_mat"] = constants()
    pw = np.zeros((DEPTH, 2, HD, 2, 2, HD), np.float32)
    for g in range(4):
        pw[:, g % 2, :, g // 2, g % 2, :] = pool_w[:, g]
    a["pool_w"] = pw.reshape(DEPTH, P, 2 * P)
    t = np.arange(S)
    dr = t[None, :] // GRID_W - t[:, None] // GRID_W + 7
    dc = np.clip(t[None, :] % GRID_W - t[:, None] % GRID_W + 15, 0, 30)
    a["rel_bias"] = np.ascontiguousarray(
        na_rel_bias[:, :, dr, dc].reshape(DEPTH, 4, 2, P, S).transpose(0, 3, 2, 1, 4)).reshape(DEPTH, P, -1)
    return a


def kernel(**inputs):
    import concourse.bacc as bacc
    from concourse.bass_utils import run_bass_kernel_spmd

    arrays = layout(**{k: np.asarray(v) for k, v in inputs.items()})
    nc = bacc.Bacc("TRN2", target_bir_lowering=False, num_devices=1)
    aps = {}
    for name in _ORDER:
        arr = arrays[name]
        aps[name] = nc.dram_tensor(f"in_{name}", arr.shape, mybir.dt.from_np(arr.dtype), kind="ExternalInput").ap()
    aps["out"] = nc.dram_tensor("out_t", (P, DC * S), F32, kind="ExternalOutput").ap()
    build(nc, aps)
    r = run_bass_kernel_spmd(nc, [{f"in_{n}": arrays[n] for n in _ORDER}], core_ids=[0])
    out = np.asarray(r.results[0]["out_t"]).reshape(P, DC, S)
    return np.ascontiguousarray(out.transpose(2, 1, 0)).reshape(1, S, D)
```

```python
from contextlib import ExitStack

import numpy as np

import concourse.bass as bass
from concourse import mybir

F32 = mybir.dt.float32
F32R = mybir.dt.float32r
I32 = mybir.dt.int32
ALU = mybir.AluOpType
ACT = mybir.ActivationFunctionType
AX = mybir.AxisListType.X

P = 128
D = 1024
DC = D // P
S = 256
T = 2 * S
CTX, LAT = 0, 1
DEPTH = 2
HD = 64
GRID_W = 64
KEY_TILES = T // P
F_DENSE = 2816
FC = F_DENSE // P
PART_CHUNKS = (8, 8, 6)
N_EXPERTS = 8
F_EXPERT = 3584
GROUPS = F_EXPERT // 256
SLOTS = 96
PASSES = -(-S // SLOTS)
EPS = 1e-6
SLAB = 2048
RING = 3
MOE_RING = 7
MOE_SPLIT = 3
LO_DVE = 3
BANKS = 5
MASKED = -1e30

CONST_COLS = {}
_at = 0
for _name, _n in (("ident", P), ("ones", P), ("perm", P), ("before", P), ("blk2", 2), ("cos", S), ("sin", S),
                  ("wmask", GRID_W), ("iota", PASSES * SLOTS), ("lower", 64), ("eps", 1)):
    CONST_COLS[_name] = (_at, _at + _n)
    _at += _n
N_CONST = _at
VEC_COLS = {}
_at = 0
for _name, _n in (("bmod", 48), ("g1", DC), ("g2", DC), ("gq", 1), ("gk", 1), ("pscale", 2)):
    for _l in range(DEPTH):
        VEC_COLS[_name, _l] = (_at, _at + _n)
        _at += _n
for _name, _n in (("final", DC), ("cond", 2 * DC), ("rw", DC * N_EXPERTS), ("rb", N_EXPERTS)):
    VEC_COLS[_name] = (_at, _at + _n)
    _at += _n
N_VEC = _at

W_IN_Q = (0, 1)
W_IN_KV, W_IN_BQ, W_IN_BK, W_IN_BV, W_IN_U, W_IN_GATE = 2, 3, 4, 5, 6, 7


MOD_AT_START, MOD_IN_ATTENTION, MOD_IN_FFN = range(8), range(8, 32), range(32, 48)


def attention_units(layer):
    streams = (LAT, CTX) if layer == 0 else (LAT,)
    return [(b, h, s) for b, n in (("A", 8), ("B", 4)) for s in streams for h in range(n)]


def is_split(slab):
    return slab[0] == "in" and slab[1] == 0 or slab[0] in ("w1", "w3", "w2")


def schedule():
    slabs, fills = [], []

    def mod(n):
        slabs.append(("mod", n))
        fills.append(("mod", n))
        if n % 4 == 3:
            fills.append(("turned_mod", n // 4))

    def norm(key):
        fills.extend([("stat", key), ("bcast", key)])

    for n in MOD_AT_START:
        mod(n)
    for layer in range(DEPTH):
        norm((layer, 1))
        for s in range(7):
            slabs.append(("in", layer, s))
        names = [("q", j) for j in range(4)] + [("k", 0), ("av", 0), ("bq", 0), ("bq", 1), ("bk", 0), ("bk", 1),
                                                ("bv", 0), ("bv", 1)]
        if layer == 0:
            names.insert(names.index(("av", 0)) + 1, ("av", 1))
        names += [("u", 0), ("u", 1)] if layer == 0 else [("u", 1)]
        fills.extend(("in", layer, n) for n in names)
        fills.append(("qkstat", layer))
        fills.extend(("qkb", layer, j) for j in range(5))
        fills.extend(("rope", layer, j) for j in range(5))
        units = attention_units(layer)
        for u in range(2):
            fills.extend(("score", layer, u, q) for q in range(2 if units[u][2] == LAT else 1))
        for u in range(len(units)):
            if u + 2 < len(units):
                fills.extend(("score", layer, u + 2, q) for q in range(2 if units[u + 2][2] == LAT else 1))
            if layer == 0:
                mod(MOD_IN_ATTENTION[u])
        fills.extend(("pool", layer, p) for p in range(2))
        fills.extend(("poolw", layer, p) for p in range(2))
        for j in range(4):
            slabs.extend(("in", layer, W_IN_GATE + 4 * b + j) for b in range(3))
            fills.extend(("gate", layer, j, b, m) for b in range(3) for m in range(2))
            slabs.append(("proj", layer, j))
            fills.extend(("proj", layer, j, b, m) for b in range(3) for m in range(2))
        for j in range(4):
            slabs.append(("out", layer, j))
            fills.extend(("out", layer, j, m) for m in range(2))
        norm((layer, 2))
        if layer == 0:
            later = list(MOD_IN_FFN)
            for part, n in enumerate(PART_CHUNKS):
                for s in range(n // 2):
                    slabs.extend([("w1", part, s), ("w3", part, s)])
                    fills.extend([("w1", part, s, 0), ("w1", part, s, 1), ("w3", part, s, 0), ("w3", part, s, 1)])
                    if later:
                        mod(later.pop(0))
                for j in range(4):
                    slabs.append(("w2", part, j))
                    fills.extend(("down", part, j, m) for m in range(2))
                    if later:
                        mod(later.pop(0))
            assert not later
    fills.append(("logit",))
    fills.extend(("turn", i) for i in range(4))
    fills.append(("prefix",))
    return {k: n for n, k in enumerate(slabs)}, {k: n for n, k in enumerate(fills)}


SLABS, FILLS = schedule()
SPLITS = {k: n for n, k in enumerate(k for k in SLABS if is_split(k))}


def last_fill(slab):
    kind = slab[0]
    if kind == "mod":
        return slab
    if kind == "in":
        _, layer, s = slab
        if s >= W_IN_GATE:
            b, j = divmod(s - W_IN_GATE, 4)
            return ("gate", layer, j, b, 1)
        return ("in", layer, (("q", 1), ("q", 3), ("av", 1 - layer), ("bq", 1), ("bk", 1), ("bv", 1), ("u", 1))[s])
    if kind == "proj":
        return ("proj", slab[1], slab[2], 2, 1)
    if kind == "out":
        return ("out", slab[1], slab[2], 1)
    if kind in ("w1", "w3"):
        return slab + (1,)
    return ("down", slab[1], slab[2], 1)

EXPERT_SLABS = []
for _g in range(GROUPS):
    EXPERT_SLABS += [("up", _g, 0), ("up", _g, 1)]
    if _g:
        EXPERT_SLABS.append(("down", _g - 1))
EXPERT_SLABS.append(("down", GROUPS - 1))
EXPERT_AT = {k: n for n, k in enumerate(EXPERT_SLABS)}
N_EXPERT_SLABS = len(EXPERT_SLABS)
ROUNDS = N_EXPERT_SLABS // MOE_RING
assert ROUNDS * MOE_RING == N_EXPERT_SLABS and N_EXPERT_SLABS % MOE_SPLIT == 0


def build(nc, a):
    with ExitStack() as ctx:
        base = -(-nc.sbuf_base // 32) * 32

        def at(name, kb, shape, dt=F32):
            return nc.alloc_sbuf_tensor_at(name, shape, dt, offset=base + -(-int(kb * 1024) // 32) * 32)

        def sem(name):
            return ctx.enter_context(nc.semaphore(name))

        def psum(name, shape):
            return ctx.enter_context(nc.psum_tensor(name, shape, F32))

        ring = [at(f"slab{i}", 8 * i, [P, DC, 256]) for i in range(RING)]
        w_hi = [at(f"w_hi{i}", 24 + 8 * i, [P, DC, 256], F32R) for i in range(2)]
        w_lo = [at(f"w_lo{i}", 40 + 8 * i, [P, DC, 256], F32R) for i in range(2)]
        Y = at("Y", 56, [P, DC, T])
        QK = at("QK", 72, [P, 5, T])
        BQ = at("BQ", 82, [P, 2, T])
        BK = at("BK", 86, [P, 2, T])
        V = at("V", 90, [P, KEY_TILES, 384])
        U = at("U", 96, [P, KEY_TILES, 256])
        M = at("M", 72, [P, DC, T])
        GATE = at("GATE", 88, [P, 6, T])
        HID_HI = at("HID_HI", 56, [P, 8, T], F32R)
        HID_LO = at("HID_LO", 72, [P, 8, T], F32R)
        HID = at("HID", 88, [P, 4, T])
        SILU = at("SILU", 96, [P, 2, T])
        H_LO = at("H_LO", 100, [P, DC, T], F32R)
        XT = at("XT", 116, [P, DC, T])
        H_HI = at("H_HI", 132, [P, DC, T], F32R)
        H = at("H", 132, [P, DC, T])
        BIAS = at("BIAS", 148, [P, 2, 4, S])
        POOL = at("POOL", 156, [P, 2, 4, S])
        PR = at("PR", 164, [P, 2, 2, T])
        PT = at("PT", 172, [P, 2, 4, S])
        SQ = at("SQ", 180, [P, 2, T])
        TMP = at("TMP", 184, [P, 2, T])
        DT = at("DT", 164, [P, 2, T])
        H_NEW = at("H_NEW", 168, [P, 4, T])
        PW = at("PW", 188, [P, 2, P])
        CONST = at("CONST", 189, [P, N_CONST])
        VEC = at("VEC", 195, [P, N_VEC])
        kb = 195 + N_VEC * 4 / 1024
        small = {}
        for name, n in (("cond", 32 * DC), ("modrow", 256), ("mod0", 96), ("mod1", 96), ("scale1", 2 * DC), ("scale2", 2 * DC),
                        ("rms", 4), ("rrms", 4), ("qks", 40), ("qkr", 40), ("gq8", 1),
                        ("mx", 48), ("nm", 48), ("rs", 48), ("ri", 48), ("t1", S)):
            kb = -(-kb * 1024 // 32) * 32 / 1024
            small[name] = at(f"s_{name}", kb, [P, n])
            kb += n * 4 / 1024
        assert kb <= 207, kb
        moe_slab = [at(f"moe_slab{i}", 8 * i, [P, 4, 512]) for i in range(MOE_RING)]
        moe_hi = [at(f"moe_hi{i}", 56 + 8 * i, [P, 4, 512], F32R) for i in range(MOE_SPLIT)]
        moe_lo = [at(f"moe_lo{i}", 80 + 8 * i, [P, 4, 512], F32R) for i in range(MOE_SPLIT)]
        HTOK = at("HTOK", 152, [P, 2, D])
        HE_HI = at("HE_HI", 160, [P, DC, SLOTS], F32R)
        HE_LO = at("HE_LO", 163, [P, DC, SLOTS], F32R)
        SE = at("SE", 166, [SLOTS, 2, 256])
        GT = at("GT", 168, [SLOTS, 2, 256])
        GE_HI = at("GE_HI", 170, [P, 2, 2, SLOTS], F32R)
        GE_LO = at("GE_LO", 171.5, [P, 2, 2, SLOTS], F32R)
        YTOK = at("YTOK", 173, [SLOTS, D])
        ONEHOT = at("ONEHOT", 177, [P, 2, SLOTS])
        WEIGHTED = at("WEIGHTED", 178, [P, 2, SLOTS])
        SCATTER = at("SCATTER", 179, [SLOTS, S])
        R1 = at("R1", 148, [P, 2, 8])
        CMP = at("CMP", 148.25, [P, 2, 8, 8])
        CMP2 = at("CMP2", 149, [P, 2, 8, 8])
        RANK, SEL, EX, W, POS, POS1, NSEL = (at(n, 149.5 + i / 8, [P, 2, 8]) for i, n in enumerate(
            ("RANK", "SEL", "EX", "W", "POS", "POS1", "NSEL")))
        RM, RSUM, RINV = (at(n, 150.5 + i / 8, [P, 2]) for i, n in enumerate(("RM", "RSUM", "RINV")))
        COUNT = at("COUNT", 151, [P, 8], I32)
        COUNTF = at("COUNTF", 151.125, [P, 8])
        MAXF = at("MAXF", 151.25, [P, 1])
        MAXI = at("MAXI", 151.375, [P, 1], I32)
        OUT = at("OUT", 132, [P, DC, S])

        def const(name, p0=0, p1=P):
            lo, hi = CONST_COLS[name]
            return CONST[p0:p1, lo:hi]

        def vec(name):
            lo, hi = VEC_COLS[name]
            return VEC[:, lo:hi]

        ident, ones, eps = const("ident"), const("ones"), const("eps")
        MOD = [small["mod0"], small["mod1"]]

        def mod_vec(layer, part, chunk, stream):
            col = (part * DC + chunk) * 2 + (1 - stream)
            return MOD[layer][:, col:col + 1]

        bank = [psum(f"bank{i}", [P, 512]) for i in range(BANKS)]
        turned = [psum(f"turned{i}", [P, 512]) for i in range(2)]
        pv_bank = psum("pv_bank", [P, 512])

        consts_in, vecs_in, x_in, pool_in = sem("consts_in"), sem("vecs_in"), sem("x_in"), sem("pool_in")
        slab_in = [sem(f"slab_in{i}") for i in range(RING)]
        hi_ready, lo_ready = sem("hi_ready"), sem("lo_ready")
        h_hi_ready, h_lo_ready = ({k: sem(f"{n}{k[1]}") for k in ((0, 1), (0, 2))}
                                  for n in ("h_hi_ready", "h_lo_ready"))
        hid_hi_ready, hid_lo_ready = sem("hid_hi_ready"), sem("hid_lo_ready")
        full = [sem(f"full{i}") for i in range(BANKS)]
        free = [sem(f"free{i}") for i in range(BANKS)]
        cond_ready, cond_zeroed = sem("cond_ready"), sem("cond_zeroed")
        dve_seq = sem("dve_seq")
        L = range(DEPTH)
        norms = [(0, 1), (0, 2), (1, 1), (1, 2), "final"]
        sq_ready = {k: sem(f"sq_ready{i}") for i, k in enumerate(norms)}
        sq_used = {k: sem(f"sq_used{i}") for i, k in enumerate(norms)}
        final_rms = sem("final_rms")
        rrms_ready = {k: sem(f"rrms_ready{i}") for i, k in enumerate(norms)}
        tmp_ready = {k: sem(f"tmp_ready{i}") for i, k in enumerate(norms)}
        h_ready = {k: sem(f"h_ready{i}") for i, k in enumerate(norms)}
        scale_ready = sem("scale_ready")
        qk_sq = [sem(f"qk_sq{l}") for l in L]
        qk_sq_used = [sem(f"qk_sq_used{l}") for l in L]
        qk_rrms = [sem(f"qk_rrms{l}") for l in L]
        qk_ready = [sem(f"qk_ready{l}") for l in L]
        bias_in, bias_ready = [sem(f"bias_in{l}") for l in L], [sem(f"bias_ready{l}") for l in L]
        pw_in = [sem(f"pw_in{l}") for l in L]
        nm_ready = [sem(f"nm_ready{l}") for l in L]
        p_ready = [sem(f"p_ready{l}") for l in L]
        turned_full = [sem(f"turned_full{l}") for l in L]
        turned_out_act = [sem(f"turned_out_act{l}") for l in L]
        turned_out_dve = [sem(f"turned_out_dve{l}") for l in L]
        pv_full = [sem(f"pv_full{l}") for l in L]
        y_ready = [sem(f"y_ready{l}") for l in L]
        routed = sem("routed")
        ex_ready = sem("ex_ready")
        sel_ready, counts_ready = sem("sel_ready"), sem("counts_ready")
        moe_in = [sem(f"moe_in{i}") for i in range(MOE_RING)]
        onehot_ready, gathered, he_ready = sem("onehot_ready"), sem("gathered"), sem("he_ready")
        weights_turned, scatter_ready = sem("weights_turned"), sem("scatter_ready")
        moe_hi_ready, moe_lo_dve, moe_lo_pool = sem("moe_hi_ready"), sem("moe_lo_dve"), sem("moe_lo_pool")
        slab_used = sem("slab_used")
        se_ready, gt_ready, ge_turned = sem("se_ready"), sem("gt_ready"), sem("ge_turned")
        ge_hi_ready, ge_lo_ready, he_lo_ready = sem("ge_hi_ready"), sem("ge_lo_ready"), sem("he_lo_ready")
        ytok_dve, ytok_act = sem("ytok_dve"), sem("ytok_act")
        scattered, x_added = sem("scattered"), sem("x_added")
        step_over = sem("step_over")
        out_ready, out_done = sem("out_ready"), sem("out_done")

        def acc(key):
            return bank[FILLS[key] % BANKS]

        def wait_full(eng, key):
            n = FILLS[key]
            eng.wait_ge(full[n % BANKS], n // BANKS + 1)

        def wait_taken(eng, key):
            n = FILLS[key]
            eng.wait_ge(free[n % BANKS], n // BANKS + 1)

        def freed(key):
            return free[FILLS[key] % BANKS]

        def slab_size(key):
            return PART_CHUNKS[key[1]] * 256 if key[0] == "w2" else SLAB

        def x_range(layer):
            return (0, T) if layer == 0 else (S, T)

        def streams_of(layer):
            return (CTX, LAT) if layer == 0 else (LAT,)

        def lat_col(layer):
            return S if layer == 0 else 0

        def wait_expert_slab(eng, k, i):
            eng.wait_ge(moe_in[k % MOE_RING], i * (16 * ROUNDS) + 16 * (k // MOE_RING + 1))

        def wait_slab_used(eng, k, i):
            eng.wait_ge(slab_used, i * N_EXPERT_SLABS + k + 1)

        def moe_low_part(eng, engine, k, i, blocks, done):
            eng.wait_ge(moe_hi_ready, i * N_EXPERT_SLABS + k + 1)
            wait_expert_slab(eng, k, i)
            n = k % MOE_SPLIT
            engine.tensor_tensor(moe_lo[n][:, blocks, :], moe_slab[k % MOE_RING][:, blocks, :],
                                 moe_hi[n][:, blocks, :].bitcast(F32), ALU.subtract).then_inc(done, 1)

        up = [bank[0], bank[1]]
        down = [bank[2], bank[3]]
        gath = [bank[4], turned[0]]
        ge_bank = turned[1]
        wt_bank = pv_bank

        def overflow_steps(eng, body, skip):
            eng.wait_ge(x_added, N_EXPERTS * 4)
            eng.wait_ge(counts_ready, 2)
            most = eng.value_load(MAXI[0:1, 0:1], min_val=0, max_val=S)
            with eng.If(most > SLOTS):
                with eng.Fori(0, N_EXPERTS) as e:
                    count = eng.value_load(COUNT[0:1, bass.ds(e, 1)], min_val=0, max_val=S)
                    for again in range(1, PASSES):
                        i = e * (PASSES - 1) + (N_EXPERTS + again - 1)
                        with eng.If(count > SLOTS * again):
                            body(e, i, again)
                            eng.wait_ge(x_added, i * 4 + 4)
                            eng.sem_inc(step_over, 1)
                        with eng.Else():
                            skip()

        block = ctx.enter_context(nc.Block())

        @block.sync
        def _(sp):
            def slab_source(key):
                kind = key[0]
                if kind == "mod":
                    return a["w_mod"][key[1]]
                if kind == "in":
                    return a["w_in"][key[1] * 19 + key[2]]
                if kind == "proj":
                    return a["w_proj"][key[1] * 4 + key[2]]
                if kind == "out":
                    return a["w_out"][key[1] * 4 + key[2]]
                _, part, i = key
                if kind in ("w1", "w3"):
                    return a["ffn_" + kind][sum(PART_CHUNKS[:part]) // 2 + i]
                return a[f"ffn_w2_{part}"][i]

            def load_slab(n, key):
                if n >= RING:
                    before = order[n - RING]
                    if is_split(before):
                        sp.wait_ge(lo_ready, SPLITS[before] + 1)
                    else:
                        wait_full(sp, last_fill(before))
                dst = ring[n % RING].rearrange("p k n -> p (k n)")[:, 0:slab_size(key)]
                sp.dma_start(dst, slab_source(key)).then_inc(slab_in[n % RING], 16)

            order = list(SLABS)
            sp.dma_start(VEC[:], a["vecs"]).then_inc(vecs_in, 16)
            for n in range(2):
                load_slab(n, order[n])
            sp.dma_start(XT[:].rearrange("p k n -> p (k n)"), a["xt"]).then_inc(x_in, 16)
            sp.dma_start(CONST[:], a["consts"]).then_inc(consts_in, 16)
            for n in range(2, len(order)):
                load_slab(n, order[n])

            def expert_load(k, e):
                kind, g = EXPERT_SLABS[k][:2]
                if kind == "up":
                    src, row, n = a["moe_up"], g * 2 * P + EXPERT_SLABS[k][2] * P, GROUPS * 2 * P
                else:
                    src, row, n = a["moe_w2"], g * P, GROUPS * P
                sp.dma_start(moe_slab[k % MOE_RING][:].rearrange("p k n -> p (k n)"),
                             src[bass.ds(e * n + row, P), :]).then_inc(moe_in[k % MOE_RING], 16)

            def expert_head(e):
                for k in range(MOE_RING):
                    expert_load(k, e)

            def wait_split(k, i):
                sp.wait_ge(moe_lo_dve, i * N_EXPERT_SLABS + k + 1)
                sp.wait_ge(moe_lo_pool, i * N_EXPERT_SLABS + k + 1)

            def expert_rest(e, i):
                for k in range(MOE_RING, N_EXPERT_SLABS):
                    wait_split(k - MOE_RING, i)
                    expert_load(k, e)

            wait_full(sp, ("out", 1, 3, 1))
            expert_head(0)
            with sp.Fori(0, N_EXPERTS - 1) as e:
                expert_rest(e, e)
                for k in range(MOE_RING):
                    wait_split(N_EXPERT_SLABS - MOE_RING + k, e)
                    expert_load(k, e + 1)
            expert_rest(N_EXPERTS - 1, N_EXPERTS - 1)

            def overflow(e, i, again):
                expert_head(e)
                expert_rest(e, i)

            overflow_steps(sp, overflow, lambda: [sp.sem_inc(s, 16 * ROUNDS) for s in moe_in])
            sp.wait_ge(out_ready, DC)
            sp.dma_start(a["out"], OUT[:].rearrange("p k n -> p (k n)")).then_inc(out_done, 16)
            sp.wait_ge(out_done, 16)

        @block.gpsimd
        def _(pool):
            pool.dma_start(POOL[:].rearrange("p a g n -> p (a g n)"), a["pool_mat"]).then_inc(pool_in, 16)
            lo_of = iter(SPLITS)

            def low_part():
                key = next(lo_of)
                n = SPLITS[key]
                size = slab_size(key)
                pool.wait_ge(hi_ready, n + 1)
                pool.wait_ge(slab_in[SLABS[key] % RING], 16 * (SLABS[key] // RING + 1))
                raw, hi, lo = (t[:].rearrange("p k n -> p (k n)")[:, 0:size]
                               for t in (ring[SLABS[key] % RING], w_hi[n % 2], w_lo[n % 2]))
                nc.gpsimd.tensor_tensor(lo, raw, hi.bitcast(F32), ALU.subtract).then_inc(lo_ready, 1)

            def h_low_parts(key):
                for c in range(DC):
                    pool.wait_ge(h_hi_ready[key], c + 1)
                    nc.gpsimd.tensor_tensor(H_LO[:, c, :], H_NEW[:, c % 4, :], H_HI[:, c, :].bitcast(F32),
                                            ALU.subtract).then_inc(h_lo_ready[key], 1)

            def small_loads(layer):
                pool.dma_start(PW[:].rearrange("p a n -> p (a n)"), a["pool_w"][layer]).then_inc(pw_in[layer], 16)
                pool.dma_start(BIAS[:].rearrange("p a h n -> p (a h n)"), a["rel_bias"][layer])\
                    .then_inc(bias_in[layer], 16)

            small_loads(0)
            for _ in range(2):
                low_part()
            h_low_parts((0, 1))
            for _ in range(2, W_IN_GATE + 2):
                low_part()
            pool.wait_ge(bias_ready[0], 2)
            pool.wait_ge(nm_ready[0], len(attention_units(0)))
            wait_full(pool, ("poolw", 0, 1))
            small_loads(1)
            for _ in range(W_IN_GATE + 2, W_IN_GATE + 12):
                low_part()
            for _ in range(2):
                low_part()
            h_low_parts((0, 2))
            q = 0
            for part, n in enumerate(PART_CHUNKS):
                for s in range(n // 2):
                    low_part()
                    for m in range(2):
                        pool.wait_ge(hid_hi_ready, q + 1)
                        nc.gpsimd.tensor_tensor(HID_LO[:, 2 * s + m, :], HID[:, q % 4, :],
                                                HID_HI[:, 2 * s + m, :].bitcast(F32), ALU.subtract)\
                            .then_inc(hid_lo_ready, 1)
                        q += 1
                    low_part()
                for j in range(4 if part < len(PART_CHUNKS) - 1 else 2):
                    low_part()
            assert next(lo_of, None) is None

            def expert(e, i, again=0):
                for k in range(N_EXPERT_SLABS):
                    moe_low_part(pool, nc.gpsimd, k, i, slice(LO_DVE, 4), moe_lo_pool)

            with pool.Fori(0, N_EXPERTS) as e:
                expert(e, e)
            overflow_steps(pool, expert, lambda: pool.sem_inc(moe_lo_pool, N_EXPERT_SLABS))

        @block.tensor
        def _(pe):
            def fill(key):
                n = FILLS[key]
                if n >= BANKS:
                    pe.wait_ge(free[n % BANKS], n // BANKS)
                return bank[n % BANKS]

            def filled(ins, key):
                ins.then_inc(full[FILLS[key] % BANKS], 1)

            def slab(key):
                if is_split(key):
                    n = SPLITS[key]
                    pe.wait_ge(lo_ready, n + 1)
                    return w_hi[n % 2], w_lo[n % 2]
                n = SLABS[key]
                pe.wait_ge(slab_in[n % RING], 16 * (n // RING + 1))
                return (ring[n % RING],)

            mm = nc.tensor.matmul

            def piece(parts, *at):
                return [t[at] for t in parts]

            def products(out, lhs, rhs, start, stop):
                if len(lhs) == 1:
                    return mm(out, lhs[0], rhs[0], start=start, stop=stop)
                mm(out, lhs[0], rhs[0], start=start, stop=False)
                mm(out, lhs[0], rhs[1], start=False, stop=False)
                return mm(out, lhs[1], rhs[0], start=False, stop=stop)

            def h_of(layer):
                return (H_HI, H_LO) if layer == 0 else (H,)

            def split_chain(out, pairs):
                last = len(pairs) - 1
                for k, (lhs, rhs) in enumerate(pairs):
                    ins = products(out, lhs, rhs, k == 0, k == last)
                return ins

            def chain(out, pairs):
                last = len(pairs) - 1
                for k, (lhs, rhs) in enumerate(pairs):
                    ins = mm(out, lhs, rhs, start=k == 0, stop=k == last)
                return ins

            def mod(n):
                (w,), out, q = slab(("mod", n)), fill(("mod", n)), n % 4
                filled(chain(out[32 * q:32 * q + 32, 0:256],
                             [(small["cond"][:, 32 * k:32 * k + 32], w[:, k, :]) for k in range(DC)]), ("mod", n))
                if q == 3:
                    key = ("turned_mod", n // 4)
                    out = fill(key)
                    for back in range(4):
                        wait_taken(pe, ("mod", n - back))
                    for m in range(2):
                        ins = nc.tensor.transpose(out[:, P * m:P * m + P], small["modrow"][:, P * m:P * m + P], ident)
                    filled(ins, key)

            def norm(key, lo, hi):
                tiles = (hi - lo) // P
                out = fill(("stat", key))
                for c in range(DC):
                    pe.wait_ge(sq_ready[key], c + 1)
                    for t in range(tiles):
                        ins = mm(out[:, t:t + 1], SQ[:, c % 2, P * t:P * t + P], ones[:, 0:1],
                                 start=c == 0 and t == 0, stop=c == DC - 1, skip_group_check=True)
                    if c < DC - 1:
                        ins.then_inc(sq_used[key], 1)
                filled(ins, ("stat", key))
                out = fill(("bcast", key))
                pe.wait_ge(rrms_ready[key], 1)
                for t in range(tiles):
                    ins = mm(out[:, P * t:P * t + P], small["rrms"][:, t:t + 1].to_broadcast([P, P]), ident,
                             start=True, stop=True)
                filled(ins, ("bcast", key))

            def in_proj(layer):
                lo, hi = x_range(layer)
                first = [True]
                ALL = slice(None)
                h = h_of(layer)

                def h_chunk(k):
                    if first[0]:
                        if layer == 0:
                            pe.wait_ge(h_lo_ready[0, 1], k + 1)
                        else:
                            pe.wait_ge(h_ready[1, 1], 2 * (k + 1))
                        if k == DC - 1:
                            first[0] = False

                def by_feature(name, w, m, c0, c1):
                    out = fill(("in", layer, name))
                    for k in range(DC):
                        h_chunk(k)
                        ins = products(out[:, 0:c1 - c0], piece(w, ALL, k, slice(P * m, P * m + P)),
                                       piece(h, ALL, k, slice(c0, c1)), k == 0, k == DC - 1)
                    filled(ins, ("in", layer, name))

                def by_token(name, w, tiles, c0, c1):
                    out = fill(("in", layer, name))
                    for n, t in enumerate(tiles):
                        ins = split_chain(out[:, n * (c1 - c0):(n + 1) * (c1 - c0)],
                                          [(piece(h, ALL, k, slice(P * t, P * t + P)),
                                            piece(w, ALL, k, slice(c0, c1))) for k in range(DC)])
                    filled(ins, ("in", layer, name))

                for s in range(2):
                    w = slab(("in", layer, s))
                    for m in range(2):
                        by_feature(("q", 2 * s + m), w, m, lo, hi)
                w = slab(("in", layer, W_IN_KV))
                by_feature(("k", 0), w, 0, 0, T)
                if layer == 0:
                    for m in range(2):
                        by_token(("av", m), w, (2 * m, 2 * m + 1), 0, 256)
                else:
                    by_token(("av", 0), w, range(4), P, 2 * P)
                w = slab(("in", layer, W_IN_BQ))
                for m in range(2):
                    by_feature(("bq", m), w, m, lo, hi)
                w = slab(("in", layer, W_IN_BK))
                for m in range(2):
                    by_feature(("bk", m), w, m, 0, T)
                w = slab(("in", layer, W_IN_BV))
                for m in range(2):
                    by_token(("bv", m), w, (2 * m, 2 * m + 1), 0, 256)
                w = slab(("in", layer, W_IN_U))
                for m in (range(2) if layer == 0 else (1,)):
                    by_token(("u", m), w, (2 * m, 2 * m + 1), 0, 256)

            def qk_norm(layer):
                tq = 4 if layer == 0 else 2
                out = fill(("qkstat", layer))
                for j in range(5):
                    pe.wait_ge(qk_sq[layer], j + 1)
                    for t in range(tq if j < 4 else 4):
                        col = 2 * (j * tq + t)
                        ins = mm(out[:, col:col + 2], SQ[:, j % 2, P * t:P * t + P], const("blk2"),
                                 start=True, stop=True)
                    if j < 4:
                        ins.then_inc(qk_sq_used[layer], 1)
                filled(ins, ("qkstat", layer))
                for j in range(5):
                    out = fill(("qkb", layer, j))
                    if j == 0:
                        pe.wait_ge(qk_rrms[layer], 1)
                    for t in range(tq if j < 4 else 4):
                        col = 2 * (j * tq + t)
                        for g in range(2):
                            ins = mm(out[HD * g:HD * g + HD, P * t:P * t + P],
                                     small["qkr"][:, col + g:col + g + 1].to_broadcast([P, HD]), ident,
                                     start=True, stop=True)
                    filled(ins, ("qkb", layer, j))
                for j in range(5):
                    out = fill(("rope", layer, j))
                    wait_taken(pe, ("qkb", layer, j))
                    c = lat_col(layer) if j < 4 else S
                    ins = mm(out[:, 0:S], const("perm"), QK[:, j, c:c + S], start=True, stop=True)
                    filled(ins, ("rope", layer, j))

            def place(branch, h):
                if branch == "A":
                    g = h // 4
                    return QK[:, h % 4], HD * g, QK[:, 4], HD * g, h % 4
                return BQ[:, h // 2], HD * (h % 2), BK[:, h // 2], P + HD * h, 4 + h // 2

            def attention(layer):
                units = attention_units(layer)
                c_lat = lat_col(layer)

                def scores(u):
                    branch, h, stream = units[u]
                    q, p0, k, _, _ = place(branch, h)
                    col = c_lat if stream == LAT else 0
                    if u == 0:
                        pe.wait_ge(qk_ready[layer], 5)
                    if branch == "B" and h == 0:
                        for name in ("bq", "bk"):
                            for m in range(2):
                                wait_taken(pe, ("in", layer, (name, m)))
                    for t in range(2):
                        lhs = q[p0:p0 + HD, col + P * t:col + P * t + P]
                        if stream == LAT:
                            out = fill(("score", layer, u, t))
                            filled(mm(out[:], lhs, k[p0:p0 + HD, :], start=True, stop=True), ("score", layer, u, t))
                        else:
                            if t == 0:
                                out = fill(("score", layer, u, 0))
                            ins = mm(out[:, S * t:S * t + S], lhs, k[p0:p0 + HD, 0:S], start=True, stop=True)
                    if stream == CTX:
                        filled(ins, ("score", layer, u, 0))

                def turn(u):
                    stream = units[u][2]
                    pe.wait_ge(p_ready[layer], u + 1)
                    if u:
                        pe.wait_ge(turned_out_act[layer], u)
                        pe.wait_ge(turned_out_dve[layer], u)
                    tiles = 4 if stream == LAT else 2
                    for t in range(tiles):
                        b, n = divmod(t, tiles // 2)
                        for qt in range(2):
                            ins = nc.tensor.transpose(turned[b][:, S * n + P * qt:S * n + P * qt + P],
                                                      PR[:, u % 2, qt, P * t:P * t + P], ident)
                    ins.then_inc(turned_full[layer], 1)

                def values(u):
                    branch, h, stream = units[u]
                    _, p0, _, vcol, _ = place(branch, h)
                    pe.wait_ge(turned_out_act[layer], u + 1)
                    pe.wait_ge(turned_out_dve[layer], u + 1)
                    if u == 0:
                        for name in (("av", 0), ("av", 1 - layer), ("bv", 0), ("bv", 1)):
                            wait_taken(pe, ("in", layer, name))
                    else:
                        pe.wait_ge(y_ready[layer], u)
                    tiles = 4 if stream == LAT else 2
                    ins = chain(pv_bank[p0:p0 + HD, 0:S],
                                [(V[:, t, vcol:vcol + HD], PT[:, u % 2, t, :]) for t in range(tiles)])
                    ins.then_inc(pv_full[layer], 1)

                scores(0)
                scores(1)
                for u in range(len(units)):
                    if u + 2 < len(units):
                        scores(u + 2)
                    if u:
                        values(u - 1)
                    turn(u)
                    if layer == 0:
                        mod(MOD_IN_ATTENTION[u])
                values(len(units) - 1)

            def pooling(layer):
                if layer == 0:
                    pe.wait_ge(pool_in, 16)
                for m in (range(2) if layer == 0 else (1,)):
                    wait_taken(pe, ("in", layer, ("u", m)))
                for p in range(2):
                    out = fill(("pool", layer, p))
                    for n, stream in enumerate(streams_of(layer)):
                        for gg in range(2):
                            g = 2 * p + gg
                            ins = chain(out[HD * gg:HD * gg + HD, S * n:S * n + S],
                                        [(U[:, 2 * stream + t, HD * g:HD * g + HD], POOL[:, t, g, :])
                                         for t in range(2)])
                    filled(ins, ("pool", layer, p))
                nq = S * len(streams_of(layer))
                pe.wait_ge(pw_in[layer], 16)
                for p in range(2):
                    out = fill(("poolw", layer, p))
                    wait_taken(pe, ("pool", layer, p))
                    filled(mm(out[:, 0:nq], PW[:, p, :], DT[:, p, 0:nq], start=True, stop=True), ("poolw", layer, p))

            BRANCH_CHUNKS = (range(0, 4), range(4, 6), range(6, 8))

            def merge(layer):
                lo, hi = x_range(layer)
                nq = hi - lo
                for j in range(4):
                    for b in range(3):
                        w = slab(("in", layer, W_IN_GATE + 4 * b + j))
                        for m in range(2):
                            key = ("gate", layer, j, b, m)
                            out = fill(key)
                            filled(split_chain(out[:, 0:nq], [
                                ([t[:, k, P * m:P * m + P] for t in w], [t[:, k, lo:hi] for t in h_of(layer)])
                                for k in range(DC)]), key)
                    (w,) = slab(("proj", layer, j))
                    if j == 0:
                        pe.wait_ge(y_ready[layer], len(attention_units(layer)))
                        for p in range(2):
                            wait_taken(pe, ("poolw", layer, p))
                    for b in range(3):
                        for m in range(2):
                            key = ("proj", layer, j, b, m)
                            out = fill(key)
                            filled(chain(out[:, 0:nq], [(w[:, k, P * m:P * m + P], Y[:, k, 0:nq])
                                                        for k in BRANCH_CHUNKS[b]]), key)

            def out_proj(layer):
                nq = S * len(streams_of(layer))
                wait_taken(pe, ("proj", layer, 3, 2, 1))
                for j in range(4):
                    (w,) = slab(("out", layer, j))
                    for m in range(2):
                        key = ("out", layer, j, m)
                        out = fill(key)
                        filled(chain(out[:, 0:nq], [(w[:, k, P * m:P * m + P], M[:, k, 0:nq])
                                                    for k in range(DC)]), key)

            def feed_forward():
                later = list(MOD_IN_FFN)
                done = 0
                for part, n in enumerate(PART_CHUNKS):
                    for s in range(n // 2):
                        for name in ("w1", "w3"):
                            w = slab((name, part, s))
                            for m in range(2):
                                key = (name, part, s, m)
                                out = fill(key)
                                for k in range(DC):
                                    if part == 0 and s == 0 and name == "w1" and m == 0:
                                        pe.wait_ge(h_lo_ready[0, 2], k + 1)
                                    ins = products(out[:], [t[:, k, P * m:P * m + P] for t in w],
                                                   [t[:, k, :] for t in (H_HI, H_LO)], k == 0, k == DC - 1)
                                filled(ins, key)
                        if later:
                            mod(later.pop(0))
                    done += n
                    pe.wait_ge(hid_lo_ready, done)
                    for j in range(4):
                        w = [t[:].rearrange("p k n -> p (k n)")[:, 0:n * 256].rearrange("p (k n) -> p k n", k=n)
                             for t in slab(("w2", part, j))]
                        for m in range(2):
                            key = ("down", part, j, m)
                            out = fill(key)
                            filled(split_chain(out[:], [
                                ([t[:, k, P * m:P * m + P] for t in w], [t[:, k, :] for t in (HID_HI, HID_LO)])
                                for k in range(n)]), key)
                        if later:
                            mod(later.pop(0))

            def route():
                out = fill(("logit",))
                for t in range(2):
                    for k in range(DC):
                        if t == 0:
                            pe.wait_ge(h_ready[1, 2], k + 1)
                        lo = VEC_COLS["rw"][0] + N_EXPERTS * k
                        ins = mm(out[:, 8 * t:8 * t + 8], H[:, k, S + P * t:S + P * t + P],
                                 VEC[:, lo:lo + N_EXPERTS], start=k == 0, stop=k == DC - 1)
                filled(ins, ("logit",))
                for i in range(4):
                    out = fill(("turn", i))
                    t, half = divmod(i, 2)
                    for c in range(4):
                        ins = nc.tensor.transpose(out[:, P * c:P * c + P],
                                                  H[:, 4 * half + c, S + P * t:S + P * t + P], ident)
                    filled(ins, ("turn", i))
                out = fill(("prefix",))
                pe.wait_ge(sel_ready, 1)
                mm(out[:, 0:8], const("before"), SEL[:, 0, :], start=True, stop=True)
                mm(out[:, 8:16], ones, SEL[:, 0, :], start=True, stop=False)
                mm(out[:, 8:16], const("before"), SEL[:, 1, :], start=False, stop=True)
                mm(out[:, 16:24], ones, SEL[:, 0, :], start=True, stop=False)
                filled(mm(out[:, 16:24], ones, SEL[:, 1, :], start=False, stop=True), ("prefix",))

            def expert(e, i, again=0):
                pe.wait_ge(onehot_ready, i + 1)
                for b in range(2):
                    for c in range(4):
                        for t in range(2):
                            ins = mm(gath[b][:, SLOTS * c:SLOTS * c + SLOTS],
                                     HTOK[:, t, P * (4 * b + c):P * (4 * b + c) + P], ONEHOT[:, t, :],
                                     start=t == 0, stop=t == 1)
                    ins.then_inc(gathered, 1)
                for t in range(2):
                    ins = nc.tensor.transpose(wt_bank[0:SLOTS, P * t:P * t + P], WEIGHTED[:, t, :], ident)
                ins.then_inc(weights_turned, 1)

                def parts(key):
                    k = EXPERT_AT[key]
                    pe.wait_ge(moe_lo_dve, i * N_EXPERT_SLABS + k + 1)
                    pe.wait_ge(moe_lo_pool, i * N_EXPERT_SLABS + k + 1)
                    return moe_hi[k % MOE_SPLIT], moe_lo[k % MOE_SPLIT]

                def up_half(g, half):
                    w = parts(("up", g, half))
                    for kk in range(4):
                        k = 4 * half + kk
                        if g == 0:
                            pe.wait_ge(he_lo_ready, 2 * i + half + 1)
                        ins = products(up[g % 2][0:SLOTS, :], (HE_HI[:, k, :], HE_LO[:, k, :]),
                                       [t[:, kk, :] for t in w], k == 0, k == DC - 1)
                    ins.then_inc(slab_used, 1)

                def turn_hidden(g):
                    pe.wait_ge(gt_ready, i * GROUPS + g + 1)
                    for m in range(2):
                        ins = nc.tensor.transpose(ge_bank[:, SLOTS * m:SLOTS * m + SLOTS],
                                                  GT[:, g % 2, P * m:P * m + P], ident[0:SLOTS, 0:SLOTS])
                    ins.then_inc(ge_turned, 1)

                def down_group(g):
                    w = parts(("down", g))
                    pe.wait_ge(ge_lo_ready, i * GROUPS + g + 1)
                    for k in range(2):
                        for n in range(2):
                            ins = products(down[n][0:SLOTS, :], (GE_HI[:, g % 2, k, :], GE_LO[:, g % 2, k, :]),
                                           [t[:, 2 * k + n, :] for t in w],
                                           g == 0 and k == 0, g == GROUPS - 1 and k == 1)
                    ins.then_inc(slab_used, 1)

                for g in range(GROUPS):
                    up_half(g, 0)
                    if g:
                        turn_hidden(g - 1)
                    up_half(g, 1)
                    if g:
                        down_group(g - 1)
                turn_hidden(GROUPS - 1)
                down_group(GROUPS - 1)
                pe.wait_ge(scatter_ready, i + 1)
                for n in range(4):
                    if n == 0:
                        pe.wait_ge(ytok_dve, i + 1)
                    if n == 2:
                        pe.wait_ge(ytok_act, i + 1)
                    if n >= 2:
                        pe.wait_ge(x_added, i * 4 + n - 1)
                    for c in range(2):
                        col = P * (2 * n + c)
                        ins = mm(gath[n % 2][:, S * c:S * c + S], YTOK[:, col:col + P], SCATTER[:],
                                 start=True, stop=True)
                    ins.then_inc(scattered, 1)
                pe.wait_ge(x_added, i * 4 + 4)

            pe.wait_ge(cond_ready, 1)
            pe.wait_ge(consts_in, 16)
            for n in MOD_AT_START:
                mod(n)
            for layer in L:
                norm((layer, 1), 0, T)
                in_proj(layer)
                qk_norm(layer)
                attention(layer)
                pooling(layer)
                merge(layer)
                out_proj(layer)
                if layer == 0:
                    norm((0, 2), 0, T)
                    feed_forward()
                else:
                    norm((1, 2), S, T)
            route()
            for i in range(4):
                wait_taken(pe, ("turn", i))
            pe.wait_ge(counts_ready, 2)
            with pe.Fori(0, N_EXPERTS) as e:
                expert(e, e)

            def skip():
                for s, n in ((gathered, 2), (weights_turned, 1), (slab_used, N_EXPERT_SLABS), (ge_turned, GROUPS),
                             (scattered, 4)):
                    pe.sem_inc(s, n)

            overflow_steps(pe, expert, skip)
            out = up[0]
            for c in range(DC):
                pe.wait_ge(sq_ready["final"], c + 1)
                for t in range(2):
                    ins = mm(out[:, t:t + 1], SQ[:, c % 2, P * t:P * t + P], ones[:, 0:1],
                             start=c == 0 and t == 0, stop=c == DC - 1, skip_group_check=True)
                ins.then_inc(sq_used["final"], 1)
            out = up[1]
            pe.wait_ge(rrms_ready["final"], 1)
            for t in range(2):
                ins = mm(out[:, P * t:P * t + P], small["rrms"][:, t:t + 1].to_broadcast([P, P]), ident,
                         start=True, stop=True)
            ins.then_inc(tmp_ready["final"], 1)

        @block.scalar
        def _(act):
            af = nc.scalar.activation

            hi_of = iter(SPLITS)

            def high_part():
                key = next(hi_of)
                n = SPLITS[key]
                act.wait_ge(slab_in[SLABS[key] % RING], 16 * (SLABS[key] // RING + 1))
                if n >= 2:
                    wait_full(act, last_fill(list(SPLITS)[n - 2]))
                raw, hi = (t[:].rearrange("p k n -> p (k n)")[:, 0:slab_size(key)]
                           for t in (ring[SLABS[key] % RING], w_hi[n % 2]))
                af(hi, raw, ACT.Copy).then_inc(hi_ready, 1)

            def squares(key, lo, hi, src_ready):
                src_ready()
                for c in range(DC):
                    if key == (0, 1) and c == 2:
                        for _ in range(2):
                            high_part()
                    if c >= 2:
                        act.wait_ge(sq_used[key], c - 1)
                    af(SQ[:, c % 2, 0:hi - lo], XT[:, c, lo:hi], ACT.Square).then_inc(sq_ready[key], 1)

            def norm(key, lo, hi, src_ready):
                layer, w = key
                squares(key, lo, hi, src_ready)
                wait_full(act, ("stat", key))
                tiles = (hi - lo) // P
                af(small["rms"][:, 0:tiles], acc(("stat", key))[:, 0:tiles], ACT.Sqrt, scale=1.0 / D, bias=eps)\
                    .then_inc(freed(("stat", key)), 1)
                part = 0 if w == 1 else 3
                scale = small["scale1" if w == 1 else "scale2"]
                if w == 1:
                    act.wait_ge(scale_ready, 2 * layer + 1)
                else:
                    act.wait_ge(scale_ready, 2 * layer + 2)
                def h_rounded(c):
                    act.wait_ge(h_ready[key], 2 * (c + 1))
                    af(H_HI[:, c, :], H_NEW[:, c % 4, :], ACT.Copy).then_inc(h_hi_ready[key], 1)

                for c in range(DC):
                    act.wait_ge(tmp_ready[key], c + 1)
                    if layer == 0 and c >= 4:
                        act.wait_ge(h_lo_ready[key], c - 3)
                    dst = H_NEW[:, c % 4, :] if layer == 0 else H[:, c, :]
                    for n, stream in enumerate((CTX, LAT) if lo == 0 else (LAT,)):
                        col = 2 * c + (1 - stream)
                        af(dst[:, S * stream:S * stream + S], TMP[:, c % 2, S * n:S * n + S], ACT.Identity,
                           scale=scale[:, col:col + 1], bias=mod_vec(layer, part, c, stream))\
                            .then_inc(h_ready[key], 1)
                    if layer == 0 and c:
                        h_rounded(c - 1)
                if layer == 0:
                    h_rounded(DC - 1)

            def in_proj(layer):
                lo, hi = x_range(layer)
                nq = hi - lo
                if layer == 0:
                    for _ in range(3):
                        high_part()
                for m in range(2):
                    key = ("in", layer, ("bq", m))
                    wait_full(act, key)
                    af(BQ[:, m, 0:nq], acc(key)[:, 0:nq], ACT.Copy, scale=HD ** -0.5).then_inc(freed(key), 1)
                if layer == 0:
                    high_part()
                for m in range(2):
                    key = ("in", layer, ("bk", m))
                    wait_full(act, key)
                    af(BK[:, m, :], acc(key)[:], ACT.Copy).then_inc(freed(key), 1)
                if layer == 0:
                    high_part()
                for m in range(2):
                    key = ("in", layer, ("bv", m))
                    wait_full(act, key)
                    af(V[:, 2 * m:2 * m + 2, P:384], acc(key)[:].rearrange("p (t n) -> p t n", t=2), ACT.Copy)\
                        .then_inc(freed(key), 1)
                for m in (range(2) if layer == 0 else (1,)):
                    key = ("in", layer, ("u", m))
                    wait_full(act, key)
                    af(U[:, 2 * m:2 * m + 2, :], acc(key)[:].rearrange("p (t n) -> p t n", t=2), ACT.Copy)\
                        .then_inc(freed(key), 1)

            def qk_norm(layer):
                lo, hi = x_range(layer)
                tq = 4 if layer == 0 else 2
                for j in range(5):
                    wait_taken(act, ("in", layer, ("q", j) if j < 4 else ("k", 0)))
                    if j >= 2:
                        act.wait_ge(qk_sq_used[layer], j - 1)
                    n = hi - lo if j < 4 else T
                    af(SQ[:, j % 2, 0:n], QK[:, j, 0:n], ACT.Square).then_inc(qk_sq[layer], 1)
                wait_full(act, ("qkstat", layer))
                cols = 2 * (4 * tq + 4)
                af(small["qks"][:, 0:cols], acc(("qkstat", layer))[:, 0:cols], ACT.Sqrt, scale=1.0 / HD, bias=eps)\
                    .then_inc(freed(("qkstat", layer)), 1)

            def attention(layer):
                units = attention_units(layer)

                def exps(u):
                    stream = units[u][2]
                    act.wait_ge(nm_ready[layer], u + 1)
                    if u >= 2:
                        act.wait_ge(turned_full[layer], u - 1)
                    for t in range(2):
                        col = 2 * u + t
                        if stream == LAT:
                            key = ("score", layer, u, t)
                            src, n = acc(key)[:], T
                        else:
                            key = ("score", layer, u, 0)
                            src, n = acc(key)[:, S * t:S * t + S], S
                        ins = af(PR[:, u % 2, t, 0:n], src, ACT.Exp, bias=small["nm"][:, col:col + 1],
                                 accum_out=small["rs"][:, col:col + 1])
                        if stream == LAT or t == 1:
                            ins.then_inc(freed(key), 1)

                def turned_out(u):
                    stream = units[u][2]
                    act.wait_ge(turned_full[layer], u + 1)
                    if u >= 2:
                        act.wait_ge(pv_full[layer], u - 1)
                    n = 2 if stream == LAT else 1
                    af(PT[:, u % 2, 0:n, :], turned[0][:, 0:S * n].rearrange("p (t n) -> p t n", t=n), ACT.Copy)\
                        .then_inc(turned_out_act[layer], 1)

                def result(u):
                    branch, h, stream = units[u]
                    p0 = HD * (h // 4) if branch == "A" else HD * (h % 2)
                    chunk = h % 4 if branch == "A" else 4 + h // 2
                    col = lat_col(layer) if stream == LAT else 0
                    act.wait_ge(pv_full[layer], u + 1)
                    af(Y[p0:p0 + HD, chunk, col:col + S], pv_bank[p0:p0 + HD, 0:S], ACT.Copy)\
                        .then_inc(y_ready[layer], 1)

                exps(0)
                for u in range(len(units)):
                    if u + 1 < len(units):
                        exps(u + 1)
                    if u:
                        result(u - 1)
                    turned_out(u)
                if layer == 0:
                    for _ in range(2):
                        high_part()
                result(len(units) - 1)

            def pooling(layer):
                nq = S * len(streams_of(layer))
                for p in range(2):
                    key = ("pool", layer, p)
                    wait_full(act, key)
                    af(DT[:, p, 0:nq], acc(key)[:, 0:nq], ACT.Copy).then_inc(freed(key), 1)
                for p in range(2):
                    key = ("poolw", layer, p)
                    wait_full(act, key)
                    lo = VEC_COLS["pscale", layer][0] + p
                    af(Y[:, 6 + p, 0:nq], acc(key)[:, 0:nq], ACT.Copy, scale=VEC[:, lo:lo + 1])\
                        .then_inc(freed(key), 1)

            def merge(layer):
                nq = S * len(streams_of(layer))
                for j in range(4):
                    for b in range(3):
                        for m in range(2):
                            i = 2 * b + m
                            key = ("gate", layer, j, b, m)
                            wait_full(act, key)
                            if j:
                                wait_taken(act, ("proj", layer, j - 1, b, m))
                            af(GATE[:, i, 0:nq], acc(key)[:, 0:nq], ACT.Sigmoid).then_inc(freed(key), 1)
                        if layer == 0 and 3 * j + b < 10:
                            high_part()

            def feed_forward():
                before = None
                q = 0
                for part, n in enumerate(PART_CHUNKS):
                    for s in range(n // 2):
                        for m in range(2):
                            key = ("w1", part, s, m)
                            wait_full(act, key)
                            if before:
                                wait_taken(act, before + (m,))
                            af(SILU[:, m, :], acc(key)[:], ACT.Silu).then_inc(freed(key), 1)
                        before = ("w3", part, s)
                        high_part()
                        for m in range(2):
                            wait_taken(act, before + (m,))
                            af(HID_HI[:, 2 * s + m, :], HID[:, q % 4, :], ACT.Copy).then_inc(hid_hi_ready, 1)
                            q += 1
                        high_part()
                    for j in range(4 if part < len(PART_CHUNKS) - 1 else 2):
                        high_part()
                assert next(hi_of, None) is None

            def expert(e, i, again=0):
                def high(key):
                    k = EXPERT_AT[key]
                    wait_expert_slab(act, k, i)
                    if k >= MOE_SPLIT:
                        wait_slab_used(act, k - MOE_SPLIT, i)
                    af(moe_hi[k % MOE_SPLIT][:], moe_slab[k % MOE_RING][:], ACT.Copy).then_inc(moe_hi_ready, 1)

                def turned_hidden(g):
                    act.wait_ge(ge_turned, i * GROUPS + g + 1)
                    af(GE_HI[:, g % 2, :, :], ge_bank[:, 0:2 * SLOTS].rearrange("p (m n) -> p m n", m=2), ACT.Copy)\
                        .then_inc(ge_hi_ready, 1)

                act.wait_ge(onehot_ready, i + 1)
                high(("up", 0, 0))
                for b in range(2):
                    act.wait_ge(gathered, 2 * i + b + 1)
                    af(HE_HI[:, 4 * b:4 * b + 4, :],
                       gath[b][:, 0:4 * SLOTS].rearrange("p (c n) -> p c n", c=4), ACT.Copy).then_inc(he_ready, 1)
                high(("up", 0, 1))
                act.wait_ge(weights_turned, i + 1)
                af(SCATTER[:], wt_bank[0:SLOTS, 0:S], ACT.Copy).then_inc(scatter_ready, 1)
                for g in range(GROUPS):
                    if g:
                        if g >= 2:
                            high(("down", g - 1))
                        turned_hidden(g - 1)
                    if g + 1 < GROUPS:
                        high(("up", g + 1, 0))
                    wait_slab_used(act, EXPERT_AT["up", g, 1], i)
                    af(SE[:, g % 2, :], up[g % 2][0:SLOTS, 0:256], ACT.Silu).then_inc(se_ready, 1)
                    if g + 1 < GROUPS:
                        high(("up", g + 1, 1))
                    if g == 0:
                        high(("down", 0))
                high(("down", GROUPS - 1))
                turned_hidden(GROUPS - 1)
                wait_slab_used(act, N_EXPERT_SLABS - 1, i)
                af(YTOK[:, 512:1024], down[1][0:SLOTS, :], ACT.Copy).then_inc(ytok_act, 1)

            act.wait_ge(vecs_in, 16)
            act.wait_ge(cond_zeroed, 1)
            af(small["cond"][:].rearrange("p (k n) -> p k n", n=32)[:, :, 0:2],
               vec("cond").rearrange("p (k n) -> p k n", n=2), ACT.Silu).then_inc(cond_ready, 1)
            act.wait_ge(consts_in, 16)
            for layer in L:
                if layer == 0:
                    norm((0, 1), 0, T, lambda: act.wait_ge(x_in, 16))
                else:
                    norm((1, 1), 0, T, lambda: wait_taken(act, ("down", 2, 3, 1)))
                in_proj(layer)
                qk_norm(layer)
                attention(layer)
                pooling(layer)
                merge(layer)
                lo, hi = x_range(layer)
                if layer == 0:
                    for _ in range(2):
                        high_part()
                norm((layer, 2), lo, hi, lambda: wait_taken(act, ("out", layer, 3, 1)))
                if layer == 0:
                    feed_forward()
            act.wait_ge(routed, 1)
            af(EX[:], R1[:], ACT.Exp).then_inc(ex_ready, 1)
            with act.Fori(0, N_EXPERTS) as e:
                expert(e, e)

            def skip():
                for s, n in ((moe_hi_ready, N_EXPERT_SLABS), (he_ready, 2), (scatter_ready, 1), (se_ready, GROUPS),
                             (ge_hi_ready, GROUPS), (ytok_act, 1)):
                    act.sem_inc(s, n)

            overflow_steps(act, expert, skip)
            for c in range(DC):
                if c >= 2:
                    act.wait_ge(sq_used["final"], c - 1)
                af(SQ[:, c % 2, 0:S], XT[:, c, S:T], ACT.Square).then_inc(sq_ready["final"], 1)
            act.wait_ge(sq_used["final"], DC)
            af(small["rms"][:, 0:2], bank[0][:, 0:2], ACT.Sqrt, scale=1.0 / D, bias=eps)\
                .then_inc(final_rms, 1)

        @block.vector
        def _(dve):
            v = nc.vector
            seq = [0]

            def link(ins):
                seq[0] += 1
                ins.then_inc(dve_seq, 1)
                dve.wait_ge(dve_seq, seq[0])

            def mod(n):
                rows = slice(32 * (n % 4), 32 * (n % 4) + 32)
                wait_full(dve, ("mod", n))
                v.tensor_copy(small["modrow"][rows, :], acc(("mod", n))[rows, 0:256]).then_inc(freed(("mod", n)), 1)
                if n % 4 < 3:
                    return
                key = ("turned_mod", n // 4)
                wait_full(dve, key)
                layer, g = divmod(n // 4, 6)
                lo = VEC_COLS["bmod", layer][0] + 8 * g
                src = acc(key)[:, 0:2 * P].rearrange("p (m q r) -> p q m r", m=2, q=4)[:, :, :, 0:2]
                b = VEC[:, lo:lo + 8].rearrange("p (q m) -> p q m", q=4).unsqueeze(3).to_broadcast([P, 4, 2, 2])
                v.tensor_tensor(MOD[layer][:, 16 * g:16 * g + 16].rearrange("p (q m r) -> p q m r", q=4, m=2),
                                src, b, ALU.add).then_inc(freed(key), 1)

            def scale(layer, w):
                wait_taken(dve, ("turned_mod", 6 * layer + (1 if w == 1 else 4)))
                part = 1 if w == 1 else 4
                lo = VEC_COLS[f"g{w}", layer][0]
                g = VEC[:, lo:lo + DC].unsqueeze(2).to_broadcast([P, DC, 2])
                v.scalar_tensor_tensor(
                    small[f"scale{w}"][:].rearrange("p (a b) -> p a b", b=2),
                    MOD[layer][:, 16 * part:16 * part + 16].rearrange("p (a b) -> p a b", b=2),
                    1.0, g, ALU.add, ALU.mult).then_inc(scale_ready, 1)

            def norm(key, lo, hi):
                tiles = (hi - lo) // P
                n = FILLS["stat", key]
                dve.wait_ge(free[n % BANKS], n // BANKS + 1)
                v.reciprocal(small["rrms"][:, 0:tiles], small["rms"][:, 0:tiles]).then_inc(rrms_ready[key], 1)
                wait_full(dve, ("bcast", key))
                streams = 2 if lo == 0 else 1
                for c in range(DC):
                    if c >= 2:
                        dve.wait_ge(h_ready[key], streams * (c - 1))
                    v.tensor_tensor(TMP[:, c % 2, 0:hi - lo], XT[:, c, lo:hi], acc(("bcast", key))[:, 0:hi - lo],
                                    ALU.mult).then_inc(tmp_ready[key], 1)
                dve.wait_ge(tmp_ready[key], DC)
                dve.sem_inc(freed(("bcast", key)), 1)

            def in_proj(layer):
                lo, hi = x_range(layer)
                for j in range(5):
                    key = ("in", layer, ("q", j) if j < 4 else ("k", 0))
                    n = hi - lo if j < 4 else T
                    wait_full(dve, key)
                    v.tensor_copy(QK[:, j, 0:n], acc(key)[:, 0:n]).then_inc(freed(key), 1)
                for m in range(2 - layer):
                    key = ("in", layer, ("av", m))
                    wait_full(dve, key)
                    if layer == 0:
                        v.tensor_copy(V[:, 2 * m:2 * m + 2, 0:P],
                                      acc(key)[:].rearrange("p (t n) -> p t n", t=2)[:, :, P:2 * P])\
                            .then_inc(freed(key), 1)
                    else:
                        v.tensor_copy(V[:, :, 0:P], acc(key)[:].rearrange("p (t n) -> p t n", t=4))\
                            .then_inc(freed(key), 1)

            def bias(layer):
                dve.wait_ge(bias_in[layer], 16)
                dve.wait_ge(consts_in, 16)
                for qt in range(2):
                    view = BIAS[:, qt, :, :].rearrange("p h (r c) -> p (h r) c", c=GRID_W)
                    v.tensor_tensor(view, view, const("wmask").unsqueeze(1).to_broadcast([P, 16, GRID_W]), ALU.add)\
                        .then_inc(bias_ready[layer], 1)

            def qk_norm(layer):
                lo, hi = x_range(layer)
                tq = 4 if layer == 0 else 2
                cols = 2 * (4 * tq + 4)
                q_lo, k_lo = VEC_COLS["gq", layer][0], VEC_COLS["gk", layer][0]
                link(v.tensor_scalar(small["gq8"][:], VEC[:, q_lo:q_lo + 1], HD ** -0.5, None, ALU.mult))
                wait_taken(dve, ("qkstat", layer))
                v.reciprocal(small["qkr"][:, 0:cols], small["qks"][:, 0:cols]).then_inc(qk_rrms[layer], 1)
                for j in range(5):
                    key = ("qkb", layer, j)
                    n = hi - lo if j < 4 else T
                    gain = small["gq8"][:, 0:1] if j < 4 else VEC[:, k_lo:k_lo + 1]
                    wait_full(dve, key)
                    v.scalar_tensor_tensor(QK[:, j, 0:n], QK[:, j, 0:n], gain, acc(key)[:, 0:n], ALU.mult, ALU.mult)\
                        .then_inc(freed(key), 1)
                for j in range(5):
                    key = ("rope", layer, j)
                    c = lat_col(layer) if j < 4 else S
                    x = QK[:, j, c:c + S]
                    wait_full(dve, key)
                    v.tensor_tensor(small["t1"][:], acc(key)[:, 0:S], const("sin"), ALU.mult).then_inc(freed(key), 1)
                    n = FILLS[key]
                    link(v.tensor_tensor(x, x, const("cos"), ALU.mult))
                    dve.wait_ge(free[n % BANKS], n // BANKS + 1)
                    v.tensor_tensor(x, x, small["t1"][:], ALU.add).then_inc(qk_ready[layer], 1)
                    dve.wait_ge(qk_ready[layer], j + 1)

            def attention(layer):
                units = attention_units(layer)

                def maxima(u):
                    branch, h, stream = units[u]
                    for t in range(2):
                        col = 2 * u + t
                        if stream == LAT:
                            key = ("score", layer, u, t)
                            wait_full(dve, key)
                            src = acc(key)[:]
                            if branch == "B":
                                link(v.tensor_tensor(acc(key)[:, S:T], acc(key)[:, S:T], BIAS[:, t, h, :], ALU.add))
                        else:
                            key = ("score", layer, u, 0)
                            if t == 0:
                                wait_full(dve, key)
                            src = acc(key)[:, S * t:S * t + S]
                        ins = v.reduce_max(small["mx"][:, col:col + 1], src, AX)
                    link(ins)
                    v.tensor_scalar(small["nm"][:, 2 * u:2 * u + 2], small["mx"][:, 2 * u:2 * u + 2], -1.0, None,
                                    ALU.mult).then_inc(nm_ready[layer], 1)

                def normalise(u):
                    stream = units[u][2]
                    for q in range(2 if stream == LAT else 1):
                        wait_taken(dve, ("score", layer, u, q))
                    link(v.reciprocal(small["ri"][:, 2 * u:2 * u + 2], small["rs"][:, 2 * u:2 * u + 2]))
                    n = T if stream == LAT else S
                    for t in range(2):
                        p = PR[:, u % 2, t, 0:n]
                        ins = v.tensor_scalar(p, p, small["ri"][:, 2 * u + t:2 * u + t + 1], None, ALU.mult)
                    ins.then_inc(p_ready[layer], 1)

                def turned_out(u):
                    stream = units[u][2]
                    dve.wait_ge(turned_full[layer], u + 1)
                    if u >= 2:
                        dve.wait_ge(pv_full[layer], u - 1)
                    n = 2 if stream == LAT else 1
                    v.tensor_copy(PT[:, u % 2, n:2 * n, :], turned[1][:, 0:S * n].rearrange("p (t n) -> p t n", t=n))\
                        .then_inc(turned_out_dve[layer], 1)

                maxima(0)
                for u in range(len(units)):
                    if u + 1 < len(units):
                        maxima(u + 1)
                    normalise(u)
                    turned_out(u)
                    if layer == 0:
                        mod(MOD_IN_ATTENTION[u])

            def merge(layer):
                nq = S * len(streams_of(layer))
                for j in range(4):
                    for b in range(3):
                        for m in range(2):
                            key = ("proj", layer, j, b, m)
                            g = GATE[:, 2 * b + m, 0:nq]
                            dst = M[:, 2 * j + m, 0:nq]
                            wait_taken(dve, ("gate", layer, j, b, m))
                            wait_full(dve, key)
                            if b == 0:
                                v.tensor_tensor(dst, g, acc(key)[:, 0:nq], ALU.mult).then_inc(freed(key), 1)
                            else:
                                link(v.tensor_tensor(TMP[:, m, 0:nq], g, acc(key)[:, 0:nq], ALU.mult))
                                wait_taken(dve, ("proj", layer, j, b - 1, m))
                                v.tensor_tensor(dst, dst, TMP[:, m, 0:nq], ALU.add).then_inc(freed(key), 1)

            def residual(layer, part, key, c):
                streams = streams_of(layer)
                wait_full(dve, key)
                for n, stream in enumerate(streams):
                    x = XT[:, c, S * stream:S * stream + S]
                    ins = v.scalar_tensor_tensor(x, acc(key)[:, S * n:S * n + S], mod_vec(layer, part, c, stream), x,
                                                 ALU.mult, ALU.add)
                ins.then_inc(freed(key), 1)

            def feed_forward():
                later = list(MOD_IN_FFN)
                q = 0
                for part, n in enumerate(PART_CHUNKS):
                    for s in range(n // 2):
                        for m in range(2):
                            k1, k3 = ("w1", part, s, m), ("w3", part, s, m)
                            wait_taken(dve, k1)
                            wait_full(dve, k3)
                            if q >= 4:
                                dve.wait_ge(hid_lo_ready, q - 3)
                            v.tensor_tensor(HID[:, q % 4, :], SILU[:, m, :], acc(k3)[:], ALU.mult)\
                                .then_inc(freed(k3), 1)
                            q += 1
                        if later:
                            mod(later.pop(0))
                    for j in range(4):
                        for m in range(2):
                            residual(0, 5, ("down", part, j, m), 2 * j + m)
                        if later:
                            mod(later.pop(0))

            def route():
                wait_full(dve, ("logit",))
                rb = vec("rb").unsqueeze(1).to_broadcast([P, 2, 8])
                lg = R1
                link(v.tensor_tensor(lg[:], acc(("logit",))[:, 0:16].rearrange("p (t e) -> p t e", t=2), rb, ALU.add))
                dve.sem_inc(freed(("logit",)), 1)
                mine = lg[:].unsqueeze(3).to_broadcast([P, 2, 8, 8])
                other = lg[:].unsqueeze(2).to_broadcast([P, 2, 8, 8])
                low = const("lower").rearrange("p (a b) -> p a b", a=8).unsqueeze(1).to_broadcast([P, 2, 8, 8])
                link(v.tensor_tensor(CMP[:], other, mine, ALU.is_equal))
                link(v.tensor_tensor(CMP[:], CMP[:], low, ALU.mult))
                link(v.tensor_tensor(CMP2[:], other, mine, ALU.is_gt))
                link(v.tensor_tensor(CMP[:], CMP[:], CMP2[:], ALU.add))
                link(v.tensor_reduce(RANK[:], CMP[:], AX, ALU.add))
                v.tensor_scalar(SEL[:], RANK[:], 2.0, None, ALU.is_lt).then_inc(sel_ready, 1)
                link(v.reduce_max(RM[:], lg[:], AX))
                v.tensor_tensor(lg[:], lg[:], RM[:].unsqueeze(2).to_broadcast([P, 2, 8]), ALU.subtract)\
                    .then_inc(routed, 1)
                for i in range(4):
                    key = ("turn", i)
                    wait_full(dve, key)
                    t, half = divmod(i, 2)
                    v.tensor_copy(HTOK[:, t, 512 * half:512 * half + 512], acc(key)[:]).then_inc(freed(key), 1)
                dve.wait_ge(ex_ready, 1)
                link(v.tensor_tensor(EX[:], EX[:], SEL[:], ALU.mult))
                link(v.tensor_reduce(RSUM[:], EX[:], AX, ALU.add))
                link(v.reciprocal(RINV[:], RSUM[:]))
                link(v.tensor_tensor(W[:], EX[:], RINV[:].unsqueeze(2).to_broadcast([P, 2, 8]), ALU.mult))
                wait_full(dve, ("prefix",))
                src = acc(("prefix",))
                link(v.scalar_tensor_tensor(POS1[:], src[:, 0:16].rearrange("p (t e) -> p t e", t=2), 1.0, SEL[:],
                                            ALU.add, ALU.mult))
                link(v.tensor_scalar(POS[:], POS1[:], -1.0, None, ALU.add))
                link(v.tensor_copy(COUNTF[:], src[:, 16:24]))
                dve.sem_inc(freed(("prefix",)), 1)
                v.tensor_copy(COUNT[:], COUNTF[:]).then_inc(counts_ready, 1)
                link(v.reduce_max(MAXF[:], COUNTF[:], AX))
                v.tensor_copy(MAXI[:], MAXF[:]).then_inc(counts_ready, 1)
            def expert(e, i, again=0):
                iota = const("iota")[:, SLOTS * again:SLOTS * (again + 1)]
                for t in range(2):
                    pos = POS[:, t, bass.ds(e, 1)]
                    v.tensor_scalar(ONEHOT[:, t, :], iota, pos, None, ALU.is_equal)
                for t in range(2):
                    ins = v.tensor_scalar(WEIGHTED[:, t, :], iota, POS[:, t, bass.ds(e, 1)],
                                          W[:, t, bass.ds(e, 1)], ALU.is_equal, ALU.mult)
                ins.then_inc(onehot_ready, 1)

                def low(key):
                    moe_low_part(dve, v, EXPERT_AT[key], i, slice(0, LO_DVE), moe_lo_dve)

                def turned_hidden(g):
                    dve.wait_ge(ge_hi_ready, i * GROUPS + g + 1)
                    v.tensor_tensor(GE_LO[:, g % 2, :, :], ge_bank[:, 0:2 * SLOTS].rearrange("p (m n) -> p m n", m=2),
                                    GE_HI[:, g % 2, :, :].bitcast(F32), ALU.subtract).then_inc(ge_lo_ready, 1)

                low(("up", 0, 0))
                for b in range(2):
                    dve.wait_ge(he_ready, 2 * i + b + 1)
                    v.tensor_tensor(HE_LO[:, 4 * b:4 * b + 4, :],
                                    gath[b][:, 0:4 * SLOTS].rearrange("p (c n) -> p c n", c=4),
                                    HE_HI[:, 4 * b:4 * b + 4, :].bitcast(F32), ALU.subtract)\
                        .then_inc(he_lo_ready, 1)
                low(("up", 0, 1))
                for g in range(GROUPS):
                    if g:
                        if g >= 2:
                            low(("down", g - 1))
                        turned_hidden(g - 1)
                    if g + 1 < GROUPS:
                        low(("up", g + 1, 0))
                    dve.wait_ge(se_ready, i * GROUPS + g + 1)
                    v.tensor_tensor(GT[:, g % 2, :], SE[:, g % 2, :], up[g % 2][0:SLOTS, 256:512], ALU.mult)\
                        .then_inc(gt_ready, 1)
                    if g + 1 < GROUPS:
                        low(("up", g + 1, 1))
                    if g == 0:
                        low(("down", 0))
                low(("down", GROUPS - 1))
                turned_hidden(GROUPS - 1)
                wait_slab_used(dve, N_EXPERT_SLABS - 1, i)
                v.tensor_copy(YTOK[:, 0:512], down[0][0:SLOTS, :]).then_inc(ytok_dve, 1)
                for n in range(4):
                    dve.wait_ge(scattered, 4 * i + n + 1)
                    for c in range(2):
                        x = XT[:, 2 * n + c, S:T]
                        ins = v.scalar_tensor_tensor(x, gath[n % 2][:, S * c:S * c + S],
                                                     mod_vec(1, 5, 2 * n + c, LAT), x, ALU.mult, ALU.add)
                    ins.then_inc(x_added, 1)

            v.memset(small["cond"][:], 0.0).then_inc(cond_zeroed, 1)
            dve.wait_ge(vecs_in, 16)
            for n in MOD_AT_START:
                mod(n)
            for layer in L:
                scale(layer, 1)
                norm((layer, 1), 0, T)
                in_proj(layer)
                bias(layer)
                qk_norm(layer)
                attention(layer)
                merge(layer)
                for c in range(DC):
                    residual(layer, 2, ("out", layer, c // 2, c % 2), c)
                scale(layer, 2)
                lo, hi = x_range(layer)
                norm((layer, 2), lo, hi)
                if layer == 0:
                    feed_forward()
            route()
            with dve.Fori(0, N_EXPERTS) as e:
                expert(e, e)

            def skip():
                for s, n in ((onehot_ready, 1), (moe_lo_dve, N_EXPERT_SLABS), (he_lo_ready, 2), (gt_ready, GROUPS),
                             (ge_lo_ready, GROUPS), (ytok_dve, 1), (x_added, 4)):
                    dve.sem_inc(s, n)

            overflow_steps(dve, expert, skip)
            dve.wait_ge(final_rms, 1)
            v.reciprocal(small["rrms"][:, 0:2], small["rms"][:, 0:2]).then_inc(rrms_ready["final"], 1)
            dve.wait_ge(tmp_ready["final"], 1)
            lo = VEC_COLS["final"][0]
            for c in range(DC):
                v.scalar_tensor_tensor(OUT[:, c, :], XT[:, c, S:T], VEC[:, lo + c:lo + c + 1], bank[1][:, 0:S],
                                       ALU.mult, ALU.mult).then_inc(out_ready, 1)


def constants():
    c = np.zeros((P, N_CONST), np.float32)

    def put(name, value):
        lo, hi = CONST_COLS[name]
        c[:, lo:hi] = value

    put("ident", np.eye(P))
    put("ones", 1.0)
    p = np.arange(P)
    partner = np.where(p % 32 < 16, p + 16, p - 16)
    perm = np.zeros((P, P))
    perm[partner, p] = 1.0
    put("perm", perm)
    put("before", p[:, None] < p[None, :])
    put("blk2", p[:, None] // HD == np.arange(2)[None, :])
    t = np.arange(S)
    pos = np.stack([t // GRID_W, t % GRID_W], -1).astype(np.float32)
    inv_freq = np.float32(10000.0) ** (-np.arange(0, 32, 2, dtype=np.float32) / np.float32(32))
    ang = pos[:, :, None] * inv_freq[None, None, :]
    axis, i = (p % HD) // 32, p % 16
    put("cos", np.cos(ang)[:, axis, i].T)
    put("sin", np.sin(ang)[:, axis, i].T * np.where(p % 32 < 16, -1.0, 1.0)[:, None])
    col = p % GRID_W
    start = np.clip(col - 8, 0, GRID_W - 16)
    kc = np.arange(GRID_W)[None, :]
    put("wmask", np.where((kc >= start[:, None]) & (kc < start[:, None] + 16), 0.0, MASKED))
    put("iota", np.arange(PASSES * SLOTS))
    e = np.arange(8)
    put("lower", (e[None, :] < e[:, None]).reshape(1, 64))
    put("eps", EPS)
    pool = np.zeros((S, 4, S), np.float32)
    for g, w in enumerate((2, 4, 8, 16)):
        for out in range(S):
            lo, hi = max(out - w // 2, 0), min(out - w // 2 + w, S)
            pool[lo:hi, g, out] = 1.0 / (hi - lo)
            pool[out, g, out] -= 1.0
    pool = pool.reshape(2, P, 4 * S).transpose(1, 0, 2).reshape(P, -1)
    return c, np.ascontiguousarray(pool)


def slabs(w):
    k, n = w.shape
    w = w.reshape(k // P, P, n // 256, 256).transpose(2, 1, 0, 3)
    return np.ascontiguousarray(w).reshape(n // 256, P, k // P * 256)


def by_chunk(x):
    return x.reshape(-1, P).T


_ORDER = ["w_mod", "w_in", "w_proj", "w_out", "ffn_w1", "ffn_w3", "ffn_w2_0", "ffn_w2_1", "ffn_w2_2", "moe_up",
          "moe_w2", "xt", "vecs", "consts", "pool_mat", "pool_w", "rel_bias"]


def layout(x, c, ctx, c_ctx, w_mod, b_mod, norm1_g, norm2_g, w_in, q_norm_g, k_norm_g, na_rel_bias, pool_w,
           pool_scale, w_branch_a, w_branch_b, w_branch_c, w_out, ffn_w1, ffn_w3, ffn_w2, router_w, router_b,
           moe_w1, moe_w3, moe_w2, final_g):
    a = {}
    heads = np.array([h for j in range(4) for h in (j, 4 + j)])
    cols = (heads[:, None] * HD + np.arange(HD)).reshape(-1)
    w_in = np.concatenate([w_in[:, :, cols], w_in[:, :, 512:]], axis=2)
    a["w_mod"] = np.concatenate([slabs(w) for w in w_mod])
    a["w_in"] = np.concatenate([slabs(w) for w in w_in])
    proj = np.concatenate([w_branch_a[:, cols], w_branch_b, w_branch_c], axis=1)
    a["w_proj"] = np.concatenate([slabs(w) for w in proj])
    a["w_out"] = np.concatenate([slabs(w) for w in w_out])
    a["ffn_w1"], a["ffn_w3"] = slabs(ffn_w1[0]), slabs(ffn_w3[0])
    f0 = 0
    for part, n in enumerate(PART_CHUNKS):
        a[f"ffn_w2_{part}"] = slabs(ffn_w2[0, P * f0:P * (f0 + n)])
        f0 += n
    w = np.stack([moe_w1[0], moe_w3[0]]).reshape(2, N_EXPERTS, 2, 4, P, GROUPS, 256)
    a["moe_up"] = np.ascontiguousarray(w.transpose(1, 5, 2, 4, 3, 0, 6)).reshape(-1, SLAB)
    w = moe_w2[0].reshape(N_EXPERTS, GROUPS, 2, P, D).transpose(0, 1, 3, 2, 4)
    a["moe_w2"] = np.ascontiguousarray(w).reshape(-1, SLAB)
    xt = np.concatenate([ctx[0], x[0]], axis=0).T.reshape(DC, P, T).transpose(1, 0, 2)
    a["xt"] = np.ascontiguousarray(xt).reshape(P, DC * T)
    vecs = np.zeros((P, N_VEC), np.float32)

    def put(name, value):
        lo, hi = VEC_COLS[name]
        vecs[:, lo:hi] = value

    for l in range(DEPTH):
        put(("bmod", l), by_chunk(b_mod[l]))
        put(("g1", l), by_chunk(norm1_g[l]))
        put(("g2", l), by_chunk(norm2_g[l]))
        put(("gq", l), np.concatenate([q_norm_g[l]] * 2)[:, None])
        put(("gk", l), np.concatenate([k_norm_g[l]] * 2)[:, None])
        put(("pscale", l), by_chunk(pool_scale[l]))
    put("final", by_chunk(final_g))
    put("cond", np.stack([by_chunk(c[0]), by_chunk(c_ctx)], -1).reshape(P, 2 * DC))
    put("rw", router_w[0].reshape(DC, P, N_EXPERTS).transpose(1, 0, 2).reshape(P, -1))
    put("rb", router_b[0][None, :])
    a["vecs"] = vecs
    a["consts"], a["pool_mat"] = constants()
    pw = np.zeros((DEPTH, 2, HD, 2, 2, HD), np.float32)
    for g in range(4):
        pw[:, g % 2, :, g // 2, g % 2, :] = pool_w[:, g]
    a["pool_w"] = pw.reshape(DEPTH, P, 2 * P)
    t = np.arange(S)
    dr = t[None, :] // GRID_W - t[:, None] // GRID_W + 7
    dc = np.clip(t[None, :] % GRID_W - t[:, None] % GRID_W + 15, 0, 30)
    a["rel_bias"] = np.ascontiguousarray(
        na_rel_bias[:, :, dr, dc].reshape(DEPTH, 4, 2, P, S).transpose(0, 3, 2, 1, 4)).reshape(DEPTH, P, -1)
    return a


def kernel(**inputs):
    import concourse.bacc as bacc
    from concourse.bass_utils import run_bass_kernel_spmd

    arrays = layout(**{k: np.asarray(v) for k, v in inputs.items()})
    nc = bacc.Bacc("TRN2", target_bir_lowering=False, num_devices=1)
    aps = {}
    for name in _ORDER:
        arr = arrays[name]
        aps[name] = nc.dram_tensor(f"in_{name}", arr.shape, mybir.dt.from_np(arr.dtype), kind="ExternalInput").ap()
    aps["out"] = nc.dram_tensor("out_t", (P, DC * S), F32, kind="ExternalOutput").ap()
    build(nc, aps)
    r = run_bass_kernel_spmd(nc, [{f"in_{n}": arrays[n] for n in _ORDER}], core_ids=[0])
    out = np.asarray(r.results[0]["out_t"]).reshape(P, DC, S)
    return np.ascontiguousarray(out.transpose(2, 1, 0)).reshape(1, S, D)
```

```python
from contextlib import ExitStack

import numpy as np

import concourse.bass as bass
from concourse import mybir

F32 = mybir.dt.float32
F32R = mybir.dt.float32r
I32 = mybir.dt.int32
ALU = mybir.AluOpType
ACT = mybir.ActivationFunctionType
AX = mybir.AxisListType.X

P = 128
D = 1024
DC = D // P
S = 256
T = 2 * S
CTX, LAT = 0, 1
DEPTH = 2
HD = 64
GRID_W = 64
KEY_TILES = T // P
F_DENSE = 2816
PART_CHUNKS = (8, 8, 6)
N_EXPERTS = 8
F_EXPERT = 3584
GROUPS = F_EXPERT // 256
SLOTS = 96
PASSES = -(-S // SLOTS)
EPS = 1e-6
SLAB = 2048
RING = 3
MOE_RING = 7
MOE_SPLIT = 3
LO_DVE = 3
BANKS = 5
MASKED = -1e30

CONST_COLS = {}
_at = 0
for _name, _n in (("ident", P), ("ones", P), ("perm", P), ("before", P), ("blk2", 2), ("cos", S), ("sin", S),
                  ("wmask", GRID_W), ("iota", PASSES * SLOTS), ("lower", 64), ("eps", 1)):
    CONST_COLS[_name] = (_at, _at + _n)
    _at += _n
N_CONST = _at
VEC_COLS = {}
_at = 0
for _name, _n in (("bmod", 48), ("g1", DC), ("g2", DC), ("gq", 1), ("gk", 1), ("pscale", 2)):
    for _l in range(DEPTH):
        VEC_COLS[_name, _l] = (_at, _at + _n)
        _at += _n
for _name, _n in (("final", DC), ("cond", 2 * DC), ("rw", DC * N_EXPERTS), ("rb", N_EXPERTS)):
    VEC_COLS[_name] = (_at, _at + _n)
    _at += _n
N_VEC = _at

W_IN_Q = (0, 1)
W_IN_KV, W_IN_BQ, W_IN_BK, W_IN_BV, W_IN_U, W_IN_GATE = 2, 3, 4, 5, 6, 7


MOD_AT_START, MOD_IN_ATTENTION, MOD_IN_FFN = range(8), range(8, 32), range(34, 42)
MOD_IN_NORM = {(0, 1): (), (0, 2): (32, 33), (1, 1): (42, 43), (1, 2): (44, 45, 46, 47)}


def attention_units(layer):
    streams = (LAT, CTX) if layer == 0 else (LAT,)
    return [(b, h, s) for b, n in (("A", 8), ("B", 4)) for s in streams for h in range(n)]


def is_split(slab):
    return slab[0] in ("in", "w1", "w3", "w2")


def schedule():
    slabs, fills = [], []

    def mod(n):
        slabs.append(("mod", n))
        fills.append(("mod", n))
        if n % 4 == 3:
            fills.append(("turned_mod", n // 4))

    def norm(key):
        fills.extend([("stat", key), ("bcast", key)])
        if key == (0, 2):
            slabs.extend([("w1", 0, 0), ("w3", 0, 0)])
        for n in MOD_IN_NORM[key]:
            mod(n)

    for n in MOD_AT_START:
        mod(n)
    for layer in range(DEPTH):
        norm((layer, 1))
        for s in range(7):
            slabs.append(("in", layer, s))
        names = [("q", j) for j in range(4)] + [("k", 0)] + [("av", m) for m in range(2)]
        fills.extend(("in", layer, n) for n in names + [("bq", 0), ("bq", 1)])
        fills.append(("qkstat", layer))
        fills.extend(("in", layer, n) for n in [("bk", 0), ("bk", 1)])
        fills.extend(("qkb", layer, j) for j in range(5))
        fills.extend(("in", layer, n) for n in [("bv", 0), ("bv", 1)])
        fills.extend(("rope", layer, j) for j in range(5))
        fills.extend(("in", layer, ("u", m)) for m in range(layer, 2))
        units = attention_units(layer)
        for u in range(2):
            fills.extend(("score", layer, u, q) for q in range(2 if units[u][2] == LAT else 1))
        for u in range(len(units)):
            if u + 2 < len(units):
                fills.extend(("score", layer, u + 2, q) for q in range(2 if units[u + 2][2] == LAT else 1))
            if layer == 0:
                mod(MOD_IN_ATTENTION[u])
        fills.extend(("pool", layer, p) for p in range(2))
        fills.extend(("poolw", layer, p) for p in range(2))
        for j in range(4):
            slabs.extend(("in", layer, W_IN_GATE + 4 * b + j) for b in range(3))
            fills.extend(("gate", layer, j, b, m) for b in range(3) for m in range(2))
            slabs.append(("proj", layer, j))
            fills.extend(("proj", layer, j, b, m) for b in range(3) for m in range(2))
        for j in range(4):
            slabs.append(("out", layer, j))
            fills.extend(("out", layer, j, m) for m in range(2))
        norm((layer, 2))
        if layer == 0:
            later = list(MOD_IN_FFN)
            for part, n in enumerate(PART_CHUNKS):
                for s in range(n // 2):
                    if (part, s) != (0, 0):
                        slabs.extend([("w1", part, s), ("w3", part, s)])
                    fills.extend([("w1", part, s, 0), ("w1", part, s, 1), ("w3", part, s, 0), ("w3", part, s, 1)])
                    if later:
                        mod(later.pop(0))
                for j in range(4):
                    slabs.append(("w2", part, j))
                    fills.extend(("down", part, j, m) for m in range(2))
                    if later:
                        mod(later.pop(0))
            assert not later
    fills.append(("logit",))
    fills.extend(("turn", i) for i in range(4))
    fills.append(("prefix",))
    return {k: n for n, k in enumerate(slabs)}, {k: n for n, k in enumerate(fills)}


SLABS, FILLS = schedule()
SPLITS = {k: n for n, k in enumerate(k for k in SLABS if is_split(k))}
SHARED = [("in", 1, s) for s in range(2, 19)]
SHARED.sort(key=SPLITS.get)


def last_fill(slab):
    kind = slab[0]
    if kind == "mod":
        return slab
    if kind == "in":
        _, layer, s = slab
        if s >= W_IN_GATE:
            b, j = divmod(s - W_IN_GATE, 4)
            return ("gate", layer, j, b, 1)
        return ("in", layer, (("q", 1), ("q", 3), ("av", 1), ("bq", 1), ("bk", 1), ("bv", 1), ("u", 1))[s])
    if kind == "proj":
        return ("proj", slab[1], slab[2], 2, 1)
    if kind == "out":
        return ("out", slab[1], slab[2], 1)
    if kind in ("w1", "w3"):
        return slab + (1,)
    return ("down", slab[1], slab[2], 1)

EXPERT_SLABS = []
for _g in range(GROUPS):
    EXPERT_SLABS += [("up", _g, 0), ("up", _g, 1)]
    if _g:
        EXPERT_SLABS.append(("down", _g - 1))
EXPERT_SLABS.append(("down", GROUPS - 1))
EXPERT_AT = {k: n for n, k in enumerate(EXPERT_SLABS)}
N_EXPERT_SLABS = len(EXPERT_SLABS)
ROUNDS = N_EXPERT_SLABS // MOE_RING
assert ROUNDS * MOE_RING == N_EXPERT_SLABS and N_EXPERT_SLABS % MOE_SPLIT == 0


def build(nc, a):
    with ExitStack() as ctx:
        base = -(-nc.sbuf_base // 32) * 32

        def at(name, kb, shape, dt=F32):
            return nc.alloc_sbuf_tensor_at(name, shape, dt, offset=base + -(-int(kb * 1024) // 32) * 32)

        def sem(name):
            return ctx.enter_context(nc.semaphore(name))

        def psum(name, shape):
            return ctx.enter_context(nc.psum_tensor(name, shape, F32))

        ring = [at(f"slab{i}", 8 * i, [P, DC, 256]) for i in range(RING)]
        w_hi = [at(f"w_hi{i}", 24 + 8 * i, [P, DC, 256], F32R) for i in range(2)]
        w_lo = [at(f"w_lo{i}", 40 + 8 * i, [P, DC, 256], F32R) for i in range(2)]
        Y = at("Y", 56, [P, DC, T])
        QK = at("QK", 72, [P, 5, T])
        BQ = at("BQ", 82, [P, 2, T])
        BK = at("BK", 86, [P, 2, T])
        V = at("V", 90, [P, KEY_TILES, 384])
        U = at("U", 96, [P, KEY_TILES, 256])
        M = at("M", 72, [P, DC, T])
        GATE = at("GATE", 88, [P, 6, T])
        HID_HI = at("HID_HI", 56, [P, 8, T], F32R)
        HID_LO = at("HID_LO", 72, [P, 8, T], F32R)
        HID = at("HID", 88, [P, 4, T])
        SILU = at("SILU", 96, [P, 2, T])
        H_LO = at("H_LO", 100, [P, DC, T], F32R)
        XT = at("XT", 116, [P, DC, T])
        H_HI = at("H_HI", 132, [P, DC, T], F32R)
        H = at("H", 132, [P, DC, T])
        BIAS = at("BIAS", 148, [P, 2, 4, S])
        POOL = at("POOL", 156, [P, 2, 4, S])
        PR = at("PR", 164, [P, 2, 2, T])
        PT = at("PT", 172, [P, 2, 4, S])
        QK_SQ = at("QK_SQ", 164, [P, 5, T])
        SQ_SUM = at("SQ_SUM", 176, [P, T])
        SQ = at("SQ", 180, [P, 2, T])
        TMP = at("TMP", 184, [P, 2, T])
        DT = at("DT", 164, [P, 2, T])
        H_NEW = at("H_NEW", 168, [P, 4, T])
        PW = at("PW", 188, [P, 2, P])
        CONST = at("CONST", 189, [P, N_CONST])
        VEC = at("VEC", 195, [P, N_VEC])
        kb = 195 + N_VEC * 4 / 1024
        small = {}
        for name, n in (("cond", 32 * DC), ("modrow", 256), ("mod0", 96), ("mod1", 96), ("scale1", 2 * DC), ("scale2", 2 * DC),
                        ("rms", 4), ("rrms", 4), ("qks", 40), ("qkr", 40), ("gq8", 1),
                        ("mx", 48), ("nm", 48), ("rs", 48), ("ri", 48), ("t1", S)):
            kb = -(-kb * 1024 // 32) * 32 / 1024
            small[name] = at(f"s_{name}", kb, [P, n])
            kb += n * 4 / 1024
        assert kb <= 207, kb
        moe_slab = [at(f"moe_slab{i}", 8 * i, [P, 4, 512]) for i in range(MOE_RING)]
        moe_hi = [at(f"moe_hi{i}", 56 + 8 * i, [P, 4, 512], F32R) for i in range(MOE_SPLIT)]
        moe_lo = [at(f"moe_lo{i}", 80 + 8 * i, [P, 4, 512], F32R) for i in range(MOE_SPLIT)]
        HTOK = at("HTOK", 152, [P, 2, D])
        HE_HI = at("HE_HI", 160, [P, DC, SLOTS], F32R)
        HE_LO = at("HE_LO", 163, [P, DC, SLOTS], F32R)
        SE = at("SE", 166, [SLOTS, 2, 256])
        GT = at("GT", 168, [SLOTS, 2, 256])
        GE_HI = at("GE_HI", 170, [P, 2, 2, SLOTS], F32R)
        GE_LO = at("GE_LO", 171.5, [P, 2, 2, SLOTS], F32R)
        YTOK = at("YTOK", 173, [SLOTS, D])
        ONEHOT = at("ONEHOT", 177, [P, 2, SLOTS])
        WEIGHTED = at("WEIGHTED", 178, [P, 2, SLOTS])
        SCATTER = at("SCATTER", 179, [SLOTS, S])
        R1 = at("R1", 148, [P, 2, 8])
        CMP = at("CMP", 148.25, [P, 2, 8, 8])
        CMP2 = at("CMP2", 149, [P, 2, 8, 8])
        RANK, SEL, EX, POS1 = (at(n, 149.5 + i / 8, [P, 2, 8]) for i, n in enumerate(
            ("RANK", "SEL", "EX", "POS1")))
        W, POS = (at(n, 150 + i / 8, [P, 2, N_EXPERTS + 1]) for i, n in enumerate(("W", "POS")))
        RM, RSUM, RINV = (at(n, 150.5 + i / 8, [P, 2]) for i, n in enumerate(("RM", "RSUM", "RINV")))
        COUNT = at("COUNT", 151, [P, 8], I32)
        COUNTF = at("COUNTF", 151.125, [P, 8])
        MAXF = at("MAXF", 151.25, [P, 1])
        MAXI = at("MAXI", 151.375, [P, 1], I32)
        OUT = at("OUT", 132, [P, DC, S])

        def const(name, p0=0, p1=P):
            lo, hi = CONST_COLS[name]
            return CONST[p0:p1, lo:hi]

        def vec(name):
            lo, hi = VEC_COLS[name]
            return VEC[:, lo:hi]

        ident, ones, eps = const("ident"), const("ones"), const("eps")
        MOD = [small["mod0"], small["mod1"]]

        def mod_vec(layer, part, chunk, stream):
            col = (part * DC + chunk) * 2 + (1 - stream)
            return MOD[layer][:, col:col + 1]

        bank = [psum(f"bank{i}", [P, 512]) for i in range(BANKS)]
        turned = [psum(f"turned{i}", [P, 512]) for i in range(2)]
        pv_bank = psum("pv_bank", [P, 512])

        consts_in, vecs_in, x_in, pool_in = sem("consts_in"), sem("vecs_in"), sem("x_in"), sem("pool_in")
        slab_in = [sem(f"slab_in{i}") for i in range(RING)]
        hi_ready, lo_pool, lo_dve = sem("hi_ready"), sem("lo_pool"), sem("lo_dve")
        h_hi_ready, h_lo_ready = ({k: sem(f"{n}{k[0]}{k[1]}") for k in ((0, 1), (0, 2), (1, 1))}
                                  for n in ("h_hi_ready", "h_lo_ready"))
        hid_hi_ready, hid_lo_ready = sem("hid_hi_ready"), sem("hid_lo_ready")
        full = [sem(f"full{i}") for i in range(BANKS)]
        free = [sem(f"free{i}") for i in range(BANKS)]
        cond_ready, cond_zeroed = sem("cond_ready"), sem("cond_zeroed")
        dve_seq = sem("dve_seq")
        L = range(DEPTH)
        norms = [(0, 1), (0, 2), (1, 1), (1, 2), "final"]
        sq_ready = {k: sem(f"sq_ready{i}") for i, k in enumerate(norms)}
        sq_summed = {k: sem(f"sq_summed{i}") for i, k in enumerate(norms)}
        stat_ready, final_rms = sem("stat_ready"), sem("final_rms")
        rrms_ready = {k: sem(f"rrms_ready{i}") for i, k in enumerate(norms)}
        tmp_ready = {k: sem(f"tmp_ready{i}") for i, k in enumerate(norms)}
        h_ready = {k: sem(f"h_ready{i}") for i, k in enumerate(norms)}
        scale_ready = sem("scale_ready")
        qk_sq = [sem(f"qk_sq{l}") for l in L]
        qk_rrms = [sem(f"qk_rrms{l}") for l in L]
        qk_ready = [sem(f"qk_ready{l}") for l in L]
        bias_in, bias_ready = [sem(f"bias_in{l}") for l in L], [sem(f"bias_ready{l}") for l in L]
        pw_in = [sem(f"pw_in{l}") for l in L]
        nm_ready = [sem(f"nm_ready{l}") for l in L]
        p_ready = [sem(f"p_ready{l}") for l in L]
        turned_full = [sem(f"turned_full{l}") for l in L]
        turned_out_act = [sem(f"turned_out_act{l}") for l in L]
        turned_out_dve = [sem(f"turned_out_dve{l}") for l in L]
        pv_full = [sem(f"pv_full{l}") for l in L]
        y_ready = [sem(f"y_ready{l}") for l in L]
        routed = sem("routed")
        ex_ready = sem("ex_ready")
        sel_ready, counts_ready = sem("sel_ready"), sem("counts_ready")
        moe_in = [sem(f"moe_in{i}") for i in range(MOE_RING)]
        onehot_ready, gathered, he_ready = sem("onehot_ready"), sem("gathered"), sem("he_ready")
        weights_turned, scatter_ready = sem("weights_turned"), sem("scatter_ready")
        moe_hi_ready, moe_lo_dve, moe_lo_pool = sem("moe_hi_ready"), sem("moe_lo_dve"), sem("moe_lo_pool")
        slab_used = sem("slab_used")
        se_ready, gt_ready, ge_turned = sem("se_ready"), sem("gt_ready"), sem("ge_turned")
        ge_hi_ready, ge_lo_ready, he_lo_ready = sem("ge_hi_ready"), sem("ge_lo_ready"), sem("he_lo_ready")
        ytok_dve, ytok_act = sem("ytok_dve"), sem("ytok_act")
        scattered, x_added = sem("scattered"), sem("x_added")
        step_over = sem("step_over")
        out_ready, out_done = sem("out_ready"), sem("out_done")

        def acc(key):
            return bank[FILLS[key] % BANKS]

        def wait_full(eng, key):
            n = FILLS[key]
            eng.wait_ge(full[n % BANKS], n // BANKS + 1)

        def wait_taken(eng, key):
            n = FILLS[key]
            eng.wait_ge(free[n % BANKS], n // BANKS + 1)

        def freed(key):
            return free[FILLS[key] % BANKS]

        def wait_parts(eng, key):
            eng.wait_ge(lo_pool, SPLITS[key] + 1)
            if key in SHARED:
                eng.wait_ge(lo_dve, SHARED.index(key) + 1)

        def low_part(eng, engine, key, lo_col, hi_col, done):
            n, at = SPLITS[key], SLABS[key]
            eng.wait_ge(hi_ready, n + 1)
            eng.wait_ge(slab_in[at % RING], 16 * (at // RING + 1))
            raw, hi, lo = (t[:].rearrange("p k n -> p (k n)")[:, lo_col:hi_col]
                           for t in (ring[at % RING], w_hi[n % 2], w_lo[n % 2]))
            engine.tensor_tensor(lo, raw, hi.bitcast(F32), ALU.subtract).then_inc(done, 1)

        def slab_size(key):
            return PART_CHUNKS[key[1]] * 256 if key[0] == "w2" else SLAB

        def x_range(layer):
            return (0, T) if layer == 0 else (S, T)

        def streams_of(layer):
            return (CTX, LAT) if layer == 0 else (LAT,)

        def lat_col(layer):
            return S if layer == 0 else 0

        def wait_expert_slab(eng, k, i):
            eng.wait_ge(moe_in[k % MOE_RING], i * (16 * ROUNDS) + 16 * (k // MOE_RING + 1))

        def wait_slab_used(eng, k, i):
            eng.wait_ge(slab_used, i * N_EXPERT_SLABS + k + 1)

        def moe_low_part(eng, engine, k, i, blocks, done):
            eng.wait_ge(moe_hi_ready, i * N_EXPERT_SLABS + k + 1)
            wait_expert_slab(eng, k, i)
            n = k % MOE_SPLIT
            engine.tensor_tensor(moe_lo[n][:, blocks, :], moe_slab[k % MOE_RING][:, blocks, :],
                                 moe_hi[n][:, blocks, :].bitcast(F32), ALU.subtract).then_inc(done, 1)


        up = [bank[0], bank[1]]
        down = [bank[2], bank[3]]
        gath = [bank[4], turned[0]]
        ge_bank = turned[1]
        wt_bank = pv_bank

        def overflow_steps(eng, body, skip):
            eng.wait_ge(x_added, N_EXPERTS * 4)
            eng.wait_ge(counts_ready, 2)
            most = eng.value_load(MAXI[0:1, 0:1], min_val=0, max_val=S)
            with eng.If(most > SLOTS):
                with eng.Fori(0, N_EXPERTS) as e:
                    count = eng.value_load(COUNT[0:1, bass.ds(e, 1)], min_val=0, max_val=S)
                    for again in range(1, PASSES):
                        i = e * (PASSES - 1) + (N_EXPERTS + again - 1)
                        with eng.If(count > SLOTS * again):
                            body(e, i, again)
                            eng.wait_ge(x_added, i * 4 + 4)
                            eng.sem_inc(step_over, 1)
                        with eng.Else():
                            skip()

        block = ctx.enter_context(nc.Block())

        @block.sync
        def _(sp):
            def slab_source(key):
                kind = key[0]
                if kind == "mod":
                    return a["w_mod"][key[1]]
                if kind == "in":
                    return a["w_in"][key[1] * 19 + key[2]]
                if kind == "proj":
                    return a["w_proj"][key[1] * 4 + key[2]]
                if kind == "out":
                    return a["w_out"][key[1] * 4 + key[2]]
                _, part, i = key
                if kind in ("w1", "w3"):
                    return a["ffn_" + kind][sum(PART_CHUNKS[:part]) // 2 + i]
                return a[f"ffn_w2_{part}"][i]

            def load_slab(n, key):
                if n >= RING:
                    before = order[n - RING]
                    if is_split(before):
                        wait_parts(sp, before)
                    else:
                        wait_full(sp, last_fill(before))
                dst = ring[n % RING].rearrange("p k n -> p (k n)")[:, 0:slab_size(key)]
                sp.dma_start(dst, slab_source(key)).then_inc(slab_in[n % RING], 16)

            order = list(SLABS)
            sp.dma_start(VEC[:], a["vecs"]).then_inc(vecs_in, 16)
            load_slab(0, order[0])
            sp.dma_start(CONST[:], a["consts"]).then_inc(consts_in, 16)
            for n in range(1, RING):
                load_slab(n, order[n])
            sp.dma_start(XT[:].rearrange("p k n -> p (k n)"), a["xt"]).then_inc(x_in, 16)
            for n in range(RING, len(order)):
                load_slab(n, order[n])

            def expert_load(k, e):
                kind, g = EXPERT_SLABS[k][:2]
                if kind == "up":
                    src, row, n = a["moe_up"], g * 2 * P + EXPERT_SLABS[k][2] * P, GROUPS * 2 * P
                else:
                    src, row, n = a["moe_w2"], g * P, GROUPS * P
                sp.dma_start(moe_slab[k % MOE_RING][:].rearrange("p k n -> p (k n)"),
                             src[bass.ds(e * n + row, P), :]).then_inc(moe_in[k % MOE_RING], 16)

            def expert_head(e):
                for k in range(MOE_RING):
                    expert_load(k, e)

            def wait_split(k, i):
                sp.wait_ge(moe_lo_dve, i * N_EXPERT_SLABS + k + 1)
                sp.wait_ge(moe_lo_pool, i * N_EXPERT_SLABS + k + 1)

            def expert_rest(e, i):
                for k in range(MOE_RING, N_EXPERT_SLABS):
                    wait_split(k - MOE_RING, i)
                    expert_load(k, e)

            wait_full(sp, ("out", 1, 3, 1))
            for k in range(RING, MOE_RING):
                expert_load(k, 0)
            wait_full(sp, ("mod", 47))
            for k in range(RING):
                expert_load(k, 0)
            with sp.Fori(0, N_EXPERTS - 1) as e:
                expert_rest(e, e)
                for k in range(MOE_RING):
                    wait_split(N_EXPERT_SLABS - MOE_RING + k, e)
                    expert_load(k, e + 1)
            expert_rest(N_EXPERTS - 1, N_EXPERTS - 1)

            def overflow(e, i, again):
                expert_head(e)
                expert_rest(e, i)

            overflow_steps(sp, overflow, lambda: [sp.sem_inc(s, 16 * ROUNDS) for s in moe_in])
            for c in range(0, DC, 2):
                sp.wait_ge(out_ready, c + 2)
                sp.dma_start(a["out"][:, S * c:S * (c + 2)], OUT[:, c:c + 2, :].rearrange("p k n -> p (k n)"))\
                    .then_inc(out_done, 16)
            sp.wait_ge(out_done, 16 * DC // 2)

        @block.gpsimd
        def _(pool):
            lo_of = iter(SPLITS)

            def next_low_part():
                key = next(lo_of)
                low_part(pool, nc.gpsimd, key, SLAB // 2 if key in SHARED else 0, slab_size(key), lo_pool)

            def h_low_parts(key):
                for c in range(DC):
                    pool.wait_ge(h_hi_ready[key], c + 1)
                    nc.gpsimd.tensor_tensor(H_LO[:, c, :], H_NEW[:, c % 4, :], H_HI[:, c, :].bitcast(F32),
                                            ALU.subtract).then_inc(h_lo_ready[key], 1)

            def small_loads(layer):
                pool.dma_start(PW[:].rearrange("p a n -> p (a n)"), a["pool_w"][layer]).then_inc(pw_in[layer], 16)
                pool.dma_start(BIAS[:].rearrange("p a h n -> p (a h n)"), a["rel_bias"][layer])\
                    .then_inc(bias_in[layer], 16)

            for _ in range(2):
                next_low_part()
            h_low_parts((0, 1))
            pool.dma_start(POOL[:].rearrange("p a g n -> p (a g n)"), a["pool_mat"]).then_inc(pool_in, 16)
            small_loads(0)
            for _ in range(2, W_IN_GATE + 2):
                next_low_part()
            pool.wait_ge(bias_ready[0], 2)
            pool.wait_ge(nm_ready[0], len(attention_units(0)))
            wait_full(pool, ("poolw", 0, 1))
            small_loads(1)
            for _ in range(W_IN_GATE + 2, W_IN_GATE + 12):
                next_low_part()
            for _ in range(2):
                next_low_part()
            h_low_parts((0, 2))
            q = 0
            for part, n in enumerate(PART_CHUNKS):
                for s in range(n // 2):
                    next_low_part()
                    for m in range(2):
                        pool.wait_ge(hid_hi_ready, q + 1)
                        nc.gpsimd.tensor_tensor(HID_LO[:, 2 * s + m, :], HID[:, q % 4, :],
                                                HID_HI[:, 2 * s + m, :].bitcast(F32), ALU.subtract)\
                            .then_inc(hid_lo_ready, 1)
                        q += 1
                    next_low_part()
                for j in range(4 if part < len(PART_CHUNKS) - 1 else 2):
                    next_low_part()
            next_low_part()
            h_low_parts((1, 1))
            for _ in range(1, 19):
                next_low_part()
            assert next(lo_of, None) is None

            def expert(e, i, again=0):
                for k in range(N_EXPERT_SLABS):
                    moe_low_part(pool, nc.gpsimd, k, i, slice(LO_DVE, 4), moe_lo_pool)

            with pool.Fori(0, N_EXPERTS) as e:
                expert(e, e)
            overflow_steps(pool, expert, lambda: pool.sem_inc(moe_lo_pool, N_EXPERT_SLABS))

        @block.tensor
        def _(pe):
            def fill(key):
                n = FILLS[key]
                if n >= BANKS:
                    pe.wait_ge(free[n % BANKS], n // BANKS)
                return bank[n % BANKS]

            def filled(ins, key):
                ins.then_inc(full[FILLS[key] % BANKS], 1)

            def slab(key):
                if is_split(key):
                    wait_parts(pe, key)
                    return w_hi[SPLITS[key] % 2], w_lo[SPLITS[key] % 2]
                n = SLABS[key]
                pe.wait_ge(slab_in[n % RING], 16 * (n // RING + 1))
                return (ring[n % RING],)

            mm = nc.tensor.matmul

            def piece(parts, *at):
                return [t[at] for t in parts]

            def products(out, lhs, rhs, start, stop):
                if len(lhs) == 1:
                    return mm(out, lhs[0], rhs[0], start=start, stop=stop)
                mm(out, lhs[0], rhs[0], start=start, stop=False)
                mm(out, lhs[0], rhs[1], start=False, stop=False)
                return mm(out, lhs[1], rhs[0], start=False, stop=stop)

            def split_chain(out, pairs):
                last = len(pairs) - 1
                for k, (lhs, rhs) in enumerate(pairs):
                    ins = products(out, lhs, rhs, k == 0, k == last)
                return ins

            def chain(out, pairs):
                last = len(pairs) - 1
                for k, (lhs, rhs) in enumerate(pairs):
                    ins = mm(out, lhs, rhs, start=k == 0, stop=k == last)
                return ins

            def mod(n):
                (w,), out, q = slab(("mod", n)), fill(("mod", n)), n % 4
                filled(chain(out[32 * q:32 * q + 32, 0:256],
                             [(small["cond"][:, 32 * k:32 * k + 32], w[:, k, :]) for k in range(DC)]), ("mod", n))
                if q == 3:
                    key = ("turned_mod", n // 4)
                    out = fill(key)
                    if n == 3:
                        pe.wait_ge(consts_in, 16)
                    for back in range(4):
                        wait_taken(pe, ("mod", n - back))
                    for m in range(2):
                        ins = nc.tensor.transpose(out[:, P * m:P * m + P], small["modrow"][:, P * m:P * m + P], ident)
                    filled(ins, key)

            def norm(key, lo, hi):
                tiles = (hi - lo) // P
                out = fill(("stat", key))
                pe.wait_ge(sq_summed[key], DC - 1)
                for t in range(tiles):
                    ins = mm(out[:, t:t + 1], SQ_SUM[:, P * t:P * t + P], ones[:, 0:1], start=True, stop=True)
                filled(ins, ("stat", key))
                out = fill(("bcast", key))
                pe.wait_ge(rrms_ready[key], 1)
                for t in range(tiles):
                    ins = mm(out[:, P * t:P * t + P], small["rrms"][:, t:t + 1].to_broadcast([P, P]), ident,
                             start=True, stop=True)
                filled(ins, ("bcast", key))
                for n in MOD_IN_NORM[key]:
                    mod(n)

            def in_proj(layer):
                lo, hi = x_range(layer)
                first = [True]
                ALL = slice(None)
                h = (H_HI, H_LO)

                def h_chunk(k):
                    if first[0]:
                        pe.wait_ge(h_lo_ready[layer, 1], k + 1)
                        if k == DC - 1:
                            first[0] = False

                def by_feature(name, w, m, c0, c1):
                    out = fill(("in", layer, name))
                    for k in range(DC):
                        h_chunk(k)
                        ins = products(out[:, 0:c1 - c0], piece(w, ALL, k, slice(P * m, P * m + P)),
                                       piece(h, ALL, k, slice(c0, c1)), k == 0, k == DC - 1)
                    filled(ins, ("in", layer, name))

                def by_token(name, w, tiles, c0, c1):
                    out = fill(("in", layer, name))
                    for n, t in enumerate(tiles):
                        ins = split_chain(out[:, n * (c1 - c0):(n + 1) * (c1 - c0)],
                                          [(piece(h, ALL, k, slice(P * t, P * t + P)),
                                            piece(w, ALL, k, slice(c0, c1))) for k in range(DC)])
                    filled(ins, ("in", layer, name))

                for s in range(2):
                    w = slab(("in", layer, s))
                    for m in range(2):
                        by_feature(("q", 2 * s + m), w, m, lo, hi)
                w = slab(("in", layer, W_IN_KV))
                by_feature(("k", 0), w, 0, 0, T)
                for m in range(2):
                    by_token(("av", m), w, (2 * m, 2 * m + 1), 0, 256)
                w = slab(("in", layer, W_IN_BQ))
                for m in range(2):
                    by_feature(("bq", m), w, m, lo, hi)
                qk_stat(layer)
                w = slab(("in", layer, W_IN_BK))
                for m in range(2):
                    by_feature(("bk", m), w, m, 0, T)
                qk_bcast(layer)
                w = slab(("in", layer, W_IN_BV))
                for m in range(2):
                    by_token(("bv", m), w, (2 * m, 2 * m + 1), 0, 256)
                rope(layer)
                w = slab(("in", layer, W_IN_U))
                for m in (range(2) if layer == 0 else (1,)):
                    by_token(("u", m), w, (2 * m, 2 * m + 1), 0, 256)

            def qk_stat(layer):
                tq = 4 if layer == 0 else 2
                out = fill(("qkstat", layer))
                for j in range(5):
                    pe.wait_ge(qk_sq[layer], j + 1)
                    for t in range(tq if j < 4 else 4):
                        col = 2 * (j * tq + t)
                        ins = mm(out[:, col:col + 2], QK_SQ[:, j, P * t:P * t + P], const("blk2"),
                                 start=True, stop=True)
                filled(ins, ("qkstat", layer))

            def qk_bcast(layer):
                tq = 4 if layer == 0 else 2
                for j in range(5):
                    out = fill(("qkb", layer, j))
                    if j == 0:
                        pe.wait_ge(qk_rrms[layer], 1)
                    for t in range(tq if j < 4 else 4):
                        col = 2 * (j * tq + t)
                        for g in range(2):
                            ins = mm(out[HD * g:HD * g + HD, P * t:P * t + P],
                                     small["qkr"][:, col + g:col + g + 1].to_broadcast([P, HD]), ident,
                                     start=True, stop=True)
                    filled(ins, ("qkb", layer, j))

            def rope(layer):
                for j in range(5):
                    out = fill(("rope", layer, j))
                    wait_taken(pe, ("qkb", layer, j))
                    c = lat_col(layer) if j < 4 else S
                    ins = mm(out[:, 0:S], const("perm"), QK[:, j, c:c + S], start=True, stop=True)
                    filled(ins, ("rope", layer, j))

            def place(branch, h):
                if branch == "A":
                    g = h // 4
                    return QK[:, h % 4], HD * g, QK[:, 4], HD * g, h % 4
                return BQ[:, h // 2], HD * (h % 2), BK[:, h // 2], P + HD * h, 4 + h // 2

            def attention(layer):
                units = attention_units(layer)
                c_lat = lat_col(layer)

                def scores(u):
                    branch, h, stream = units[u]
                    q, p0, k, _, _ = place(branch, h)
                    col = c_lat if stream == LAT else 0
                    if u == 0:
                        pe.wait_ge(qk_ready[layer], 5)
                    if branch == "B" and h == 0:
                        for name in ("bq", "bk"):
                            for m in range(2):
                                wait_taken(pe, ("in", layer, (name, m)))
                    for t in range(2):
                        lhs = q[p0:p0 + HD, col + P * t:col + P * t + P]
                        if stream == LAT:
                            out = fill(("score", layer, u, t))
                            filled(mm(out[:], lhs, k[p0:p0 + HD, :], start=True, stop=True), ("score", layer, u, t))
                        else:
                            if t == 0:
                                out = fill(("score", layer, u, 0))
                            ins = mm(out[:, S * t:S * t + S], lhs, k[p0:p0 + HD, 0:S], start=True, stop=True)
                    if stream == CTX:
                        filled(ins, ("score", layer, u, 0))

                def turn(u):
                    stream = units[u][2]
                    pe.wait_ge(p_ready[layer], u + 1)
                    if u:
                        pe.wait_ge(turned_out_act[layer], u)
                        pe.wait_ge(turned_out_dve[layer], u)
                    tiles = 4 if stream == LAT else 2
                    for t in range(tiles):
                        b, n = divmod(t, tiles // 2)
                        for qt in range(2):
                            ins = nc.tensor.transpose(turned[b][:, S * n + P * qt:S * n + P * qt + P],
                                                      PR[:, u % 2, qt, P * t:P * t + P], ident)
                    ins.then_inc(turned_full[layer], 1)

                def values(u):
                    branch, h, stream = units[u]
                    _, p0, _, vcol, _ = place(branch, h)
                    pe.wait_ge(turned_out_act[layer], u + 1)
                    pe.wait_ge(turned_out_dve[layer], u + 1)
                    if u == 0:
                        for name in (("av", 0), ("av", 1), ("bv", 0), ("bv", 1)):
                            wait_taken(pe, ("in", layer, name))
                    else:
                        pe.wait_ge(y_ready[layer], u)
                    tiles = 4 if stream == LAT else 2
                    ins = chain(pv_bank[p0:p0 + HD, 0:S],
                                [(V[:, t, vcol:vcol + HD], PT[:, u % 2, t, :]) for t in range(tiles)])
                    ins.then_inc(pv_full[layer], 1)

                scores(0)
                scores(1)
                for u in range(len(units)):
                    if u + 2 < len(units):
                        scores(u + 2)
                    if u:
                        values(u - 1)
                    turn(u)
                    if layer == 0:
                        mod(MOD_IN_ATTENTION[u])
                values(len(units) - 1)

            def pooling(layer):
                if layer == 0:
                    pe.wait_ge(pool_in, 16)
                for m in (range(2) if layer == 0 else (1,)):
                    wait_taken(pe, ("in", layer, ("u", m)))
                for p in range(2):
                    out = fill(("pool", layer, p))
                    for n, stream in enumerate(streams_of(layer)):
                        for gg in range(2):
                            g = 2 * p + gg
                            ins = chain(out[HD * gg:HD * gg + HD, S * n:S * n + S],
                                        [(U[:, 2 * stream + t, HD * g:HD * g + HD], POOL[:, t, g, :])
                                         for t in range(2)])
                    filled(ins, ("pool", layer, p))
                nq = S * len(streams_of(layer))
                pe.wait_ge(pw_in[layer], 16)
                for p in range(2):
                    out = fill(("poolw", layer, p))
                    wait_taken(pe, ("pool", layer, p))
                    filled(mm(out[:, 0:nq], PW[:, p, :], DT[:, p, 0:nq], start=True, stop=True), ("poolw", layer, p))

            BRANCH_CHUNKS = (range(0, 4), range(4, 6), range(6, 8))

            def merge(layer):
                lo, hi = x_range(layer)
                nq = hi - lo
                for j in range(4):
                    for b in range(3):
                        w = slab(("in", layer, W_IN_GATE + 4 * b + j))
                        for m in range(2):
                            key = ("gate", layer, j, b, m)
                            out = fill(key)
                            filled(split_chain(out[:, 0:nq], [
                                ([t[:, k, P * m:P * m + P] for t in w], [t[:, k, lo:hi] for t in (H_HI, H_LO)])
                                for k in range(DC)]), key)
                    (w,) = slab(("proj", layer, j))
                    if j == 0:
                        pe.wait_ge(y_ready[layer], len(attention_units(layer)))
                        for p in range(2):
                            wait_taken(pe, ("poolw", layer, p))
                    for b in range(3):
                        for m in range(2):
                            key = ("proj", layer, j, b, m)
                            out = fill(key)
                            filled(chain(out[:, 0:nq], [(w[:, k, P * m:P * m + P], Y[:, k, 0:nq])
                                                        for k in BRANCH_CHUNKS[b]]), key)

            def out_proj(layer):
                nq = S * len(streams_of(layer))
                wait_taken(pe, ("proj", layer, 3, 2, 1))
                for j in range(4):
                    (w,) = slab(("out", layer, j))
                    for m in range(2):
                        key = ("out", layer, j, m)
                        out = fill(key)
                        filled(chain(out[:, 0:nq], [(w[:, k, P * m:P * m + P], M[:, k, 0:nq])
                                                    for k in range(DC)]), key)

            def feed_forward():
                later = list(MOD_IN_FFN)
                done = 0
                for part, n in enumerate(PART_CHUNKS):
                    for s in range(n // 2):
                        for name in ("w1", "w3"):
                            w = slab((name, part, s))
                            for m in range(2):
                                key = (name, part, s, m)
                                out = fill(key)
                                for k in range(DC):
                                    if part == 0 and s == 0 and name == "w1" and m == 0:
                                        pe.wait_ge(h_lo_ready[0, 2], k + 1)
                                    ins = products(out[:], [t[:, k, P * m:P * m + P] for t in w],
                                                   [t[:, k, :] for t in (H_HI, H_LO)], k == 0, k == DC - 1)
                                filled(ins, key)
                        if later:
                            mod(later.pop(0))
                    done += n
                    pe.wait_ge(hid_lo_ready, done)
                    for j in range(4):
                        w = [t[:].rearrange("p k n -> p (k n)")[:, 0:n * 256].rearrange("p (k n) -> p k n", k=n)
                             for t in slab(("w2", part, j))]
                        for m in range(2):
                            key = ("down", part, j, m)
                            out = fill(key)
                            filled(split_chain(out[:], [
                                ([t[:, k, P * m:P * m + P] for t in w], [t[:, k, :] for t in (HID_HI, HID_LO)])
                                for k in range(n)]), key)
                        if later:
                            mod(later.pop(0))

            def route():
                out = fill(("logit",))
                for t in range(2):
                    for k in range(DC):
                        if t == 0:
                            pe.wait_ge(h_ready[1, 2], k + 1)
                        lo = VEC_COLS["rw"][0] + N_EXPERTS * k
                        ins = mm(out[:, 8 * t:8 * t + 8], H[:, k, S + P * t:S + P * t + P],
                                 VEC[:, lo:lo + N_EXPERTS], start=k == 0, stop=k == DC - 1)
                filled(ins, ("logit",))
                for i in range(4):
                    out = fill(("turn", i))
                    t, half = divmod(i, 2)
                    for c in range(4):
                        ins = nc.tensor.transpose(out[:, P * c:P * c + P],
                                                  H[:, 4 * half + c, S + P * t:S + P * t + P], ident)
                    filled(ins, ("turn", i))
                out = fill(("prefix",))
                pe.wait_ge(sel_ready, 1)
                mm(out[:, 0:8], const("before"), SEL[:, 0, :], start=True, stop=True)
                mm(out[:, 8:16], ones, SEL[:, 0, :], start=True, stop=False)
                mm(out[:, 8:16], const("before"), SEL[:, 1, :], start=False, stop=True)
                mm(out[:, 16:24], ones, SEL[:, 0, :], start=True, stop=False)
                filled(mm(out[:, 16:24], ones, SEL[:, 1, :], start=False, stop=True), ("prefix",))

            def gather(n):
                pe.wait_ge(onehot_ready, n + 1)
                for b in range(2):
                    for c in range(4):
                        for t in range(2):
                            ins = mm(gath[b][:, SLOTS * c:SLOTS * c + SLOTS],
                                     HTOK[:, t, P * (4 * b + c):P * (4 * b + c) + P], ONEHOT[:, t, :],
                                     start=t == 0, stop=t == 1)
                    ins.then_inc(gathered, 1)

            def expert(e, i, again=0):
                mine = i + 1 if again else i
                if again:
                    gather(mine)
                for t in range(2):
                    ins = nc.tensor.transpose(wt_bank[0:SLOTS, P * t:P * t + P], WEIGHTED[:, t, :], ident)
                ins.then_inc(weights_turned, 1)

                def parts(key):
                    k = EXPERT_AT[key]
                    pe.wait_ge(moe_lo_dve, i * N_EXPERT_SLABS + k + 1)
                    pe.wait_ge(moe_lo_pool, i * N_EXPERT_SLABS + k + 1)
                    return moe_hi[k % MOE_SPLIT], moe_lo[k % MOE_SPLIT]

                def up_half(g, half):
                    w = parts(("up", g, half))
                    for kk in range(4):
                        k = 4 * half + kk
                        if g == 0:
                            pe.wait_ge(he_lo_ready, 2 * mine + half + 1)
                        ins = products(up[g % 2][0:SLOTS, :], (HE_HI[:, k, :], HE_LO[:, k, :]),
                                       [t[:, kk, :] for t in w], k == 0, k == DC - 1)
                    ins.then_inc(slab_used, 1)

                def turn_hidden(g):
                    pe.wait_ge(gt_ready, i * GROUPS + g + 1)
                    for m in range(2):
                        ins = nc.tensor.transpose(ge_bank[:, SLOTS * m:SLOTS * m + SLOTS],
                                                  GT[:, g % 2, P * m:P * m + P], ident[0:SLOTS, 0:SLOTS])
                    ins.then_inc(ge_turned, 1)

                def down_group(g):
                    w = parts(("down", g))
                    pe.wait_ge(ge_lo_ready, i * GROUPS + g + 1)
                    for k in range(2):
                        for n in range(2):
                            ins = products(down[n][0:SLOTS, :], (GE_HI[:, g % 2, k, :], GE_LO[:, g % 2, k, :]),
                                           [t[:, 2 * k + n, :] for t in w],
                                           g == 0 and k == 0, g == GROUPS - 1 and k == 1)
                    ins.then_inc(slab_used, 1)

                for g in range(GROUPS):
                    up_half(g, 0)
                    if g:
                        turn_hidden(g - 1)
                    up_half(g, 1)
                    if g == GROUPS - 1 and not again:
                        gather(i + 1)
                    if g:
                        down_group(g - 1)
                turn_hidden(GROUPS - 1)
                down_group(GROUPS - 1)
                pe.wait_ge(scatter_ready, i + 1)
                pe.wait_ge(he_lo_ready, 2 * i + 4)
                for n in range(4):
                    if n == 0:
                        pe.wait_ge(ytok_dve, i + 1)
                    if n == 2:
                        pe.wait_ge(ytok_act, i + 1)
                    if n >= 2:
                        pe.wait_ge(x_added, i * 4 + n - 1)
                    for c in range(2):
                        col = P * (2 * n + c)
                        ins = mm(gath[n % 2][:, S * c:S * c + S], YTOK[:, col:col + P], SCATTER[:],
                                 start=True, stop=True)
                    ins.then_inc(scattered, 1)
                pe.wait_ge(x_added, i * 4 + 4)

            pe.wait_ge(cond_ready, 1)
            for n in MOD_AT_START:
                mod(n)
            for layer in L:
                norm((layer, 1), 0, T)
                in_proj(layer)
                attention(layer)
                pooling(layer)
                merge(layer)
                out_proj(layer)
                if layer == 0:
                    norm((0, 2), 0, T)
                    feed_forward()
                else:
                    norm((1, 2), S, T)
            route()
            for i in range(4):
                wait_taken(pe, ("turn", i))
            pe.wait_ge(counts_ready, 2)
            gather(0)
            with pe.Fori(0, N_EXPERTS) as e:
                expert(e, e)

            def skip():
                for s, n in ((gathered, 2), (weights_turned, 1), (slab_used, N_EXPERT_SLABS), (ge_turned, GROUPS),
                             (scattered, 4)):
                    pe.sem_inc(s, n)

            overflow_steps(pe, expert, skip)
            out = up[0]
            pe.wait_ge(sq_summed["final"], DC - 1)
            for t in range(2):
                ins = mm(out[:, t:t + 1], SQ_SUM[:, P * t:P * t + P], ones[:, 0:1], start=True, stop=True)
            ins.then_inc(stat_ready, 1)
            out = up[1]
            pe.wait_ge(rrms_ready["final"], 1)
            for t in range(2):
                ins = mm(out[:, P * t:P * t + P], small["rrms"][:, t:t + 1].to_broadcast([P, P]), ident,
                         start=True, stop=True)
            ins.then_inc(tmp_ready["final"], 1)

        @block.scalar
        def _(act):
            af = nc.scalar.activation

            hi_of = iter(SPLITS)

            def high_part():
                key = next(hi_of)
                n = SPLITS[key]
                act.wait_ge(slab_in[SLABS[key] % RING], 16 * (SLABS[key] // RING + 1))
                if n >= 2:
                    wait_full(act, last_fill(list(SPLITS)[n - 2]))
                raw, hi = (t[:].rearrange("p k n -> p (k n)")[:, 0:slab_size(key)]
                           for t in (ring[SLABS[key] % RING], w_hi[n % 2]))
                af(hi, raw, ACT.Copy).then_inc(hi_ready, 1)

            def squares(key, lo, hi, chunks, src_ready):
                for c in chunks:
                    src_ready(c)
                    if c >= 2:
                        act.wait_ge(sq_summed[key], max(1, c - 2))
                    af(SQ[:, c % 2, 0:hi - lo], XT[:, c, lo:hi], ACT.Square).then_inc(sq_ready[key], 1)

            def norm(key, lo, hi):
                layer, w = key
                wait_full(act, ("stat", key))
                tiles = (hi - lo) // P
                af(small["rms"][:, 0:tiles], acc(("stat", key))[:, 0:tiles], ACT.Sqrt, scale=1.0 / D, bias=eps)\
                    .then_inc(freed(("stat", key)), 1)
                part = 0 if w == 1 else 3
                scale = small["scale1" if w == 1 else "scale2"]
                if w == 1:
                    act.wait_ge(scale_ready, 2 * layer + 1)
                else:
                    act.wait_ge(scale_ready, 2 * layer + 2)
                def h_rounded(c):
                    act.wait_ge(h_ready[key], 2 * (c + 1))
                    af(H_HI[:, c, :], H_NEW[:, c % 4, :], ACT.Copy).then_inc(h_hi_ready[key], 1)

                for c in range(DC):
                    act.wait_ge(tmp_ready[key], c + 1)
                    if key != (1, 2) and c >= 4:
                        act.wait_ge(h_lo_ready[key], c - 3)
                    dst = H_NEW[:, c % 4, :] if key != (1, 2) else H[:, c, :]
                    for n, stream in enumerate((CTX, LAT) if lo == 0 else (LAT,)):
                        col = 2 * c + (1 - stream)
                        af(dst[:, S * stream:S * stream + S], TMP[:, c % 2, S * n:S * n + S], ACT.Identity,
                           scale=scale[:, col:col + 1], bias=mod_vec(layer, part, c, stream))\
                            .then_inc(h_ready[key], 1)
                    if key != (1, 2) and c:
                        h_rounded(c - 1)
                if key != (1, 2):
                    h_rounded(DC - 1)
                if key == (1, 1):
                    high_part()

            def in_proj(layer):
                lo, hi = x_range(layer)
                nq = hi - lo
                tq = 4 if layer == 0 else 2

                def square(j):
                    wait_taken(act, ("in", layer, ("q", j) if j < 4 else ("k", 0)))
                    n = nq if j < 4 else T
                    af(QK_SQ[:, j, 0:n], QK[:, j, 0:n], ACT.Square).then_inc(qk_sq[layer], 1)

                high_part()
                square(0)
                square(1)
                high_part()
                square(2)
                square(3)
                high_part()
                square(4)
                for m in range(2):
                    key = ("in", layer, ("bq", m))
                    wait_full(act, key)
                    af(BQ[:, m, 0:nq], acc(key)[:, 0:nq], ACT.Copy, scale=HD ** -0.5).then_inc(freed(key), 1)
                high_part()
                wait_full(act, ("qkstat", layer))
                cols = 2 * (4 * tq + 4)
                af(small["qks"][:, 0:cols], acc(("qkstat", layer))[:, 0:cols], ACT.Sqrt, scale=1.0 / HD, bias=eps)\
                    .then_inc(freed(("qkstat", layer)), 1)
                for m in range(2):
                    key = ("in", layer, ("bk", m))
                    wait_full(act, key)
                    af(BK[:, m, :], acc(key)[:], ACT.Copy).then_inc(freed(key), 1)
                high_part()
                for m in range(2):
                    key = ("in", layer, ("bv", m))
                    wait_full(act, key)
                    af(V[:, 2 * m:2 * m + 2, P:384], acc(key)[:].rearrange("p (t n) -> p t n", t=2), ACT.Copy)\
                        .then_inc(freed(key), 1)
                for m in (range(2) if layer == 0 else (1,)):
                    key = ("in", layer, ("u", m))
                    wait_full(act, key)
                    af(U[:, 2 * m:2 * m + 2, :], acc(key)[:].rearrange("p (t n) -> p t n", t=2), ACT.Copy)\
                        .then_inc(freed(key), 1)

            def attention(layer):
                units = attention_units(layer)

                def exps(u):
                    stream = units[u][2]
                    act.wait_ge(nm_ready[layer], u + 1)
                    if u >= 2:
                        act.wait_ge(turned_full[layer], u - 1)
                    for t in range(2):
                        col = 2 * u + t
                        if stream == LAT:
                            key = ("score", layer, u, t)
                            src, n = acc(key)[:], T
                        else:
                            key = ("score", layer, u, 0)
                            src, n = acc(key)[:, S * t:S * t + S], S
                        ins = af(PR[:, u % 2, t, 0:n], src, ACT.Exp, bias=small["nm"][:, col:col + 1],
                                 accum_out=small["rs"][:, col:col + 1])
                        if stream == LAT or t == 1:
                            ins.then_inc(freed(key), 1)

                def turned_out(u):
                    stream = units[u][2]
                    act.wait_ge(turned_full[layer], u + 1)
                    if u >= 2:
                        act.wait_ge(pv_full[layer], u - 1)
                    n = 2 if stream == LAT else 1
                    af(PT[:, u % 2, 0:n, :], turned[0][:, 0:S * n].rearrange("p (t n) -> p t n", t=n), ACT.Copy)\
                        .then_inc(turned_out_act[layer], 1)

                def result(u):
                    branch, h, stream = units[u]
                    p0 = HD * (h // 4) if branch == "A" else HD * (h % 2)
                    chunk = h % 4 if branch == "A" else 4 + h // 2
                    col = lat_col(layer) if stream == LAT else 0
                    act.wait_ge(pv_full[layer], u + 1)
                    af(Y[p0:p0 + HD, chunk, col:col + S], pv_bank[p0:p0 + HD, 0:S], ACT.Copy)\
                        .then_inc(y_ready[layer], 1)

                exps(0)
                for u in range(len(units)):
                    if u + 1 < len(units):
                        exps(u + 1)
                    if u:
                        result(u - 1)
                    turned_out(u)
                for _ in range(2):
                    high_part()
                result(len(units) - 1)

            def pooling(layer):
                nq = S * len(streams_of(layer))
                for p in range(2):
                    key = ("pool", layer, p)
                    wait_full(act, key)
                    af(DT[:, p, 0:nq], acc(key)[:, 0:nq], ACT.Copy).then_inc(freed(key), 1)
                for p in range(2):
                    key = ("poolw", layer, p)
                    wait_full(act, key)
                    lo = VEC_COLS["pscale", layer][0] + p
                    af(Y[:, 6 + p, 0:nq], acc(key)[:, 0:nq], ACT.Copy, scale=VEC[:, lo:lo + 1])\
                        .then_inc(freed(key), 1)

            def merge(layer):
                nq = S * len(streams_of(layer))
                for j in range(4):
                    for b in range(3):
                        for m in range(2):
                            i = 2 * b + m
                            key = ("gate", layer, j, b, m)
                            wait_full(act, key)
                            if j:
                                wait_taken(act, ("proj", layer, j - 1, b, m))
                            af(GATE[:, i, 0:nq], acc(key)[:, 0:nq], ACT.Sigmoid).then_inc(freed(key), 1)
                        if 3 * j + b < 10:
                            high_part()

            def feed_forward():
                before = None
                q = 0
                for part, n in enumerate(PART_CHUNKS):
                    for s in range(n // 2):
                        for m in range(2):
                            key = ("w1", part, s, m)
                            wait_full(act, key)
                            if before:
                                wait_taken(act, before + (m,))
                            af(SILU[:, m, :], acc(key)[:], ACT.Silu).then_inc(freed(key), 1)
                        before = ("w3", part, s)
                        high_part()
                        for m in range(2):
                            wait_taken(act, before + (m,))
                            af(HID_HI[:, 2 * s + m, :], HID[:, q % 4, :], ACT.Copy).then_inc(hid_hi_ready, 1)
                            q += 1
                        high_part()
                    for j in range(4 if part < len(PART_CHUNKS) - 1 else 2):
                        high_part()
            def gathered_out(n):
                for b in range(2):
                    act.wait_ge(gathered, 2 * n + b + 1)
                    af(HE_HI[:, 4 * b:4 * b + 4, :],
                       gath[b][:, 0:4 * SLOTS].rearrange("p (c n) -> p c n", c=4), ACT.Copy).then_inc(he_ready, 1)

            def expert(e, i, again=0):
                def high(key):
                    k = EXPERT_AT[key]
                    wait_expert_slab(act, k, i)
                    if k >= MOE_SPLIT:
                        wait_slab_used(act, k - MOE_SPLIT, i)
                    af(moe_hi[k % MOE_SPLIT][:], moe_slab[k % MOE_RING][:], ACT.Copy).then_inc(moe_hi_ready, 1)

                def turned_hidden(g):
                    act.wait_ge(ge_turned, i * GROUPS + g + 1)
                    af(GE_HI[:, g % 2, :, :], ge_bank[:, 0:2 * SLOTS].rearrange("p (m n) -> p m n", m=2), ACT.Copy)\
                        .then_inc(ge_hi_ready, 1)

                high(("up", 0, 0))
                if again:
                    gathered_out(i + 1)
                high(("up", 0, 1))
                act.wait_ge(weights_turned, i + 1)
                af(SCATTER[:], wt_bank[0:SLOTS, 0:S], ACT.Copy).then_inc(scatter_ready, 1)
                for g in range(GROUPS):
                    if g:
                        if g >= 2:
                            high(("down", g - 1))
                        turned_hidden(g - 1)
                    if g + 1 < GROUPS:
                        high(("up", g + 1, 0))
                    wait_slab_used(act, EXPERT_AT["up", g, 1], i)
                    af(SE[:, g % 2, :], up[g % 2][0:SLOTS, 0:256], ACT.Silu).then_inc(se_ready, 1)
                    if g + 1 < GROUPS:
                        high(("up", g + 1, 1))
                    if g == 0:
                        high(("down", 0))
                high(("down", GROUPS - 1))
                if not again:
                    gathered_out(i + 1)
                turned_hidden(GROUPS - 1)
                wait_slab_used(act, N_EXPERT_SLABS - 1, i)
                af(YTOK[:, 512:1024], down[1][0:SLOTS, :], ACT.Copy).then_inc(ytok_act, 1)

            act.wait_ge(vecs_in, 16)
            act.wait_ge(cond_zeroed, 1)
            af(small["cond"][:].rearrange("p (k n) -> p k n", n=32)[:, :, 0:2],
               vec("cond").rearrange("p (k n) -> p k n", n=2), ACT.Silu).then_inc(cond_ready, 1)
            act.wait_ge(consts_in, 16)
            squares((0, 1), 0, T, range(DC), lambda c: act.wait_ge(x_in, 16))
            for _ in range(2):
                high_part()
            for layer in L:
                norm((layer, 1), 0, T)
                in_proj(layer)
                attention(layer)
                pooling(layer)
                merge(layer)
                lo, hi = x_range(layer)
                def out_added(c):
                    wait_taken(act, ("out", layer, c // 2, c % 2))

                squares((layer, 2), lo, hi, range(0, 4), out_added)
                if layer == 0:
                    high_part()
                squares((layer, 2), lo, hi, range(4, 6), out_added)
                if layer == 0:
                    high_part()
                squares((layer, 2), lo, hi, range(6, 8), out_added)
                norm((layer, 2), lo, hi)
                if layer == 0:
                    feed_forward()

                    def down_added(c):
                        wait_taken(act, ("down", 2, c // 2, c % 2))

                    squares((1, 1), 0, T, range(6), down_added)
                    high_part()
                    squares((1, 1), 0, T, range(6, DC), down_added)
            assert next(hi_of, None) is None
            act.wait_ge(routed, 1)
            af(EX[:], R1[:], ACT.Exp).then_inc(ex_ready, 1)
            gathered_out(0)
            with act.Fori(0, N_EXPERTS) as e:
                expert(e, e)

            def skip():
                for s, n in ((moe_hi_ready, N_EXPERT_SLABS), (he_ready, 2), (scatter_ready, 1), (se_ready, GROUPS),
                             (ge_hi_ready, GROUPS), (ytok_act, 1)):
                    act.sem_inc(s, n)

            overflow_steps(act, expert, skip)
            squares("final", S, T, range(DC), lambda c: None)
            act.wait_ge(stat_ready, 1)
            af(small["rms"][:, 0:2], bank[0][:, 0:2], ACT.Sqrt, scale=1.0 / D, bias=eps)\
                .then_inc(final_rms, 1)

        @block.vector
        def _(dve):
            v = nc.vector
            seq = [0]

            def link(ins):
                seq[0] += 1
                ins.then_inc(dve_seq, 1)
                dve.wait_ge(dve_seq, seq[0])

            def mod(n):
                rows = slice(32 * (n % 4), 32 * (n % 4) + 32)
                wait_full(dve, ("mod", n))
                v.tensor_copy(small["modrow"][rows, :], acc(("mod", n))[rows, 0:256]).then_inc(freed(("mod", n)), 1)
                if n % 4 < 3:
                    return
                key = ("turned_mod", n // 4)
                wait_full(dve, key)
                layer, g = divmod(n // 4, 6)
                lo = VEC_COLS["bmod", layer][0] + 8 * g
                src = acc(key)[:, 0:2 * P].rearrange("p (m q r) -> p q m r", m=2, q=4)[:, :, :, 0:2]
                b = VEC[:, lo:lo + 8].rearrange("p (q m) -> p q m", q=4).unsqueeze(3).to_broadcast([P, 4, 2, 2])
                v.tensor_tensor(MOD[layer][:, 16 * g:16 * g + 16].rearrange("p (q m r) -> p q m r", q=4, m=2),
                                src, b, ALU.add).then_inc(freed(key), 1)

            def scale(layer, w):
                wait_taken(dve, ("turned_mod", 6 * layer + (1 if w == 1 else 4)))
                part = 1 if w == 1 else 4
                lo = VEC_COLS[f"g{w}", layer][0]
                g = VEC[:, lo:lo + DC].unsqueeze(2).to_broadcast([P, DC, 2])
                v.scalar_tensor_tensor(
                    small[f"scale{w}"][:].rearrange("p (a b) -> p a b", b=2),
                    MOD[layer][:, 16 * part:16 * part + 16].rearrange("p (a b) -> p a b", b=2),
                    1.0, g, ALU.add, ALU.mult).then_inc(scale_ready, 1)

            def norm(key, lo, hi):
                tiles = (hi - lo) // P
                n = FILLS["stat", key]
                dve.wait_ge(free[n % BANKS], n // BANKS + 1)
                v.reciprocal(small["rrms"][:, 0:tiles], small["rms"][:, 0:tiles]).then_inc(rrms_ready[key], 1)
                wait_full(dve, ("bcast", key))
                streams = 2 if lo == 0 else 1
                mods = list(MOD_IN_NORM[key])
                for c in range(DC):
                    if c >= 2:
                        dve.wait_ge(h_ready[key], streams * (c - 1))
                    v.tensor_tensor(TMP[:, c % 2, 0:hi - lo], XT[:, c, lo:hi], acc(("bcast", key))[:, 0:hi - lo],
                                    ALU.mult).then_inc(tmp_ready[key], 1)
                    if c in (1, 3, 5) and mods:
                        mod(mods.pop(0))
                dve.wait_ge(tmp_ready[key], DC)
                dve.sem_inc(freed(("bcast", key)), 1)
                for n in mods:
                    mod(n)

            def sum_squares(key, lo, hi, c):
                dve.wait_ge(sq_ready[key], c + 1)
                n = hi - lo
                if c > 1:
                    dve.wait_ge(sq_summed[key], c - 1)
                v.tensor_tensor(SQ_SUM[:, 0:n], SQ[:, 0, 0:n] if c == 1 else SQ_SUM[:, 0:n], SQ[:, c % 2, 0:n], ALU.add)\
                    .then_inc(sq_summed[key], 1)

            def residuals(layer, part, keys, norm_key):
                for c, key in enumerate(keys):
                    residual(layer, part, key, c)
                    if norm_key and c >= 2:
                        sum_squares(norm_key, *x_range(layer), c - 1)
                    if c % 2 and later and norm_key != (layer, 2):
                        mod(later.pop(0))
                if norm_key:
                    sum_squares(norm_key, *x_range(layer), DC - 1)

            def in_proj(layer):
                lo, hi = x_range(layer)
                for j in range(5):
                    key = ("in", layer, ("q", j) if j < 4 else ("k", 0))
                    n = hi - lo if j < 4 else T
                    wait_full(dve, key)
                    v.tensor_copy(QK[:, j, 0:n], acc(key)[:, 0:n]).then_inc(freed(key), 1)
                    if layer == 1 and j % 2:
                        low_half(2 + j // 2)
                for m in range(2):
                    key = ("in", layer, ("av", m))
                    wait_full(dve, key)
                    v.tensor_copy(V[:, 2 * m:2 * m + 2, 0:P],
                                  acc(key)[:].rearrange("p (t n) -> p t n", t=2)[:, :, P:2 * P])\
                        .then_inc(freed(key), 1)
                if layer == 1:
                    low_half(4)

            def low_half(slab):
                low_part(dve, v, ("in", 1, slab), 0, SLAB // 2, lo_dve)

            def bias(layer):
                dve.wait_ge(bias_in[layer], 16)
                dve.wait_ge(consts_in, 16)
                for qt in range(2):
                    view = BIAS[:, qt, :, :].rearrange("p h (r c) -> p (h r) c", c=GRID_W)
                    v.tensor_tensor(view, view, const("wmask").unsqueeze(1).to_broadcast([P, 16, GRID_W]), ALU.add)\
                        .then_inc(bias_ready[layer], 1)

            def qk_norm(layer):
                lo, hi = x_range(layer)
                tq = 4 if layer == 0 else 2
                cols = 2 * (4 * tq + 4)
                q_lo, k_lo = VEC_COLS["gq", layer][0], VEC_COLS["gk", layer][0]
                link(v.tensor_scalar(small["gq8"][:], VEC[:, q_lo:q_lo + 1], HD ** -0.5, None, ALU.mult))
                wait_taken(dve, ("qkstat", layer))
                v.reciprocal(small["qkr"][:, 0:cols], small["qks"][:, 0:cols]).then_inc(qk_rrms[layer], 1)
                if layer == 1:
                    low_half(5)
                for j in range(5):
                    key = ("qkb", layer, j)
                    n = hi - lo if j < 4 else T
                    gain = small["gq8"][:, 0:1] if j < 4 else VEC[:, k_lo:k_lo + 1]
                    wait_full(dve, key)
                    v.scalar_tensor_tensor(QK[:, j, 0:n], QK[:, j, 0:n], gain, acc(key)[:, 0:n], ALU.mult, ALU.mult)\
                        .then_inc(freed(key), 1)
                if layer == 1:
                    low_half(6)
                for j in range(5):
                    key = ("rope", layer, j)
                    c = lat_col(layer) if j < 4 else S
                    x = QK[:, j, c:c + S]
                    wait_full(dve, key)
                    v.tensor_tensor(small["t1"][:], acc(key)[:, 0:S], const("sin"), ALU.mult).then_inc(freed(key), 1)
                    n = FILLS[key]
                    link(v.tensor_tensor(x, x, const("cos"), ALU.mult))
                    dve.wait_ge(free[n % BANKS], n // BANKS + 1)
                    v.tensor_tensor(x, x, small["t1"][:], ALU.add).then_inc(qk_ready[layer], 1)
                    dve.wait_ge(qk_ready[layer], j + 1)

            def attention(layer):
                units = attention_units(layer)

                def maxima(u):
                    branch, h, stream = units[u]
                    for t in range(2):
                        col = 2 * u + t
                        if stream == LAT:
                            key = ("score", layer, u, t)
                            wait_full(dve, key)
                            src = acc(key)[:]
                            if branch == "B":
                                link(v.tensor_tensor(acc(key)[:, S:T], acc(key)[:, S:T], BIAS[:, t, h, :], ALU.add))
                        else:
                            key = ("score", layer, u, 0)
                            if t == 0:
                                wait_full(dve, key)
                            src = acc(key)[:, S * t:S * t + S]
                        ins = v.reduce_max(small["mx"][:, col:col + 1], src, AX)
                    link(ins)
                    v.tensor_scalar(small["nm"][:, 2 * u:2 * u + 2], small["mx"][:, 2 * u:2 * u + 2], -1.0, None,
                                    ALU.mult).then_inc(nm_ready[layer], 1)

                def normalise(u):
                    stream = units[u][2]
                    for q in range(2 if stream == LAT else 1):
                        wait_taken(dve, ("score", layer, u, q))
                    link(v.reciprocal(small["ri"][:, 2 * u:2 * u + 2], small["rs"][:, 2 * u:2 * u + 2]))
                    n = T if stream == LAT else S
                    for t in range(2):
                        p = PR[:, u % 2, t, 0:n]
                        ins = v.tensor_scalar(p, p, small["ri"][:, 2 * u + t:2 * u + t + 1], None, ALU.mult)
                    ins.then_inc(p_ready[layer], 1)

                def turned_out(u):
                    stream = units[u][2]
                    dve.wait_ge(turned_full[layer], u + 1)
                    if u >= 2:
                        dve.wait_ge(pv_full[layer], u - 1)
                    n = 2 if stream == LAT else 1
                    v.tensor_copy(PT[:, u % 2, n:2 * n, :], turned[1][:, 0:S * n].rearrange("p (t n) -> p t n", t=n))\
                        .then_inc(turned_out_dve[layer], 1)

                maxima(0)
                maxima(1)
                for u in range(len(units)):
                    normalise(u)
                    if u + 2 < len(units):
                        maxima(u + 2)
                    turned_out(u)
                    if layer == 0:
                        mod(MOD_IN_ATTENTION[u])

            def merge(layer):
                nq = S * len(streams_of(layer))
                gates = [W_IN_GATE + 4 * b + j for j in range(4) for b in range(3)]
                if layer == 1:
                    low_half(gates[0])
                    low_half(gates[1])
                for j in range(4):
                    if layer == 1:
                        for slab in gates[3 * j + 2:3 * j + 5]:
                            low_half(slab)
                    for b in range(3):
                        for m in range(2):
                            key = ("proj", layer, j, b, m)
                            g = GATE[:, 2 * b + m, 0:nq]
                            dst = M[:, 2 * j + m, 0:nq]
                            wait_taken(dve, ("gate", layer, j, b, m))
                            wait_full(dve, key)
                            if b == 0:
                                v.tensor_tensor(dst, g, acc(key)[:, 0:nq], ALU.mult).then_inc(freed(key), 1)
                            else:
                                link(v.tensor_tensor(TMP[:, m, 0:nq], g, acc(key)[:, 0:nq], ALU.mult))
                                wait_taken(dve, ("proj", layer, j, b - 1, m))
                                v.tensor_tensor(dst, dst, TMP[:, m, 0:nq], ALU.add).then_inc(freed(key), 1)

            def residual(layer, part, key, c):
                streams = streams_of(layer)
                wait_full(dve, key)
                for n, stream in enumerate(streams):
                    x = XT[:, c, S * stream:S * stream + S]
                    ins = v.scalar_tensor_tensor(x, acc(key)[:, S * n:S * n + S], mod_vec(layer, part, c, stream), x,
                                                 ALU.mult, ALU.add)
                ins.then_inc(freed(key), 1)

            def feed_forward():
                q = 0
                for part, n in enumerate(PART_CHUNKS):
                    for s in range(n // 2):
                        for m in range(2):
                            k1, k3 = ("w1", part, s, m), ("w3", part, s, m)
                            wait_taken(dve, k1)
                            wait_full(dve, k3)
                            if q >= 4:
                                dve.wait_ge(hid_lo_ready, q - 3)
                            v.tensor_tensor(HID[:, q % 4, :], SILU[:, m, :], acc(k3)[:], ALU.mult)\
                                .then_inc(freed(k3), 1)
                            q += 1
                        if later:
                            mod(later.pop(0))
                    residuals(0, 5, [("down", part, c // 2, c % 2) for c in range(DC)], (1, 1) if part == 2 else None)

            def route():
                wait_full(dve, ("logit",))
                rb = vec("rb").unsqueeze(1).to_broadcast([P, 2, 8])
                lg = R1
                link(v.tensor_tensor(lg[:], acc(("logit",))[:, 0:16].rearrange("p (t e) -> p t e", t=2), rb, ALU.add))
                dve.sem_inc(freed(("logit",)), 1)
                mine = lg[:].unsqueeze(3).to_broadcast([P, 2, 8, 8])
                other = lg[:].unsqueeze(2).to_broadcast([P, 2, 8, 8])
                low = const("lower").rearrange("p (a b) -> p a b", a=8).unsqueeze(1).to_broadcast([P, 2, 8, 8])
                link(v.tensor_tensor(CMP[:], other, mine, ALU.is_equal))
                link(v.tensor_tensor(CMP[:], CMP[:], low, ALU.mult))
                link(v.tensor_tensor(CMP2[:], other, mine, ALU.is_gt))
                link(v.tensor_tensor(CMP[:], CMP[:], CMP2[:], ALU.add))
                link(v.tensor_reduce(RANK[:], CMP[:], AX, ALU.add))
                v.tensor_scalar(SEL[:], RANK[:], 2.0, None, ALU.is_lt).then_inc(sel_ready, 1)
                link(v.reduce_max(RM[:], lg[:], AX))
                v.tensor_tensor(lg[:], lg[:], RM[:].unsqueeze(2).to_broadcast([P, 2, 8]), ALU.subtract)\
                    .then_inc(routed, 1)
                for i in range(4):
                    key = ("turn", i)
                    wait_full(dve, key)
                    t, half = divmod(i, 2)
                    v.tensor_copy(HTOK[:, t, 512 * half:512 * half + 512], acc(key)[:]).then_inc(freed(key), 1)
                dve.wait_ge(ex_ready, 1)
                link(v.tensor_tensor(EX[:], EX[:], SEL[:], ALU.mult))
                link(v.tensor_reduce(RSUM[:], EX[:], AX, ALU.add))
                link(v.reciprocal(RINV[:], RSUM[:]))
                v.memset(W[:], 0.0)
                link(v.memset(POS[:], -1.0))
                link(v.tensor_tensor(W[:, :, 0:8], EX[:], RINV[:].unsqueeze(2).to_broadcast([P, 2, 8]), ALU.mult))
                wait_full(dve, ("prefix",))
                src = acc(("prefix",))
                link(v.scalar_tensor_tensor(POS1[:], src[:, 0:16].rearrange("p (t e) -> p t e", t=2), 1.0, SEL[:],
                                            ALU.add, ALU.mult))
                link(v.tensor_scalar(POS[:, :, 0:8], POS1[:], -1.0, None, ALU.add))
                link(v.tensor_copy(COUNTF[:], src[:, 16:24]))
                dve.sem_inc(freed(("prefix",)), 1)
                v.tensor_copy(COUNT[:], COUNTF[:]).then_inc(counts_ready, 1)
                link(v.reduce_max(MAXF[:], COUNTF[:], AX))
                v.tensor_copy(MAXI[:], MAXF[:]).then_inc(counts_ready, 1)
            def onehots(e, again=0):
                iota = const("iota")[:, SLOTS * again:SLOTS * (again + 1)]
                for t in range(2):
                    pos = POS[:, t, bass.ds(e, 1)]
                    v.tensor_scalar(ONEHOT[:, t, :], iota, pos, None, ALU.is_equal)
                for t in range(2):
                    ins = v.tensor_scalar(WEIGHTED[:, t, :], iota, POS[:, t, bass.ds(e, 1)],
                                          W[:, t, bass.ds(e, 1)], ALU.is_equal, ALU.mult)
                ins.then_inc(onehot_ready, 1)

            def gathered_out(n):
                for b in range(2):
                    dve.wait_ge(he_ready, 2 * n + b + 1)
                    v.tensor_tensor(HE_LO[:, 4 * b:4 * b + 4, :],
                                    gath[b][:, 0:4 * SLOTS].rearrange("p (c n) -> p c n", c=4),
                                    HE_HI[:, 4 * b:4 * b + 4, :].bitcast(F32), ALU.subtract)\
                        .then_inc(he_lo_ready, 1)

            def expert(e, i, again=0):
                if again:
                    onehots(e, again)

                def low(key):
                    moe_low_part(dve, v, EXPERT_AT[key], i, slice(0, LO_DVE), moe_lo_dve)

                def turned_hidden(g):
                    dve.wait_ge(ge_hi_ready, i * GROUPS + g + 1)
                    v.tensor_tensor(GE_LO[:, g % 2, :, :], ge_bank[:, 0:2 * SLOTS].rearrange("p (m n) -> p m n", m=2),
                                    GE_HI[:, g % 2, :, :].bitcast(F32), ALU.subtract).then_inc(ge_lo_ready, 1)

                low(("up", 0, 0))
                if again:
                    gathered_out(i + 1)
                low(("up", 0, 1))
                for g in range(GROUPS):
                    if g:
                        if g >= 2:
                            low(("down", g - 1))
                        turned_hidden(g - 1)
                    if g + 1 < GROUPS:
                        low(("up", g + 1, 0))
                    dve.wait_ge(se_ready, i * GROUPS + g + 1)
                    v.tensor_tensor(GT[:, g % 2, :], SE[:, g % 2, :], up[g % 2][0:SLOTS, 256:512], ALU.mult)\
                        .then_inc(gt_ready, 1)
                    if g + 1 < GROUPS:
                        low(("up", g + 1, 1))
                    if g == 0:
                        low(("down", 0))
                    if g == 1 and not again:
                        dve.wait_ge(weights_turned, i + 1)
                        onehots(e + 1)
                low(("down", GROUPS - 1))
                if not again:
                    gathered_out(i + 1)
                turned_hidden(GROUPS - 1)
                wait_slab_used(dve, N_EXPERT_SLABS - 1, i)
                v.tensor_copy(YTOK[:, 0:512], down[0][0:SLOTS, :]).then_inc(ytok_dve, 1)
                for n in range(4):
                    dve.wait_ge(scattered, 4 * i + n + 1)
                    for c in range(2):
                        x = XT[:, 2 * n + c, S:T]
                        ins = v.scalar_tensor_tensor(x, gath[n % 2][:, S * c:S * c + S],
                                                     mod_vec(1, 5, 2 * n + c, LAT), x, ALU.mult, ALU.add)
                    ins.then_inc(x_added, 1)

            later = list(MOD_IN_FFN)
            v.memset(small["cond"][:], 0.0).then_inc(cond_zeroed, 1)
            dve.wait_ge(vecs_in, 16)
            for n in MOD_AT_START:
                if n == 4:
                    for c in range(1, DC):
                        sum_squares((0, 1), 0, T, c)
                mod(n)
            for layer in L:
                scale(layer, 1)
                norm((layer, 1), 0, T)
                in_proj(layer)
                bias(layer)
                qk_norm(layer)
                attention(layer)
                merge(layer)
                residuals(layer, 2, [("out", layer, c // 2, c % 2) for c in range(DC)], (layer, 2))
                scale(layer, 2)
                lo, hi = x_range(layer)
                norm((layer, 2), lo, hi)
                if layer == 0:
                    feed_forward()
            route()
            onehots(0)
            gathered_out(0)
            with dve.Fori(0, N_EXPERTS) as e:
                expert(e, e)

            def skip():
                for s, n in ((onehot_ready, 1), (moe_lo_dve, N_EXPERT_SLABS), (he_lo_ready, 2), (gt_ready, GROUPS),
                             (ge_lo_ready, GROUPS), (ytok_dve, 1), (x_added, 4)):
                    dve.sem_inc(s, n)

            overflow_steps(dve, expert, skip)
            for c in range(1, DC):
                sum_squares("final", S, T, c)
            dve.wait_ge(final_rms, 1)
            v.reciprocal(small["rrms"][:, 0:2], small["rms"][:, 0:2]).then_inc(rrms_ready["final"], 1)
            dve.wait_ge(tmp_ready["final"], 1)
            lo = VEC_COLS["final"][0]
            for c in range(DC):
                v.scalar_tensor_tensor(OUT[:, c, :], XT[:, c, S:T], VEC[:, lo + c:lo + c + 1], bank[1][:, 0:S],
                                       ALU.mult, ALU.mult).then_inc(out_ready, 1)


def constants():
    c = np.zeros((P, N_CONST), np.float32)

    def put(name, value):
        lo, hi = CONST_COLS[name]
        c[:, lo:hi] = value

    put("ident", np.eye(P))
    put("ones", 1.0)
    p = np.arange(P)
    partner = np.where(p % 32 < 16, p + 16, p - 16)
    perm = np.zeros((P, P))
    perm[partner, p] = 1.0
    put("perm", perm)
    put("before", p[:, None] < p[None, :])
    put("blk2", p[:, None] // HD == np.arange(2)[None, :])
    t = np.arange(S)
    pos = np.stack([t // GRID_W, t % GRID_W], -1).astype(np.float32)
    inv_freq = np.float32(10000.0) ** (-np.arange(0, 32, 2, dtype=np.float32) / np.float32(32))
    ang = pos[:, :, None] * inv_freq[None, None, :]
    axis, i = (p % HD) // 32, p % 16
    put("cos", np.cos(ang)[:, axis, i].T)
    put("sin", np.sin(ang)[:, axis, i].T * np.where(p % 32 < 16, -1.0, 1.0)[:, None])
    col = p % GRID_W
    start = np.clip(col - 8, 0, GRID_W - 16)
    kc = np.arange(GRID_W)[None, :]
    put("wmask", np.where((kc >= start[:, None]) & (kc < start[:, None] + 16), 0.0, MASKED))
    put("iota", np.arange(PASSES * SLOTS))
    e = np.arange(8)
    put("lower", (e[None, :] < e[:, None]).reshape(1, 64))
    put("eps", EPS)
    pool = np.zeros((S, 4, S), np.float32)
    for g, w in enumerate((2, 4, 8, 16)):
        for out in range(S):
            lo, hi = max(out - w // 2, 0), min(out - w // 2 + w, S)
            pool[lo:hi, g, out] = 1.0 / (hi - lo)
            pool[out, g, out] -= 1.0
    pool = pool.reshape(2, P, 4 * S).transpose(1, 0, 2).reshape(P, -1)
    return c, np.ascontiguousarray(pool)


def slabs(w):
    k, n = w.shape
    w = w.reshape(k // P, P, n // 256, 256).transpose(2, 1, 0, 3)
    return np.ascontiguousarray(w).reshape(n // 256, P, k // P * 256)


def by_chunk(x):
    return x.reshape(-1, P).T


_ORDER = ["w_mod", "w_in", "w_proj", "w_out", "ffn_w1", "ffn_w3", "ffn_w2_0", "ffn_w2_1", "ffn_w2_2", "moe_up",
          "moe_w2", "xt", "vecs", "consts", "pool_mat", "pool_w", "rel_bias"]


def layout(x, c, ctx, c_ctx, w_mod, b_mod, norm1_g, norm2_g, w_in, q_norm_g, k_norm_g, na_rel_bias, pool_w,
           pool_scale, w_branch_a, w_branch_b, w_branch_c, w_out, ffn_w1, ffn_w3, ffn_w2, router_w, router_b,
           moe_w1, moe_w3, moe_w2, final_g):
    a = {}
    heads = np.array([h for j in range(4) for h in (j, 4 + j)])
    cols = (heads[:, None] * HD + np.arange(HD)).reshape(-1)
    w_in = np.concatenate([w_in[:, :, cols], w_in[:, :, 512:]], axis=2)
    a["w_mod"] = np.concatenate([slabs(w) for w in w_mod])
    a["w_in"] = np.concatenate([slabs(w) for w in w_in])
    proj = np.concatenate([w_branch_a[:, cols], w_branch_b, w_branch_c], axis=1)
    a["w_proj"] = np.concatenate([slabs(w) for w in proj])
    a["w_out"] = np.concatenate([slabs(w) for w in w_out])
    a["ffn_w1"], a["ffn_w3"] = slabs(ffn_w1[0]), slabs(ffn_w3[0])
    f0 = 0
    for part, n in enumerate(PART_CHUNKS):
        a[f"ffn_w2_{part}"] = slabs(ffn_w2[0, P * f0:P * (f0 + n)])
        f0 += n
    w = np.stack([moe_w1[0], moe_w3[0]]).reshape(2, N_EXPERTS, 2, 4, P, GROUPS, 256)
    a["moe_up"] = np.ascontiguousarray(w.transpose(1, 5, 2, 4, 3, 0, 6)).reshape(-1, SLAB)
    w = moe_w2[0].reshape(N_EXPERTS, GROUPS, 2, P, D).transpose(0, 1, 3, 2, 4)
    a["moe_w2"] = np.ascontiguousarray(w).reshape(-1, SLAB)
    xt = np.concatenate([ctx[0], x[0]], axis=0).T.reshape(DC, P, T).transpose(1, 0, 2)
    a["xt"] = np.ascontiguousarray(xt).reshape(P, DC * T)
    vecs = np.zeros((P, N_VEC), np.float32)

    def put(name, value):
        lo, hi = VEC_COLS[name]
        vecs[:, lo:hi] = value

    for l in range(DEPTH):
        put(("bmod", l), by_chunk(b_mod[l]))
        put(("g1", l), by_chunk(norm1_g[l]))
        put(("g2", l), by_chunk(norm2_g[l]))
        put(("gq", l), np.concatenate([q_norm_g[l]] * 2)[:, None])
        put(("gk", l), np.concatenate([k_norm_g[l]] * 2)[:, None])
        put(("pscale", l), by_chunk(pool_scale[l]))
    put("final", by_chunk(final_g))
    put("cond", np.stack([by_chunk(c[0]), by_chunk(c_ctx)], -1).reshape(P, 2 * DC))
    put("rw", router_w[0].reshape(DC, P, N_EXPERTS).transpose(1, 0, 2).reshape(P, -1))
    put("rb", router_b[0][None, :])
    a["vecs"] = vecs
    a["consts"], a["pool_mat"] = constants()
    pw = np.zeros((DEPTH, 2, HD, 2, 2, HD), np.float32)
    for g in range(4):
        pw[:, g % 2, :, g // 2, g % 2, :] = pool_w[:, g]
    a["pool_w"] = pw.reshape(DEPTH, P, 2 * P)
    t = np.arange(S)
    dr = t[None, :] // GRID_W - t[:, None] // GRID_W + 7
    dc = np.clip(t[None, :] % GRID_W - t[:, None] % GRID_W + 15, 0, 30)
    a["rel_bias"] = np.ascontiguousarray(
        na_rel_bias[:, :, dr, dc].reshape(DEPTH, 4, 2, P, S).transpose(0, 3, 2, 1, 4)).reshape(DEPTH, P, -1)
    return a


def kernel(**inputs):
    import concourse.bacc as bacc
    from concourse.bass_utils import run_bass_kernel_spmd

    arrays = layout(**{k: np.asarray(v) for k, v in inputs.items()})
    nc = bacc.Bacc("TRN2", target_bir_lowering=False, num_devices=1)
    aps = {}
    for name in _ORDER:
        arr = arrays[name]
        aps[name] = nc.dram_tensor(f"in_{name}", arr.shape, mybir.dt.from_np(arr.dtype), kind="ExternalInput").ap()
    aps["out"] = nc.dram_tensor("out_t", (P, DC * S), F32, kind="ExternalOutput").ap()
    build(nc, aps)
    r = run_bass_kernel_spmd(nc, [{f"in_{n}": arrays[n] for n in _ORDER}], core_ids=[0])
    out = np.asarray(r.results[0]["out_t"]).reshape(P, DC, S)
    return np.ascontiguousarray(out.transpose(2, 1, 0)).reshape(1, S, D)
```
